# Optimizing a Trainium2 kernel written in Bass

```python
import math
import jax
import jax.numpy as jnp
from jax import lax
import numpy as np
import jax, jax.numpy as jnp

D_MODEL = 1024
BATCH = 1
SEQ = 512
DEPTH = 1

GRID_W = 64
N_MEM = 256
HEAD_DIM = 64
MIX_WIDTH = D_MODEL
POOL_WIDTH = MIX_WIDTH // 4
POOL_WINDOWS = (2, 4, 8, 16)
POOL_GROUP = POOL_WIDTH // len(POOL_WINDOWS)
MLSTM_WIDTH = MIX_WIDTH // 4
MLSTM_HEADS = MLSTM_WIDTH // HEAD_DIM
MLSTM_CHUNK = 128
MLSTM_CONV = 5
ATTN_Q_WIDTH = MIX_WIDTH // 2
ATTN_Q_HEADS = ATTN_Q_WIDTH // HEAD_DIM
ATTN_KV_HEADS = ATTN_Q_HEADS // 4
ATTN_KV_WIDTH = ATTN_KV_HEADS * HEAD_DIM
Q_BLOCK = 128
ROPE_THETA = 10000.0
IN_SPLITS = (POOL_WIDTH, MLSTM_WIDTH, MLSTM_WIDTH, MLSTM_WIDTH, MLSTM_WIDTH,
             2 * MLSTM_HEADS, 2 * MLSTM_HEADS, ATTN_Q_WIDTH, ATTN_KV_WIDTH, ATTN_KV_WIDTH)
IN_COLS = sum(IN_SPLITS)
CA_HEADS = 4
CA_WIDTH = D_MODEL // 2
CA_HEAD_DIM = CA_WIDTH // CA_HEADS
N_EXPERTS = 16
EC_CAPACITY_FACTOR = 2
D_FF_EXPERT = 2 * D_MODEL
EPS = 1e-6


F32 = jnp.float32

def rmsnorm(x, g):
    xf = x.astype(F32)
    y = xf * lax.rsqrt(jnp.mean(xf * xf, axis=-1, keepdims=True) + EPS)
    return (y * g.astype(F32)).astype(x.dtype)

def head_rmsnorm(a, g):
    af = a.astype(F32)
    return af * lax.rsqrt(jnp.mean(af * af, axis=-1, keepdims=True) + EPS) * g.astype(F32)

def axial_rope_tables(s):
    rows = s // GRID_W
    row_ids = jnp.repeat(jnp.arange(rows), GRID_W).astype(F32)
    col_ids = jnp.tile(jnp.arange(GRID_W), rows).astype(F32)
    n_freq = HEAD_DIM // 4
    inv_freq = ROPE_THETA ** (-jnp.arange(n_freq, dtype=F32) / n_freq)
    ang = jnp.concatenate([row_ids[:, None] * inv_freq, col_ids[:, None] * inv_freq], axis=-1)
    return jnp.cos(ang), jnp.sin(ang)

def apply_rope(a, cos, sin):
    a2 = a.reshape(*a.shape[:-1], HEAD_DIM // 2, 2)
    x0, x1 = a2[..., 0], a2[..., 1]
    c = cos[None, :, None, :]
    sn = sin[None, :, None, :]
    return jnp.stack([x0 * c - x1 * sn, x0 * sn + x1 * c], axis=-1).reshape(a.shape)

def pool_mixer(u, w, scale):
    b, s, _ = u.shape
    uf = u.astype(F32)
    cs = jnp.concatenate([jnp.zeros((b, 1, POOL_WIDTH), F32), jnp.cumsum(uf, axis=1)], axis=1)
    t = jnp.arange(s)
    diffs = []
    for g, win in enumerate(POOL_WINDOWS):
        lo = jnp.clip(t - win // 2, 0, s)
        hi = jnp.clip(t + win // 2, 0, s)
        c0 = g * POOL_GROUP
        csg = cs[:, :, c0:c0 + POOL_GROUP]
        mean = (csg[:, hi] - csg[:, lo]) / (hi - lo).astype(F32)[None, :, None]
        diffs.append(mean - uf[:, :, c0:c0 + POOL_GROUP])
    d = jnp.stack(diffs, axis=2)
    y = jnp.einsum('bsgc,gce->bsge', d, w.astype(F32)).reshape(b, s, POOL_WIDTH)
    return (y * scale.astype(F32)).astype(u.dtype)

def mlstm_scan(q, k, v, log_i, log_f):
    b, h, s, dh = q.shape
    nc = s // MLSTM_CHUNK

    def chunks(a):
        a = a.reshape(b, h, nc, MLSTM_CHUNK, *a.shape[3:])
        return jnp.moveaxis(a, 2, 0)

    lower = jnp.tril(jnp.ones((MLSTM_CHUNK, MLSTM_CHUNK), dtype=bool))

    def step(carry, inp):
        c_st, n_st, m_st = carry
        qc, kc, vc, li, lf = inp
        bcum = jnp.cumsum(lf, axis=-1)
        dmat = jnp.where(lower, bcum[..., :, None] - bcum[..., None, :] + li[..., None, :], -jnp.inf)
        inter = bcum + m_st[..., None]
        m_j = jnp.maximum(inter, jnp.max(dmat, axis=-1))
        a_mat = jnp.exp(dmat - m_j[..., None]) * jnp.einsum('bhjd,bhsd->bhjs', qc, kc)
        a_int = jnp.exp(inter - m_j)
        num = (jnp.einsum('bhjs,bhse->bhje', a_mat, vc)
               + a_int[..., None] * jnp.einsum('bhed,bhjd->bhje', c_st, qc))
        den = jnp.sum(a_mat, axis=-1) + a_int * jnp.einsum('bhd,bhjd->bhj', n_st, qc)
        h_out = num / jnp.maximum(jnp.abs(den), jnp.exp(-m_j))[..., None]
        b_last = bcum[..., -1]
        g = b_last[..., None] - bcum + li
        m_new = jnp.maximum(b_last + m_st, jnp.max(g, axis=-1))
        w_s = jnp.exp(g - m_new[..., None])
        decay = jnp.exp(b_last + m_st - m_new)
        c_new = decay[..., None, None] * c_st + jnp.einsum('bhs,bhse,bhsd->bhed', w_s, vc, kc)
        n_new = decay[..., None] * n_st + jnp.einsum('bhs,bhsd->bhd', w_s, kc)
        return (c_new, n_new, m_new), h_out

    init = (jnp.zeros((b, h, dh, dh), F32), jnp.zeros((b, h, dh), F32), jnp.zeros((b, h), F32))
    _, hs = lax.scan(step, init, (chunks(q), chunks(k), chunks(v), chunks(log_i), chunks(log_f)))
    return jnp.moveaxis(hs, 0, 2).reshape(b, h, s, dh)

def mlstm_mixer(q, k, v, o, i_pre, f_pre, conv_w, norm_g):
    b, s, _ = q.shape
    qk = jnp.concatenate([q, k], axis=-1)
    qk = lax.conv_general_dilated(qk, conv_w[:, None, :].astype(qk.dtype), window_strides=(1,),
                                  padding=[(MLSTM_CONV // 2, MLSTM_CONV // 2)],
                                  dimension_numbers=('NWC', 'WIO', 'NWC'),
                                  feature_group_count=2 * MLSTM_WIDTH)
    qk = jax.nn.silu(qk)
    q, k = jnp.split(qk, 2, axis=-1)

    def heads(a):
        return a.astype(F32).reshape(b, s, MLSTM_HEADS, HEAD_DIM).transpose(0, 2, 1, 3)

    qh, kh, vh = heads(q), heads(k) / math.sqrt(HEAD_DIM), heads(v)
    log_i = i_pre.astype(F32).reshape(b, s, 2, MLSTM_HEADS).transpose(2, 0, 3, 1)
    log_f = jax.nn.log_sigmoid(f_pre.astype(F32)).reshape(b, s, 2, MLSTM_HEADS).transpose(2, 0, 3, 1)
    flip = lambda a: jnp.flip(a, axis=2)
    h_fwd = mlstm_scan(qh, kh, vh, log_i[0], log_f[0])
    h_bwd = flip(mlstm_scan(flip(qh), flip(kh), flip(vh), flip(log_i[1]), flip(log_f[1])))
    hsum = h_fwd + h_bwd
    hsum = hsum * lax.rsqrt(jnp.mean(hsum * hsum, axis=-1, keepdims=True) + EPS)
    hsum = hsum.transpose(0, 2, 1, 3).reshape(b, s, MLSTM_WIDTH) * norm_g.astype(F32)
    return (hsum * jax.nn.sigmoid(o.astype(F32))).astype(q.dtype)

def attn_mixer(q, k, v, qn_g, kn_g, cos, sin):
    b, s, _ = q.shape
    group = ATTN_Q_HEADS // ATTN_KV_HEADS
    qh = apply_rope(head_rmsnorm(q.reshape(b, s, ATTN_Q_HEADS, HEAD_DIM), qn_g), cos, sin)
    kh = apply_rope(head_rmsnorm(k.reshape(b, s, ATTN_KV_HEADS, HEAD_DIM), kn_g), cos, sin)
    qh = (qh * HEAD_DIM ** -0.5).astype(q.dtype)
    kh = kh.astype(k.dtype).transpose(0, 2, 1, 3)
    vh = v.reshape(b, s, ATTN_KV_HEADS, HEAD_DIM).transpose(0, 2, 1, 3)
    nb = s // Q_BLOCK
    qb = qh.reshape(b, nb, Q_BLOCK, ATTN_KV_HEADS, group, HEAD_DIM).transpose(1, 0, 3, 4, 2, 5)

    def block(qi):
        sc = jnp.einsum('bhgqd,bhkd->bhgqk', qi, kh, preferred_element_type=F32)
        p = jax.nn.softmax(sc, axis=-1).astype(vh.dtype)
        return jnp.einsum('bhgqk,bhkd->bhgqd', p, vh)

    ob = lax.map(block, qb)
    return ob.transpose(1, 0, 4, 2, 3, 5).reshape(b, s, ATTN_Q_WIDTH)

def mem_cross_attn(hn, mem, wq, wkv, wo):
    b, s, _ = hn.shape
    q = (hn @ wq).reshape(b, s, CA_HEADS, CA_HEAD_DIM)
    kv = (mem @ wkv).reshape(b, mem.shape[1], 2, CA_HEADS, CA_HEAD_DIM)
    sc = jnp.einsum('bshd,bmhd->bhsm', q, kv[:, :, 0], preferred_element_type=F32) * CA_HEAD_DIM ** -0.5
    p = jax.nn.softmax(sc, axis=-1).astype(hn.dtype)
    o = jnp.einsum('bhsm,bmhd->bshd', p, kv[:, :, 1]).reshape(b, s, CA_WIDTH)
    return o @ wo

def ec_moe(h, router_w, w_gu, w_down):
    b, n, d = h.shape
    cap = EC_CAPACITY_FACTOR * n // N_EXPERTS
    logits = jnp.einsum('bnd,de->bne', h, router_w, preferred_element_type=F32)
    aff = jax.nn.softmax(logits, axis=-1)
    gates, idx = lax.top_k(jnp.swapaxes(aff, 1, 2), cap)
    xs = jax.vmap(lambda hb, ib: hb[ib])(h, idx)

    def expert(args):
        xe, wgu, wd = args
        gu = jnp.einsum('bcd,df->bcf', xe, wgu)
        ga, up = jnp.split(gu, 2, axis=-1)
        return jnp.einsum('bcf,fd->bcd', jax.nn.silu(ga) * up, wd)

    ys = lax.map(expert, (jnp.swapaxes(xs, 0, 1), w_gu, w_down))
    ys = jnp.swapaxes(ys, 0, 1) * gates[..., None].astype(ys.dtype)
    return jax.vmap(lambda ib, yb: jnp.zeros((n, d), yb.dtype).at[ib.reshape(-1)].add(yb.reshape(-1, d)))(idx, ys)

def first_inputs(seed: int = 0) -> dict:
    key = jax.random.key(seed)
    ks = jax.random.split(key, 24)
    nrm = lambda k, shape, scale: jax.random.normal(k, shape, F32) * scale
    gain = lambda k, shape: 1.0 + 0.05 * jax.random.normal(k, shape, F32)
    gate_b = jnp.concatenate([nrm(ks[7], (DEPTH, 2 * MLSTM_HEADS), 0.1),
                              3.0 + nrm(ks[8], (DEPTH, 2 * MLSTM_HEADS), 0.5)], axis=-1)
    return {
        'x': nrm(ks[0], (BATCH, SEQ, D_MODEL), 1.0),
        'mem': nrm(ks[1], (BATCH, N_MEM, D_MODEL), 1.0),
        'norm_mix_g': gain(ks[2], (DEPTH, D_MODEL)),
        'w_in': nrm(ks[3], (DEPTH, D_MODEL, IN_COLS), D_MODEL ** -0.5),
        'pool_w': nrm(ks[4], (DEPTH, len(POOL_WINDOWS), POOL_GROUP, POOL_GROUP), POOL_GROUP ** -0.5),
        'pool_scale': gain(ks[5], (DEPTH, POOL_WIDTH)),
        'mlstm_conv_w': nrm(ks[6], (DEPTH, MLSTM_CONV, 2 * MLSTM_WIDTH), MLSTM_CONV ** -0.5),
        'mlstm_gate_b': gate_b,
        'mlstm_norm_g': gain(ks[9], (DEPTH, MLSTM_WIDTH)),
        'q_norm_g': gain(ks[10], (DEPTH, HEAD_DIM)),
        'k_norm_g': gain(ks[11], (DEPTH, HEAD_DIM)),
        'w_out': nrm(ks[12], (DEPTH, MIX_WIDTH, D_MODEL), MIX_WIDTH ** -0.5),
        'norm_mem_g': gain(ks[13], (DEPTH, D_MODEL)),
        'ca_wq': nrm(ks[14], (DEPTH, D_MODEL, CA_WIDTH), D_MODEL ** -0.5),
        'ca_wkv': nrm(ks[15], (DEPTH, D_MODEL, 2 * CA_WIDTH), D_MODEL ** -0.5),
        'ca_wo': nrm(ks[16], (DEPTH, CA_WIDTH, D_MODEL), CA_WIDTH ** -0.5),
        'norm_ffn_g': gain(ks[17], (DEPTH, D_MODEL)),
        'router_w': nrm(ks[18], (DEPTH, D_MODEL, N_EXPERTS), D_MODEL ** -0.5),
        'expert_w_gu': nrm(ks[19], (DEPTH, N_EXPERTS, D_MODEL, 2 * D_FF_EXPERT), D_MODEL ** -0.5),
        'expert_w_down': nrm(ks[20], (DEPTH, N_EXPERTS, D_FF_EXPERT, D_MODEL), D_FF_EXPERT ** -0.5),
        'final_norm_g': gain(ks[21], (D_MODEL,)),
    }

def first_block(x, mem, norm_mix_g, w_in, pool_w, pool_scale, mlstm_conv_w, mlstm_gate_b,
              mlstm_norm_g, q_norm_g, k_norm_g, w_out, norm_mem_g, ca_wq, ca_wkv, ca_wo,
              norm_ffn_g, router_w, expert_w_gu, expert_w_down, final_norm_g):
    s = x.shape[1]
    cos, sin = axial_rope_tables(s)
    offsets = np.cumsum(IN_SPLITS)[:-1].tolist()
    n_gate = 2 * MLSTM_HEADS
    for layer in range(DEPTH):
        hn = rmsnorm(x, norm_mix_g[layer])
        proj = hn @ w_in[layer]
        u_pool, m_q, m_k, m_v, m_o, m_i, m_f, a_q, a_k, a_v = jnp.split(proj, offsets, axis=-1)
        gb = mlstm_gate_b[layer]
        y_pool = pool_mixer(u_pool, pool_w[layer], pool_scale[layer])
        y_mlstm = mlstm_mixer(m_q, m_k, m_v, m_o, m_i + gb[:n_gate], m_f + gb[n_gate:],
                              mlstm_conv_w[layer], mlstm_norm_g[layer])
        y_attn = attn_mixer(a_q, a_k, a_v, q_norm_g[layer], k_norm_g[layer], cos, sin)
        x = x + jnp.concatenate([y_pool, y_mlstm, y_attn], axis=-1) @ w_out[layer]
        x = x + mem_cross_attn(rmsnorm(x, norm_mem_g[layer]), mem, ca_wq[layer], ca_wkv[layer], ca_wo[layer])
        x = x + ec_moe(rmsnorm(x, norm_ffn_g[layer]), router_w[layer], expert_w_gu[layer], expert_w_down[layer])
    return rmsnorm(x, final_norm_g)


CTX_LEN = 256
MLA_HEADS = 8
MLA_NOPE = 64
MLA_ROPE = 32
MLA_V = 64
Q_LORA = 256
KV_LORA = 128
MLA_WIDTH = MLA_HEADS * MLA_V
NA_HEADS = 8
NA_DIM = 64
NA_KR = 8
NA_KC = 16
NA_WIDTH = NA_HEADS * NA_DIM


KV_SPLITS = (KV_LORA, MLA_ROPE, NA_WIDTH, NA_WIDTH)
Q_SPLITS = (Q_LORA, MLA_WIDTH, NA_WIDTH, NA_WIDTH, D_MODEL, D_MODEL)
KV_COLS = KV_LORA + MLA_ROPE + 2 * NA_WIDTH
IN_WIDTH = KV_COLS + Q_LORA + MLA_WIDTH + 2 * NA_WIDTH + 2 * D_MODEL


def rmsnorm_2(x, g):
    xf = x.astype(jnp.float32)
    y = xf * lax.rsqrt(jnp.mean(xf * xf, axis=-1, keepdims=True) + EPS)
    return (y * g.astype(jnp.float32)).astype(x.dtype)

def split_cols(p, sizes):
    idx = np.cumsum(np.array(sizes))[:-1].tolist()
    return jnp.split(p, idx, axis=-1)

def heads(t, n):
    b, s, _ = t.shape
    return t.reshape(b, s, n, -1)

def rope_1d(x, pos):
    half = x.shape[-1] // 2
    freqs = ROPE_THETA ** (-jnp.arange(half, dtype=jnp.float32) / half)
    ang = pos.astype(jnp.float32)[:, None] * freqs[None, :]
    cos = jnp.cos(ang)[None, :, None, :]
    sin = jnp.sin(ang)[None, :, None, :]
    x1 = x[..., :half].astype(jnp.float32)
    x2 = x[..., half:].astype(jnp.float32)
    out = jnp.concatenate([x1 * cos - x2 * sin, x2 * cos + x1 * sin], axis=-1)
    return out.astype(x.dtype)

def rope_2d(x, rows, cols):
    d = x.shape[-1] // 2
    return jnp.concatenate([rope_1d(x[..., :d], rows), rope_1d(x[..., d:], cols)], axis=-1)

def mla_q(cq, g_cq, w_uq):
    b, s, _ = cq.shape
    q = (rmsnorm_2(cq, g_cq) @ w_uq).reshape(b, s, MLA_HEADS, MLA_NOPE + MLA_ROPE)
    return q[..., :MLA_NOPE], q[..., MLA_NOPE:]

def mla_kv(ckv, g_ckv, w_ukv):
    b, s, _ = ckv.shape
    kv = (rmsnorm_2(ckv, g_ckv) @ w_ukv).reshape(b, s, MLA_HEADS, MLA_NOPE + MLA_V)
    return kv[..., :MLA_NOPE], kv[..., MLA_NOPE:]

def block_attention(q, k, v, scale):
    b, s, h, dk = q.shape
    dv = v.shape[-1]
    nb = s // Q_BLOCK
    qb = q.reshape(b, nb, Q_BLOCK, h, dk).transpose(1, 0, 2, 3, 4)

    def one(qblk):
        sc = jnp.einsum('bqhd,bkhd->bhqk', qblk, k, preferred_element_type=jnp.float32) * scale
        p = jax.nn.softmax(sc, axis=-1).astype(v.dtype)
        return jnp.einsum('bhqk,bkhd->bqhd', p, v)

    o = lax.map(one, qb)
    return o.transpose(1, 0, 2, 3, 4).reshape(b, s, h * dv)

def neighborhood_attention(q, k, v, kc, vc, rpb):
    b, s, h, d = q.shape
    rows = s // GRID_W
    kr = min(NA_KR, rows)
    qg = q.reshape(b, rows, GRID_W, h, d)
    kg = k.reshape(b, rows, GRID_W, h, d)
    vg = v.reshape(b, rows, GRID_W, h, d)
    col = jnp.arange(GRID_W)
    c_start = jnp.clip(col - NA_KC // 2, 0, GRID_W - NA_KC)
    c_idx = c_start[:, None] + jnp.arange(NA_KC)[None, :]
    c_off = c_idx - col[:, None] + (NA_KC - 1)
    scale = d ** -0.5

    def one_row(r):
        r_start = jnp.clip(r - kr // 2, 0, rows - kr)
        k_slab = lax.dynamic_slice_in_dim(kg, r_start, kr, axis=1)
        v_slab = lax.dynamic_slice_in_dim(vg, r_start, kr, axis=1)
        k_win = k_slab[:, :, c_idx]
        v_win = v_slab[:, :, c_idx]
        qr = lax.dynamic_index_in_dim(qg, r, axis=1, keepdims=False)
        r_off = r_start + jnp.arange(kr) - r + (NA_KR - 1)
        bias = rpb[:, r_off[:, None, None], c_off[None, :, :]]
        bias = bias.transpose(0, 2, 1, 3).reshape(h, GRID_W, kr * NA_KC).astype(jnp.float32)
        s_win = jnp.einsum('bwhd,brwchd->bhwrc', qr, k_win, preferred_element_type=jnp.float32)
        s_win = s_win.reshape(b, h, GRID_W, kr * NA_KC) * scale + bias[None]
        s_ctx = jnp.einsum('bwhd,blhd->bhwl', qr, kc, preferred_element_type=jnp.float32) * scale
        p = jax.nn.softmax(jnp.concatenate([s_win, s_ctx], axis=-1), axis=-1).astype(v.dtype)
        p_win = p[..., :kr * NA_KC].reshape(b, h, GRID_W, kr, NA_KC)
        p_ctx = p[..., kr * NA_KC:]
        return (jnp.einsum('bhwrc,brwchd->bwhd', p_win, v_win)
                + jnp.einsum('bhwl,blhd->bwhd', p_ctx, vc))

    o = lax.map(one_row, jnp.arange(rows))
    return o.transpose(1, 0, 2, 3, 4).reshape(b, s, h * d)

def second_inputs(seed: int = 0) -> dict:
    key = jax.random.key(seed)
    ks = jax.random.split(key, 20)
    n = jax.random.normal
    D = D_MODEL
    return {
        "x": n(ks[0], (BATCH, SEQ, D), jnp.float32),
        "c": n(ks[1], (BATCH, D), jnp.float32),
        "ctx": n(ks[2], (BATCH, CTX_LEN, D), jnp.float32),
        "c_ctx": n(ks[3], (D,), jnp.float32),
        "w_mod": n(ks[4], (DEPTH, D, 3 * D), jnp.float32) * (0.5 * D ** -0.5),
        "b_mod": n(ks[5], (DEPTH, 3 * D), jnp.float32) * 0.01,
        "norm_g": 1.0 + 0.05 * n(ks[6], (DEPTH, D), jnp.float32),
        "w_in": n(ks[7], (DEPTH, D, IN_WIDTH), jnp.float32) * D ** -0.5,
        "g_cq": 1.0 + 0.05 * n(ks[8], (DEPTH, Q_LORA), jnp.float32),
        "w_uq": n(ks[9], (DEPTH, Q_LORA, MLA_HEADS * (MLA_NOPE + MLA_ROPE)), jnp.float32) * Q_LORA ** -0.5,
        "g_ckv": 1.0 + 0.05 * n(ks[10], (DEPTH, KV_LORA), jnp.float32),
        "w_ukv": n(ks[11], (DEPTH, KV_LORA, MLA_HEADS * (MLA_NOPE + MLA_V)), jnp.float32) * KV_LORA ** -0.5,
        "rpb": 0.02 * n(ks[12], (DEPTH, NA_HEADS, 2 * NA_KR - 1, 2 * NA_KC - 1), jnp.float32),
        "w_oa": n(ks[13], (DEPTH, MLA_WIDTH, D), jnp.float32) * MLA_WIDTH ** -0.5,
        "w_ob": n(ks[14], (DEPTH, NA_WIDTH, D), jnp.float32) * NA_WIDTH ** -0.5,
        "w_out": n(ks[15], (DEPTH, D, D), jnp.float32) * D ** -0.5,
        "final_g": 1.0 + 0.05 * n(ks[16], (D,), jnp.float32),
    }

def second_block(x, c, ctx, c_ctx, w_mod, b_mod, norm_g, w_in, g_cq, w_uq, g_ckv, w_ukv,
              rpb, w_oa, w_ob, w_out, final_g):
    b, s, _ = x.shape
    t = jnp.arange(s)
    row_pos = t // GRID_W
    col_pos = t % GRID_W
    mla_scale = (MLA_NOPE + MLA_ROPE) ** -0.5
    na_scale = NA_DIM ** -0.5
    sc = jax.nn.silu(c)
    scc = jax.nn.silu(c_ctx)
    for i in range(DEPTH):
        last = i == DEPTH - 1
        shift, scale, gate = jnp.split((sc @ w_mod[i] + b_mod[i])[:, None, :], 3, axis=-1)
        shift_c, scale_c, gate_c = jnp.split(scc @ w_mod[i] + b_mod[i], 3, axis=-1)
        h = rmsnorm_2(x, norm_g[i]) * (1 + scale) + shift
        hc = rmsnorm_2(ctx, norm_g[i]) * (1 + scale_c) + shift_c

        ckv, kr, kb, vb, cq, za, qb, zb, ga, gb = split_cols(h @ w_in[i], KV_SPLITS + Q_SPLITS)
        if last:
            c_ckv, c_kr, c_kb, c_vb = split_cols(hc @ w_in[i][:, :KV_COLS], KV_SPLITS)
        else:
            (c_ckv, c_kr, c_kb, c_vb, c_cq, c_za, c_qb, c_zb, c_ga, c_gb) = split_cols(
                hc @ w_in[i], KV_SPLITS + Q_SPLITS)

        qa_n, qa_r = mla_q(cq, g_cq[i], w_uq[i])
        qa = jnp.concatenate([qa_n, rope_2d(qa_r, row_pos, col_pos)], axis=-1)
        ka_n, va = mla_kv(ckv, g_ckv[i], w_ukv[i])
        ka_r = rope_2d(kr[:, :, None, :], row_pos, col_pos)
        ka = jnp.concatenate([ka_n, jnp.broadcast_to(ka_r, ka_n.shape[:-1] + (MLA_ROPE,))], axis=-1)
        kca_n, vca = mla_kv(c_ckv, g_ckv[i], w_ukv[i])
        kca = jnp.concatenate(
            [kca_n, jnp.broadcast_to(c_kr[:, :, None, :], kca_n.shape[:-1] + (MLA_ROPE,))], axis=-1)
        oa = block_attention(qa, jnp.concatenate([ka, kca], axis=1),
                             jnp.concatenate([va, vca], axis=1), mla_scale)

        ob = neighborhood_attention(heads(qb, NA_HEADS), heads(kb, NA_HEADS), heads(vb, NA_HEADS),
                                    heads(c_kb, NA_HEADS), heads(c_vb, NA_HEADS), rpb[i])

        ya = (oa * jax.nn.silu(za)) @ w_oa[i]
        yb = (ob * jax.nn.silu(zb)) @ w_ob[i]
        y = (jax.nn.sigmoid(ga) * ya + jax.nn.sigmoid(gb) * yb) @ w_out[i]

        if not last:
            qca_n, qca_r = mla_q(c_cq, g_cq[i], w_uq[i])
            oca = block_attention(jnp.concatenate([qca_n, qca_r], axis=-1), kca, vca, mla_scale)
            ocb = block_attention(heads(c_qb, NA_HEADS), heads(c_kb, NA_HEADS),
                                  heads(c_vb, NA_HEADS), na_scale)
            yca = (oca * jax.nn.silu(c_za)) @ w_oa[i]
            ycb = (ocb * jax.nn.silu(c_zb)) @ w_ob[i]
            yc = (jax.nn.sigmoid(c_ga) * yca + jax.nn.sigmoid(c_gb) * ycb) @ w_out[i]
            ctx = ctx + gate_c * yc

        x = x + gate * y
    return rmsnorm_2(x, final_g)


def setup_inputs(seed=0):
    out = dict(first_inputs(seed))
    for name, value in second_inputs(seed + 1).items():
        if name != "x":
            out[name + "_2"] = value
    return out


def reference(
    x, mem, norm_mix_g, w_in, pool_w, pool_scale, mlstm_conv_w, mlstm_gate_b, mlstm_norm_g,
    q_norm_g, k_norm_g, w_out, norm_mem_g, ca_wq, ca_wkv, ca_wo, norm_ffn_g, router_w,
    expert_w_gu, expert_w_down, final_norm_g, c_2, ctx_2, c_ctx_2, w_mod_2, b_mod_2, norm_g_2,
    w_in_2, g_cq_2, w_uq_2, g_ckv_2, w_ukv_2, rpb_2, w_oa_2, w_ob_2, w_out_2, final_g_2,
):
    x = first_block(
        x, mem, norm_mix_g, w_in, pool_w, pool_scale, mlstm_conv_w, mlstm_gate_b, mlstm_norm_g,
        q_norm_g, k_norm_g, w_out, norm_mem_g, ca_wq, ca_wkv, ca_wo, norm_ffn_g, router_w,
        expert_w_gu, expert_w_down, final_norm_g,
    )
    return second_block(
        x, c_2, ctx_2, c_ctx_2, w_mod_2, b_mod_2, norm_g_2, w_in_2, g_cq_2, w_uq_2, g_ckv_2,
        w_ukv_2, rpb_2, w_oa_2, w_ob_2, w_out_2, final_g_2,
    )


_drawn_inputs = setup_inputs


def setup_inputs(seed=0):
    import zlib

    import numpy as np

    out = dict(_drawn_inputs(seed))
    spreads = {}
    factors = {'mlstm_norm_g': 3.433,
     'q_norm_g': 8.0,
     'k_norm_g': 8.0,
     'norm_mem_g': 5.406,
     'ctx_2': 5.752,
     'b_mod_2': 8.0,
     'norm_g_2': 8.0,
     'g_cq_2': 8.0,
     'w_uq_2': 5.453,
     'g_ckv_2': 8.0,
     'rpb_2': 55.545}
    for name, (base, spread) in spreads.items():
        noise = np.random.default_rng([zlib.crc32(name.encode()), seed]).standard_normal(out[name].shape)
        drawn = base * np.exp(spread * noise) if base else spread * noise
        out[name] = jnp.asarray(drawn.astype(out[name].dtype))
    for name, factor in factors.items():
        out[name] = (out[name] * factor).astype(out[name].dtype)
    return out
```

```python
import math
from contextlib import ExitStack

import numpy as np

import concourse.bass as bass
from concourse import mybir

F32 = mybir.dt.float32
ACT = mybir.ActivationFunctionType
ALU = mybir.AluOpType
AX = mybir.AxisListType.X

P = 128
D = 1024
KD = D // P
S = 512
T = S // P
N_MEM = 256
HD = 64
GRID_W = 64
GRID_H = S // GRID_W
POOL_WINDOWS = (2, 4, 8, 16)
POOL_G = 64
PADL = 8
UP = S + 2 * PADL
ML_H = 4
ML_CONV = 5
QKP = S + ML_CONV - 1
AT_H = 8
CA_H, CA_HD = 4, 128
N_EXP = 16
CAP = 2 * S // N_EXP
FF = 2 * D
EPS = 1e-6
CTX = 256
NTOK = S + CTX
KT2 = NTOK // P
MLA_H, NOPE, ROPE = 8, 64, 32
QK_MLA = NOPE + ROPE
Q_LORA, KV_LORA = 256, 128
NA_H, NA_KR, NA_KC = 8, 8, 16
ROPE_THETA = 10000.0
BANK = 512
NBANK = 8
SLOT = 4096
NSLOT = 8
NEG = -1e30
SMALL = 700
N_COLUMNS = 17

GATE0, GATE1 = 1280, 1296
IN_COLS = 2064
MAIN = IN_COLS - 16
C2 = {"ckv": 0, "kb": 160, "vb": 672, "cq": 1184, "za": 1440, "qb": 1952, "zb": 2464, "ga": 2976, "gb": 4000}

C_ID, C_MF, C_MB, C_COS, C_SIN, C_IOTA, C_COS2, C_SIN2, C_ONE, C_END = np.cumsum(
    [0, 128, 128, 128, 128, 128, 64, 64, 64, 128]).tolist()


def shape_constants():
    c = np.zeros((P, C_END), np.float32)
    i = np.arange(P)
    c[:, C_ID:C_ID + P] = np.eye(P)
    c[:, C_MF:C_MF + P] = np.where(i[:, None] <= i[None, :], 0, NEG)
    c[:, C_MB:C_MB + P] = np.where(i[:, None] >= i[None, :], 0, NEG)
    tok = np.arange(S)
    row, col = (tok // GRID_W).astype(np.float32), (tok % GRID_W).astype(np.float32)

    def angles(n):
        f = (np.float32(ROPE_THETA) ** (-np.arange(n, dtype=np.float32) / np.float32(n))).astype(np.float32)
        return np.concatenate([row[:, None] * f, col[:, None] * f], axis=-1).astype(np.float32)

    def by_tile(a):
        return a.reshape(T, P, -1).transpose(1, 0, 2).reshape(P, -1)

    a = angles(HD // 4)
    c[:, C_COS:C_COS + 128], c[:, C_SIN:C_SIN + 128] = by_tile(np.cos(a)), by_tile(np.sin(a))
    a = angles(ROPE // 4)
    c[:, C_COS2:C_COS2 + 64], c[:, C_SIN2:C_SIN2 + 64] = by_tile(np.cos(a)), by_tile(np.sin(a))
    c[:, C_IOTA:C_IOTA + CAP] = np.arange(CAP)
    c[:, C_ONE:C_ONE + P] = 1.0
    inv = np.zeros((P, 2, S), np.float32)
    for g, w in enumerate(POOL_WINDOWS):
        n = np.clip(tok + w // 2, 0, S) - np.clip(tok - w // 2, 0, S)
        inv[(g % 2) * 64:(g % 2) * 64 + 64, g // 2] = (1.0 / n).astype(np.float32)
    return c, inv.reshape(P, 2 * S)


class Banks:

    def __init__(self, nc, ctx, psum):
        self.psum = psum
        self.full_sem = [ctx.enter_context(nc.semaphore(f"bank_full{b}")) for b in range(NBANK)]
        self.free_sem = [ctx.enter_context(nc.semaphore(f"bank_free{b}")) for b in range(NBANK)]
        self.next = 0

    def take(self, n):
        g = self.next
        self.next += n
        return range(g, g + n)

    def at(self, g):
        return self.psum[:, g % NBANK, :]

    def acquire(self, pe, g):
        if g >= NBANK:
            pe.wait_ge(self.free_sem[g % NBANK], g // NBANK)

    def filled(self, ins, g):
        ins.then_inc(self.full_sem[g % NBANK], 1)

    def full(self, eng, g):
        eng.wait_ge(self.full_sem[g % NBANK], g // NBANK + 1)

    def release(self, ins, g):
        ins.then_inc(self.free_sem[g % NBANK], 1)

    def drained(self, eng, g):
        eng.wait_ge(self.free_sem[g % NBANK], g // NBANK + 1)


def build(nc, a, out):
    ctx = ExitStack()
    pe, act, dve, pool, sp = nc.tensor, nc.scalar, nc.vector, nc.gpsimd, nc.sync
    with ctx:
        sems = {}

        def sem(name):
            if name not in sems:
                sems[name] = ctx.enter_context(nc.semaphore(name))
            return sems[name]

        def sb(name, cols, parts=P):
            return ctx.enter_context(nc.sbuf_tensor(name, [parts, cols], F32))

        psum = ctx.enter_context(nc.psum_tensor("psum", [P, NBANK, BANK], F32))
        B = Banks(nc, ctx, psum)

        ring = sb("ring", NSLOT * SLOT)
        x_flat = sb("x_res", T * D)
        hn_flat = sb("hn", T * D)
        W = sb("work_area", 10272)
        const = sb("const_sb", C_END)
        fill = sb("fill", 240)
        small = sb("small", SMALL)
        x_sb = x_flat[:].rearrange("p (t d) -> p t d", t=T)
        hn = hn_flat[:].rearrange("p (t d) -> p t d", t=T)
        taken = [0]

        def sm(n, parts=P):
            o = taken[0]
            taken[0] += n
            assert taken[0] <= SMALL
            return small[0:parts, o:o + n]

        def cut(base, o, *dims, parts=P):
            n = int(np.prod(dims))
            v = base[0:parts, o:o + n]
            if len(dims) == 2:
                v = v.rearrange("p (a b) -> p a b", a=dims[0])
            if len(dims) == 3:
                v = v.rearrange("p (a b c) -> p a b c", a=dims[0], b=dims[1])
            return v

        def slot(s):
            return ring[:, s * SLOT:(s + 1) * SLOT]

        ident = const[:, C_ID:C_ID + P]
        ones = const[:, C_ONE:C_ONE + P]
        gain = {n: sm(KD) for n in ("norm_mix_g", "norm_mem_g", "norm_ffn_g", "norm_g_2")}
        c_col = sm(2 * KD).rearrange("p (k v) -> p k v", v=2)
        b_mod_col = sm(2 * KD)
        pool_scale = sm(2)
        conv_w = sm(4 * ML_CONV).rearrange("p (c w) -> p c w", c=4)
        gate_i, gate_f = sm(1, 2 * ML_H), sm(1, 2 * ML_H)
        g_cq_col, g_ckv_col = sm(2), sm(1)
        stat = sm(64)
        mod = sm(2 * KD * 2).rearrange("p (j v) -> p j v", v=2)
        router_w = sm(KD * N_EXP).rearrange("p (k e) -> p k e", k=KD)
        aff = sm(T * N_EXP).rearrange("p (t e) -> p t e", t=T)
        slot_of = sm(T * N_EXP).rearrange("p (t e) -> p t e", t=T)
        gcols = sm(P).rearrange("p (k t r) -> p k t r", k=4, t=T)
        posc = sm(T * 2).rearrange("p (t e) -> p t e", t=T)
        gatec = sm(T * 2).rearrange("p (t e) -> p t e", t=T)
        ml_stat = sm(3 * T).rearrange("p (i t) -> p i t", i=3)

        slot_free = [sem(f"slot_free{s}") for s in range(NSLOT)]
        slot_loaded = [sem(f"slot_loaded{s}") for s in range(NSLOT)]
        dve_step = sem("dve_step")
        n_dve = [0]

        def link(ins):
            n_dve[0] += 1
            ins.then_inc(dve_step, 1)
            dve.wait_ge(dve_step, n_dve[0])

        w_in = ring[:, 0:4 * SLOT].rearrange("p (k c) -> p k c", k=KD)
        w_gate = cut(W, 9232, KD, 16)
        ca_wkv = ring[:, 4 * SLOT:6 * SLOT].rearrange("p (k c) -> p k c", k=KD)
        mem = cut(slot(6), 0, 2, D)
        memT = cut(slot(6), 2048, KD, N_MEM)
        kT_ca = cut(W, 0, CA_H, N_MEM)
        v_ca = cut(W, 1024, 2, CA_H * CA_HD)
        hT = cut(slot(7), 0, KD, S)
        four = 4 * SLOT
        qkpad = cut(ring, four, 4, QKP)
        sig_o = cut(ring, four + 2064, T, ML_H * HD)
        aq = cut(ring, four + 3088, T, AT_H, HD)
        ak = cut(ring, four + 5136, T, 2, HD)
        av = cut(ring, four + 5648, T, 2 * HD)
        kT_at = ring[:, four + 6160:four + 6672]
        pool_w = cut(ring, four + 6672, 2, POOL_G)
        ml_g = ring[:, four + 6800:four + 7056]
        qg = ring[:, four + 7056:four + 7120]
        kg = ring[:, four + 7120:four + 7184]
        upad = cut(slot(6), 0, 2, UP)
        p1 = cut(slot(6), 1056, 2, UP)
        p2 = cut(slot(6), 2112, 2, UP)
        p3 = slot(6)[:, 3168:3168 + UP]
        inv_n = cut(W, 9232, 2, S)
        d_pool = cut(hn_flat, 2048, 2, S)
        ymixT = cut(hn_flat, 0, KD, S)
        grow = [W[0:2 * ML_H, 2048 + i * S:2048 + (i + 1) * S] for i in range(8)]
        qkT = cut(W, 6144, 4, S)
        v_aug = cut(W, 8192, T, ML_H, HD + 1)
        hsum = cut(slot(6), 0, T, ML_H, HD)
        htmp = cut(slot(6), 1024, T, ML_H, HD)
        Pt = [cut(slot(7), 0, T, S), cut(slot(7), 2048, T, S)]
        sq_q = cut(ring, four, T, AT_H, HD)
        w_out = ring[:, 0:2 * SLOT].rearrange("p (k c) -> p k c", k=KD)
        ca_wq = cut(slot(2), 0, KD, CA_H * CA_HD)
        ca_wo = cut(slot(3), 0, CA_H, D)
        rope_t = [cut(W, 2048 + i * 1024, T, AT_H, HD // 2) for i in range(2)]
        qT_at = cut(slot(7), 0, 4, S)
        p_at = [slot(7)[:, 2048 + i * S:2048 + (i + 1) * S] for i in range(4)]
        pt_at = [cut(slot(6), i * 2048, T, S) for i in range(2)]
        qT_ca = cut(W, 2048, CA_H, S)
        oT_ca = cut(W, 4096, CA_H, S)
        p_ca = [W[:, 6144 + i * N_MEM:6144 + (i + 1) * N_MEM] for i in range(4)]
        pt_ca = [cut(W, 7168, 2, S), cut(W, 8192, 2, S)]
        affT, left, slotT, zero16 = (W[0:N_EXP, 2048 + i * S:2048 + (i + 1) * S] for i in range(4))
        top8 = W[0:N_EXP, 4096:4096 + CAP]

        xsT = cut(W, 0, KD, P)
        silu_g = cut(W, 1024, 2, BANK)
        hid = cut(W, 2048, 2, BANK)
        hidT = [cut(W, 3072 + b * 512, 4, 2, CAP) for b in range(2)]
        sel = cut(W, 4096, T, P)
        selg = cut(W, 4608, T, P)
        selgT = W[:, 5120:5632]
        ypair = W[:, 5632:6656]

        R2 = 2 * SLOT
        blk = [slot(0), slot(1)]
        h2T = cut(ring, R2, KD, S)
        hcT = cut(ring, R2 + 4096, KD, CTX)
        oaT = cut(ring, R2 + 6144, 4, S)
        ctx_n = cut(ring, R2 + 8192, 2, D)
        kT_mla = cut(ring, R2 + 8192, MLA_H, NTOK, parts=QK_MLA)
        pt2 = [cut(ring, R2 + 14336 + i * 3072, KT2, S) for i in range(2)]
        q_tok = cut(ring, R2 + 14336, T, MLA_H, QK_MLA)
        cq = cut(ring, R2 + 17408, T, Q_LORA)
        cqT = cut(ring, R2 + 18432, 2, S)
        rope2_t = [cut(ring, R2 + 19456 + i * 128, MLA_H, 2, 8) for i in range(2)]
        ckv = cut(ring, R2 + 20480, KT2, KV_LORA + ROPE)
        ckvT = ring[:, R2 + 21440:R2 + 22208]
        p2b = [ring[:, R2 + 22208 + i * NTOK:R2 + 22208 + (i + 1) * NTOK] for i in range(3)]
        va = cut(W, 0, KT2, MLA_H * HD)
        uq = cut(W, 4096, 2, MLA_H * QK_MLA)
        ukv = cut(W, 5632, MLA_H, NOPE + HD)
        ctx_t = cut(W, 6656, 2, D)
        sc_rep = cut(W, 8704, KD, P)
        g_row = W[:, 0:D]
        qT_mla = cut(hn_flat, 0, MLA_H, S, parts=QK_MLA)
        qbT = cut(hn_flat, 0, 4, S)
        obT = cut(hn_flat, 2048, 4, S)
        kbT = cut(ring, R2 + 8192, 4, NTOK)
        vb = cut(ring, R2 + 11264, KT2, NA_H * HD)
        gate_row = W[:, 0:D]
        na_table = cut(W, 3072, NA_H, 14 * GRID_W)
        woa = cut(ring, R2 + 8192, 4, D)
        wob = cut(ring, R2 + 12288, 4, D)
        yT = cut(ring, R2 + 16384, KD, S)
        w_out2 = [cut(W, 3072, 4, D), cut(ring, R2 + 20480, 4, D)]
        sg = [W[:, 7168 + i * S:7168 + (i + 1) * S] for i in range(4)]
        ysum = [W[:, 9216:9216 + S], W[:, 2048:2048 + S]]
        g_fin = W[:, D:2 * D]

        na_dram = nc.dram_tensor("na_scratch", [NA_H * (2 * NA_KR - 1), GRID_W, GRID_W], F32, kind="Internal").ap()

        def copy(eng, o, i, scale=None, bias=None):
            if eng is act:
                kw = {}
                if scale is not None:
                    kw["scale"] = scale
                if bias is not None:
                    kw["bias"] = bias
                return act.activation(o, i, ACT.Identity, **kw)
            if scale is None and bias is None:
                return dve.tensor_copy(o, i)
            if scale is None:
                return dve.tensor_scalar(o, i, bias, None, ALU.add)
            if bias is None:
                return dve.tensor_scalar(o, i, scale, None, ALU.mult)
            return dve.tensor_scalar(o, i, scale, bias, ALU.mult, ALU.add)

        norms = [0, 0]

        def rms_rows(src, dst, tiles, width, mark):
            ss, ms, rt, rs = (stat[:, i * 8:i * 8 + tiles] for i in range(4))
            squared, mean_ready, root_ready = sem("rows_squared"), sem("mean_ready"), sem("root_ready")
            norms[0] += 1
            norms[1] += tiles
            turn, rows = norms

            def on_act(junk=None):
                for t in range(tiles):
                    act.activation((junk or dst)[:, t, :], src[:, t, :], ACT.Square,
                                   accum_out=ss[:, t:t + 1]).then_inc(squared, 1)
                act.wait_ge(mean_ready, turn)
                act.activation(rt, ms, ACT.Sqrt).then_inc(root_ready, 1)

            def on_dve():
                dve.wait_ge(squared, rows)
                dve.tensor_scalar(ms, ss, 1.0 / width, EPS, ALU.mult, ALU.add).then_inc(mean_ready, 1)
                dve.wait_ge(root_ready, turn)
                link(dve.reciprocal(rs, rt))
                for t in range(tiles):
                    dve.tensor_scalar(dst[:, t, :], src[:, t, :], rs[:, t:t + 1], None, ALU.mult).then_inc(mark, 1)

            return on_act, on_dve

        def product(g, o, pairs):
            for i, (l, r) in enumerate(pairs):
                ins = pe.matmul(o, l, r, start=(i == 0), stop=(i == len(pairs) - 1))
            return ins

        def transpose_rows(groups, src, tiles):
            per = BANK // (tiles * P)
            for i, g in enumerate(groups):
                B.acquire(pe, g)
                for k in range(i * per, (i + 1) * per):
                    for t in range(tiles):
                        o = ((k - i * per) * tiles + t) * P
                        ins = pe.transpose(B.at(g)[:, o:o + P], src[:, t, k * P:(k + 1) * P], ident)
                B.filled(ins, g)

        def drain_rows(eng, groups, tiles, dst, scale=None, bias=None):
            per = BANK // (tiles * P)
            for i, g in enumerate(groups):
                if (g % 2 == 0) == (eng is act):
                    B.full(eng, g)
                    for k in range(i * per, (i + 1) * per):
                        o = (k - i * per) * tiles * P
                        ins = copy(eng, dst[:, k, :], B.at(g)[:, o:o + tiles * P],
                                   None if scale is None else scale[:, k:k + 1],
                                   None if bias is None else bias[:, k:k + 1])
                    B.release(ins, g)

        def drain(eng, g, o, i, scale=None, bias=None):
            if (g % 2 == 0) == (eng is act):
                B.full(eng, g)
                B.release(copy(eng, o, i, scale, bias), g)

        def plan_attention(name, heads, segs, nkt):
            units = [(c, qt, j) for c in range(len(heads)) for qt in range(T) for j in range(len(heads[c]))]
            per, lag, order = len(heads[0]) * T, 2, []
            for i in range(len(units) + lag + 1):
                if i < len(units):
                    order.append(("S", i))
                if 0 <= i - lag < len(units):
                    order.append(("T", i - lag))
                if i - lag >= 1 and (i - lag) % per == 0:
                    order.append(("O", (i - lag) // per - 1))
            size = {"S": len(segs), "T": -(-nkt // 4), "O": 1}
            return units, order, {(kind, i): list(B.take(size[kind])) for kind, i in order}

        def attention(name, heads, segs, q_at, k_at, v_at, dv, pbuf, ptbuf, o_out, ready, bias=None):
            nkt, nseg, np_ = sum(segs) // P, len(segs), len(pbuf)
            units, order, gid = plan_attention(name, heads, segs, nkt)
            sets = len(ptbuf) // len(heads[0])
            per = len(heads[0]) * T
            maxed, normed = sem(name + "_max"), sem(name + "_weights")
            exp_biased = sem(name + "_exp") if bias is not None else None
            tmp_max = lambda i: stat[:, 32 + 2 * (i % 4):34 + 2 * (i % 4)]
            neg_max = lambda i: stat[:, 40 + i % 4:41 + i % 4]
            sums = lambda i: stat[:, 44 + 2 * (i % 4):46 + 2 * (i % 4)]
            recip = lambda i: stat[:, 52 + 2 * (i % 4):54 + 2 * (i % 4)]
            turned = lambda c, j: ptbuf[(c % sets) * len(heads[0]) + j]
            last_out = gid["O", len(heads) - 1][0]

            def on_pe():
                for s, n in ready:
                    pe.wait_ge(s, n)
                for kind, i in order:
                    gs = gid[kind, i]
                    if kind == "S":
                        c, qt, j = units[i]
                        for si, g in enumerate(gs):
                            B.acquire(pe, g)
                            B.filled(product(g, B.at(g)[:, 0:segs[si]], [(q_at(heads[c][j], qt), k_at(heads[c][j], si))]), g)
                    elif kind == "T":
                        pe.wait_ge(normed, i + 1)
                        for n, g in enumerate(gs):
                            B.acquire(pe, g)
                            for kt in range(4 * n, min(4 * n + 4, nkt)):
                                ins = pe.transpose(B.at(g)[:, (kt % 4) * P:(kt % 4 + 1) * P],
                                                   pbuf[i % np_][:, kt * P:(kt + 1) * P], ident)
                            B.filled(ins, g)
                    else:
                        g = gs[0]
                        B.acquire(pe, g)
                        for u in range(i * per, (i + 1) * per):
                            for gt in gid["T", u]:
                                B.drained(pe, gt)
                        for kt in range(nkt):
                            for j, h in enumerate(heads[i]):
                                ins = pe.matmul(B.at(g)[j * dv:(j + 1) * dv, :], v_at(h, kt), turned(i, j)[:, kt, :],
                                                start=(kt == 0), stop=(kt == nkt - 1), skip_group_check=True)
                        B.filled(ins, g)

            def on_act():
                for kind, i in order:
                    gs = gid[kind, i]
                    if kind == "S":
                        act.wait_ge(maxed, i + 1)
                        if i >= np_ and bias is None:
                            B.full(act, gid["T", i - np_][-1])
                        o = 0
                        for n, g in enumerate(gs):
                            dst = pbuf[i % np_][:, o:o + segs[n]]
                            o += segs[n]
                            if bias is not None and n == 0:
                                act.activation(dst, dst, ACT.Exp, bias=neg_max(i),
                                               accum_out=sums(i)[:, 0:1]).then_inc(exp_biased, 1)
                            else:
                                B.release(act.activation(dst, B.at(g)[:, 0:segs[n]], ACT.Exp, bias=neg_max(i),
                                                         accum_out=sums(i)[:, n:n + 1]), g)
                    elif kind == "T":
                        c, qt, j = units[i]
                        if qt == 0 and j == 0 and c >= sets:
                            B.full(act, gid["O", c - sets][0])
                        for n, g in enumerate(gs):
                            m = min(4, nkt - 4 * n)
                            B.full(act, g)
                            B.release(act.activation(turned(c, j)[:, 4 * n:4 * n + m, qt * P:(qt + 1) * P],
                                                     B.at(g)[:, 0:m * P].rearrange("p (k q) -> p k q", k=m),
                                                     ACT.Identity), g)

            def on_dve():
                def divide(i):
                    if bias is not None:
                        dve.wait_ge(exp_biased, i + 1)
                    for g in gid["S", i][1 if bias is not None else 0:]:
                        B.drained(dve, g)
                    s = sums(i)[:, 0:1]
                    if nseg == 2:
                        link(dve.tensor_tensor(recip(i)[:, 0:1], sums(i)[:, 0:1], sums(i)[:, 1:2], ALU.add))
                        s = recip(i)[:, 0:1]
                    link(dve.reciprocal(recip(i)[:, 1:2], s))
                    dve.tensor_scalar(pbuf[i % np_], pbuf[i % np_], recip(i)[:, 1:2], None, ALU.mult).then_inc(normed, 1)

                for kind, i in order:
                    gs = gid[kind, i]
                    if kind == "S":
                        c, qt, j = units[i]
                        for n, g in enumerate(gs):
                            B.full(dve, g)
                            if bias is not None and n == 0:
                                if i >= np_:
                                    B.full(dve, gid["T", i - np_][-1])
                                B.release(dve.tensor_tensor_reduce(
                                    out=pbuf[i % np_][:, 0:segs[0]], in0=B.at(g)[:, 0:segs[0]],
                                    in1=bias(heads[c][j], qt), scale=1.0, scalar=NEG * 2, op0=ALU.add, op1=ALU.max,
                                    accum_out=tmp_max(i)[:, 0:1]), g)
                                B.drained(dve, g)
                            elif nseg == 1:
                                dve.tensor_reduce(neg_max(i), B.at(g)[:, 0:segs[0]], AX, ALU.max,
                                                  negate=True).then_inc(maxed, 1)
                            else:
                                link(dve.tensor_reduce(tmp_max(i)[:, n:n + 1], B.at(g)[:, 0:segs[n]], AX, ALU.max))
                        if nseg == 2:
                            dve.tensor_reduce(neg_max(i), tmp_max(i), AX, ALU.max, negate=True).then_inc(maxed, 1)
                        if i >= 1:
                            divide(i - 1)
                        if i == len(units) - 1:
                            divide(i)
                    elif kind == "O":
                        B.full(dve, gs[0])
                        B.release(o_out(i, B.at(gs[0])), gs[0])

            return on_pe, on_act, on_dve, last_out

        g_memT = B.take(4)
        g_kca = B.take(2)
        g_vca = B.take(2)

        def memory_pe():
            pe.wait_ge(sem("const_in"), 16)
            pe.wait_ge(sem("mem_in"), 16)
            transpose_rows(g_memT, mem, 2)
            pe.wait_ge(sem("ca_wkv_in"), 16)
            for g in g_memT:
                B.drained(pe, g)
            for i, g in enumerate(g_kca):
                B.acquire(pe, g)
                for h in (2 * i, 2 * i + 1):
                    ins = product(g, B.at(g)[:, (h % 2) * N_MEM:(h % 2 + 1) * N_MEM],
                                  [(ca_wkv[:, k, h * CA_HD:(h + 1) * CA_HD], memT[:, k, :]) for k in range(KD)])
                B.filled(ins, g)
            for m, g in enumerate(g_vca):
                B.acquire(pe, g)
                B.filled(product(g, B.at(g), [(memT[:, k, m * P:(m + 1) * P], ca_wkv[:, k, BANK:]) for k in range(KD)]), g)

        def memory_drain(eng):
            drain_rows(eng, g_memT, 2, memT)
            for i, g in enumerate(g_kca):
                drain(eng, g, kT_ca[:, 2 * i:2 * i + 2, :], B.at(g).rearrange("p (h m) -> p h m", h=2))
            for m, g in enumerate(g_vca):
                drain(eng, g, v_ca[:, m, :], B.at(g))

        hn_mix = sem("hn_mix")
        norm1_act, norm1_dve = rms_rows(x_sb, hn, T, D, hn_mix)
        g_h1 = B.take(KD)

        g_chan = B.take(6)
        g_gate = B.take(2)
        g_vo = B.take(T)
        g_aq = B.take(T)
        g_akv = B.take(T)

        def project_pe():
            pe.wait_ge(sem("w_in_in"), 16 * 8)
            pe.wait_ge(sem("w_gate_in"), 16)
            for g in g_h1:
                B.drained(pe, g)
            for c, g in enumerate(g_chan):
                B.acquire(pe, g)
                B.filled(product(g, B.at(g), [(w_in[:, k, c * P:(c + 1) * P], hT[:, k, :]) for k in range(KD)]), g)
            for i, g in enumerate(g_gate):
                B.acquire(pe, g)
                B.filled(product(g, B.at(g)[0:8, :], [(w_gate[:, k, 8 * i:8 * i + 8], hT[:, k, :]) for k in range(KD)]), g)
            for groups, c0, n in ((g_vo, 768, 512), (g_aq, 1280, 512), (g_akv, 1792, 256)):
                for t, g in enumerate(groups):
                    B.acquire(pe, g)
                    B.filled(product(g, B.at(g)[:, 0:n], [(hT[:, k, t * P:(t + 1) * P], w_in[:, k, c0:c0 + n])
                                                         for k in range(KD)]), g)

        def project_act():
            for c, g in enumerate(g_chan):
                B.full(act, g)
                if c == 0:
                    act.wait_ge(sem("pads"), 2)
                dst = upad[:, c, PADL:PADL + S] if c < 2 else qkpad[:, c - 2, 2:2 + S]
                B.release(copy(act, dst, B.at(g)), g)
            act.wait_ge(sem("columns_in"), 16 * N_COLUMNS)
            for g, dst, b in zip(g_gate, grow[0:2], (gate_i, gate_f)):
                B.full(act, g)
                B.release(copy(act, dst, B.at(g)[0:8, :], None, b), g)
            for t, g in enumerate(g_vo):
                B.full(act, g)
                if t == 0:
                    act.wait_ge(sem("pads"), 3)
                act.activation(sig_o[:, t, :], B.at(g)[:, 256:512], ACT.Sigmoid).then_inc(sem("sig_o"), 1)
                B.release(copy(act, v_aug[:, t, :, 0:HD], B.at(g)[:, 0:256].rearrange("p (h d) -> p h d", h=ML_H)), g)
            for t, g in enumerate(g_aq):
                B.full(act, g)
                B.release(copy(act, aq[:, t].rearrange("p (i g) d -> p g i d", g=2),
                               B.at(g).rearrange("p (g i d) -> p g i d", g=2, i=4)), g)
            for t, g in enumerate(g_akv):
                B.full(act, g)
                act.activation(ak[:, t], B.at(g)[:, 0:128].rearrange("p (h d) -> p h d", h=2),
                               ACT.Identity).then_inc(sem("ak"), 1)
                B.release(copy(act, av[:, t, :], B.at(g)[:, 128:256]), g)

        def pool_dve():
            for g in g_chan[0:2]:
                B.drained(dve, g)
            L = UP
            link(dve.tensor_tensor(p1[:, :, 1:L], upad[:, :, 0:L - 1], upad[:, :, 1:L], ALU.add))
            link(dve.tensor_tensor(p2[:, :, 2:L - 1], p1[:, :, 1:L - 2], p1[:, :, 3:L], ALU.add))
            link(dve.tensor_tensor(p3[:, 4:L - 3], p2[:, 1, 2:L - 5], p2[:, 1, 6:L - 1], ALU.add))
            link(dve.tensor_tensor(p1[64:128, 1, 8:L - 7], p3[64:128, 4:L - 11], p3[64:128, 12:L - 3], ALU.add))
            dve.wait_ge(sem("inv_n_in"), 16)
            B.full(dve, g_h1[-1])
            w = slice(PADL, PADL + S)
            for c, lo, hi, s in ((0, 0, 64, p1[0:64, 0, w]), (0, 64, 128, p2[64:128, 0, w]),
                                 (1, 0, 64, p3[0:64, w]), (1, 64, 128, p1[64:128, 1, w])):
                link(dve.tensor_tensor(d_pool[lo:hi, c, :], s, inv_n[lo:hi, c, :], ALU.mult))
                dve.tensor_tensor(d_pool[lo:hi, c, :], d_pool[lo:hi, c, :], upad[lo:hi, c, w],
                                  ALU.subtract).then_inc(sem("pooled"), 1)

        def pool_pe():
            pe.wait_ge(sem("pooled"), 4)
            pe.wait_ge(sem("pool_w_in"), 16)
            for c, g in enumerate(g_pool):
                B.acquire(pe, g)
                for lo in (0, 64):
                    ins = pe.matmul(B.at(g)[lo:lo + 64, :], pool_w[lo:lo + 64, c, :], d_pool[lo:lo + 64, c, :],
                                    start=True, stop=True)
                B.filled(ins, g)

        def pool_act():
            for c, g in enumerate(g_pool):
                B.full(act, g)
                B.release(copy(act, ymixT[:, c, :], B.at(g), pool_scale[:, c:c + 1]), g)

        def conv_dve():
            for g in g_chan[2:6]:
                B.drained(dve, g)
            for c in range(4):
                link(dve.tensor_scalar(qkT[:, c, :], qkpad[:, c, 0:S], conv_w[:, c, 0:1], None, ALU.mult))
                for w in range(1, ML_CONV):
                    ins = dve.scalar_tensor_tensor(out=qkT[:, c, :], in0=qkpad[:, c, w:w + S], scalar=conv_w[:, c, w:w + 1],
                                                   in1=qkT[:, c, :], op0=ALU.mult, op1=ALU.add)
                    if w < ML_CONV - 1:
                        link(ins)
                    else:
                        ins.then_inc(sem("conv"), 1)

        def conv_act():
            for c in range(4):
                act.wait_ge(sem("conv"), c + 1)
                act.activation(qkT[:, c, :], qkT[:, c, :], ACT.Silu).then_inc(sem("qk_silu"), 1)

        gi, gf, e_f, l_f, bsum, arow, mrow, bm = grow
        arow2, mrow2, bm2 = gi, l_f, gf
        g_cols = B.take(1)
        g_pool = B.take(2)
        rows_f, rows_b = sem("gate_rows_f"), sem("gate_rows_b")

        def gates_dve():
            for g in g_gate:
                B.drained(dve, g)
            dve.scalar_tensor_tensor(out=e_f, in0=gf, scalar=-1.0, in1=gf, op0=ALU.mult, op1=ALU.min).then_inc(sem("neg_abs_f"), 1)
            dve.wait_ge(sem("log_f"), 1)
            link(dve.scalar_tensor_tensor(out=e_f, in0=gf, scalar=0.0, in1=l_f, op0=ALU.min, op1=ALU.subtract))
            ones8 = const[0:8, C_ONE:C_ONE + 1].to_broadcast([8, S])
            link(dve.tensor_tensor_scan(bsum, ones8, e_f, 0.0, ALU.mult, ALU.add))
            link(dve.tensor_tensor(arow, gi, bsum, ALU.subtract))
            link(dve.tensor_tensor_scan(mrow, arow, arow, 0.0, ALU.max, ALU.max))
            link(dve.tensor_tensor(bm, bsum, mrow, ALU.add))
            dve.tensor_scalar(mrow, mrow, -1.0, None, ALU.mult).then_inc(rows_f, 1)
            link(dve.tensor_tensor_scan(bsum[:, ::-1], ones8, e_f[:, ::-1], 0.0, ALU.mult, ALU.add))
            link(dve.tensor_tensor(arow2, gi, bsum, ALU.subtract))
            link(dve.tensor_tensor_scan(mrow2[:, ::-1], arow2[:, ::-1], arow2[:, ::-1], 0.0, ALU.max, ALU.max))
            link(dve.tensor_tensor(bm2, bsum, mrow2, ALU.add))
            dve.tensor_scalar(mrow2, mrow2, -1.0, None, ALU.mult).then_inc(rows_b, 1)
            B.full(dve, g_cols[0])
            v = B.at(g_cols[0])[:, 0:P].rearrange("p (k t r) -> p k t r", k=4, t=T)
            B.release(dve.tensor_copy(gcols, v), g_cols[0])

        def gates_act():
            act.wait_ge(sem("neg_abs_f"), 1)
            act.activation(e_f, e_f, ACT.Exp).then_inc(sem("exp_f"), 1)
            act.wait_ge(sem("exp_f"), 1)
            act.activation(l_f, e_f, ACT.Ln, bias=1.0).then_inc(sem("log_f"), 1)
            B.drained(act, g_cols[0])
            act.activation(gcols[:, 2:4], gcols[:, 2:4], ACT.Exp, scale=-1.0).then_inc(sem("exp_m"), 1)

        def gates_pe():
            pe.wait_ge(rows_f, 1)
            pe.wait_ge(rows_b, 1)
            g = g_cols[0]
            B.acquire(pe, g)
            for k, r in enumerate((arow, arow2, bm, bm2)):
                for t in range(T):
                    ins = pe.transpose(B.at(g)[:, (k * T + t) * 8:(k * T + t) * 8 + 8], r[:, t * P:(t + 1) * P], ident[0:8, 0:8])
            B.filled(ins, g)

        g_ml = [B.take(10) for _ in range(ML_H)]

        def mlstm_pe():
            pe.wait_ge(sem("qk_silu"), 4)
            for h in range(ML_H):
                lo, c = (h % 2) * HD, h // 2
                gs = g_ml[h]
                for i in range(T):
                    B.acquire(pe, gs[i])
                    B.filled(product(gs[i], B.at(gs[i]), [(qkT[lo:lo + HD, 2 + c, i * P:(i + 1) * P], qkT[lo:lo + HD, c, :])]), gs[i])
                for d, m, mask in ((0, mrow, C_MF), (1, mrow2, C_MB)):
                    r = d * ML_H + h
                    pick = ident[0:8, r:r + 1].to_broadcast([8, P])
                    g0, g1 = gs[4 + 2 * d], gs[5 + 2 * d]
                    B.acquire(pe, g0)
                    B.filled(product(g0, B.at(g0), [(pick, m)]), g0)
                    B.acquire(pe, g1)
                    triangle = const[:, mask:mask + P].unsqueeze(1).to_broadcast([P, T, P])
                    B.filled(product(g1, B.at(g1), [(pick, m), (ident, triangle)]), g1)
                for d in range(2):
                    g = gs[8 + d]
                    B.acquire(pe, g)
                    if d == 0:
                        pe.wait_ge(sem("ml_weights0"), T * (h + 1))
                    else:
                        for i in range(T):
                            B.drained(pe, gs[i])
                    for j in range(T):
                        tiles = range(0, j + 1) if d == 0 else range(j, T)
                        ins = product(g, B.at(g)[:, j * (HD + 1):(j + 1) * (HD + 1)],
                                      [(Pt[d][:, i, j * P:(j + 1) * P], v_aug[:, i, h, :]) for i in tiles])
                    B.filled(ins, g)

        def off_diagonal(d, i):
            return slice((i + 1) * P, S) if d == 0 else slice(0, i * P)

        def mlstm_act():
            for h in range(ML_H):
                gs = g_ml[h]
                for d in range(2):
                    r = d * ML_H + h
                    g0, g1 = gs[4 + 2 * d], gs[5 + 2 * d]
                    if h:
                        B.full(act, g_ml[h - 1][8 + d])
                    B.full(act, g0)
                    rest = range(0, T - 1) if d == 0 else range(1, T)
                    for i in rest:
                        o = off_diagonal(d, i)
                        ins = act.activation(Pt[d][:, i, o], B.at(g0)[:, o], ACT.Exp, bias=gcols[:, d, i, r:r + 1])
                    B.release(ins, g0)
                    B.full(act, g1)
                    for i in range(T):
                        o = slice(i * P, (i + 1) * P)
                        ins = act.activation(Pt[d][:, i, o], B.at(g1)[:, o], ACT.Exp, bias=gcols[:, d, i, r:r + 1])
                    B.release(ins, g1)

        def mlstm_dve():
            for h in range(ML_H):
                gs = g_ml[h]
                for d in range(2):
                    B.drained(dve, gs[4 + 2 * d])
                    B.drained(dve, gs[5 + 2 * d])
                    for i in range(T):
                        o = slice(i * P, S) if d == 0 else slice(0, (i + 1) * P)
                        B.full(dve, gs[i])
                        ins = dve.scalar_tensor_tensor(out=Pt[d][:, i, o], in0=B.at(gs[i])[:, o], scalar=HD ** -0.5,
                                                       in1=Pt[d][:, i, o], op0=ALU.mult, op1=ALU.mult)
                        if d == 0:
                            ins.then_inc(sem("ml_weights0"), 1)
                        else:
                            B.release(ins, gs[i])
                for d in range(2):
                    g, r = gs[8 + d], d * ML_H + h
                    B.full(dve, g)
                    v = B.at(g)[:, 0:T * (HD + 1)].rearrange("p (t e) -> p t e", t=T)
                    link(dve.tensor_copy(ml_stat[:, 1, :], v[:, :, HD]))
                    link(dve.scalar_tensor_tensor(out=ml_stat[:, 0, :], in0=ml_stat[:, 1, :], scalar=-1.0,
                                                  in1=ml_stat[:, 1, :], op0=ALU.mult, op1=ALU.max))
                    if h == 0 and d == 0:
                        dve.wait_ge(sem("exp_m"), 1)
                    link(dve.tensor_tensor(ml_stat[:, 1, :], ml_stat[:, 0, :], gcols[:, 2 + d, :, r], ALU.max))
                    link(dve.reciprocal(ml_stat[:, 2, :], ml_stat[:, 1, :]))
                    w = ml_stat[:, 2, :].unsqueeze(2).to_broadcast([P, T, HD])
                    if d == 0:
                        B.release(dve.tensor_tensor(hsum[:, :, h, :], v[:, :, 0:HD], w, ALU.mult), g)
                    else:
                        B.release(dve.tensor_tensor(htmp[:, :, h, :], v[:, :, 0:HD], w, ALU.mult), g)
                        B.drained(dve, g)
                        link(dve.tensor_tensor(hsum[:, :, h, :], hsum[:, :, h, :], htmp[:, :, h, :], ALU.add))
            link(dve.tensor_tensor(htmp, hsum, hsum, ALU.mult))
            link(dve.tensor_reduce(stat[:, 0:16].rearrange("p (t h) -> p t h", t=T), htmp, AX, ALU.add))
            dve.tensor_scalar(stat[:, 16:32], stat[:, 0:16], 1.0 / HD, EPS, ALU.mult, ALU.add).then_inc(sem("ml_mean"), 1)
            dve.wait_ge(sem("ml_root"), 1)
            link(dve.reciprocal(stat[:, 16:32], stat[:, 0:16]))
            rs = stat[:, 16:32].rearrange("p (t h) -> p t h", t=T).unsqueeze(3).to_broadcast([P, T, ML_H, HD])
            link(dve.tensor_tensor(hsum, hsum, rs, ALU.mult))
            dve.wait_ge(sem("rows_in"), 16 * 3)
            flat = hsum.rearrange("p t h d -> p t (h d)")
            link(dve.tensor_tensor(flat, flat, ml_g.unsqueeze(1).to_broadcast([P, T, ML_H * HD]), ALU.mult))
            dve.wait_ge(sem("sig_o"), T)
            dve.tensor_tensor(flat, flat, sig_o, ALU.mult).then_inc(sem("y_mlstm"), 1)

        def mlstm_norm_act():
            act.wait_ge(sem("ml_mean"), 1)
            act.activation(stat[:, 0:16], stat[:, 16:32], ACT.Sqrt).then_inc(sem("ml_root"), 1)

        g_mlT = B.take(2)

        def mlstm_out_pe():
            pe.wait_ge(sem("y_mlstm"), 1)
            transpose_rows(g_mlT, hsum.rearrange("p t h d -> p t (h d)"), T)

        def mlstm_out_drain(eng):
            drain_rows(eng, g_mlT, T, ymixT[:, 2:4, :])

        g_qT = B.take(4)
        g_kT = B.take(1)

        def rope_pairs(v, heads):
            even, odd = v[:, :, :, 0::2], v[:, :, :, 1::2]
            cos, sin = (const[:, c:c + 128].rearrange("p (t f) -> p t f", t=T).unsqueeze(2).to_broadcast([P, T, heads, 32])
                        for c in (C_COS, C_SIN))
            t0, t1 = (r[:, :, 0:heads, :] for r in rope_t)
            for t in range(T):
                link(dve.tensor_tensor(t0[:, t], even[:, t], sin[:, t], ALU.mult))
                link(dve.tensor_tensor(t1[:, t], odd[:, t], sin[:, t], ALU.mult))
                link(dve.tensor_tensor(even[:, t], even[:, t], cos[:, t], ALU.mult))
                link(dve.tensor_tensor(odd[:, t], odd[:, t], cos[:, t], ALU.mult))
                link(dve.tensor_tensor(even[:, t], even[:, t], t1[:, t], ALU.subtract))
                ins = dve.tensor_tensor(odd[:, t], odd[:, t], t0[:, t], ALU.add)
                if t < T - 1:
                    link(ins)
            return ins

        def heads_dve():
            for g in g_aq:
                B.drained(dve, g)
            for v, heads, gn, o, name in ((aq, AT_H, qg, 0, "q"), (ak, 2, kg, 32, "k")):
                if name == "k":
                    dve.wait_ge(sem("ak"), T)
                n = T * heads
                sq = sq_q[:, :, 0:heads, :]
                link(dve.tensor_tensor(sq, v, v, ALU.mult))
                link(dve.tensor_reduce(stat[:, 0:n].rearrange("p (t h) -> p t h", t=T), sq, AX, ALU.add))
                dve.tensor_scalar(stat[:, 32:32 + n], stat[:, 0:n], 1.0 / HD, EPS, ALU.mult,
                                  ALU.add).then_inc(sem(f"head_mean_{name}"), 1)
                dve.wait_ge(sem(f"head_root_{name}"), 1)
                link(dve.reciprocal(stat[:, 32:32 + n], stat[:, 0:n]))
                rs = stat[:, 32:32 + n].rearrange("p (t h) -> p t h", t=T).unsqueeze(3).to_broadcast([P, T, heads, HD])
                link(dve.tensor_tensor(v, v, rs, ALU.mult))
                flat = v.rearrange("p t h d -> p (t h) d")
                link(dve.tensor_tensor(flat, flat, gn.unsqueeze(1).to_broadcast([P, n, HD]), ALU.mult))
                rope_pairs(v, heads).then_inc(sem(f"roped_{name}"), 1)

        def heads_act():
            for name, n in (("q", T * AT_H), ("k", T * 2)):
                act.wait_ge(sem(f"head_mean_{name}"), 1)
                act.activation(stat[:, 0:n], stat[:, 32:32 + n], ACT.Sqrt).then_inc(sem(f"head_root_{name}"), 1)

        def heads_pe():
            pe.wait_ge(sem("roped_q"), 1)
            for i, g in enumerate(g_qT):
                B.acquire(pe, g)
                for t in range(T):
                    ins = pe.transpose(B.at(g)[:, t * P:(t + 1) * P], aq[:, t, 2 * i:2 * i + 2, :].rearrange("p g d -> p (g d)"), ident)
                B.filled(ins, g)
            pe.wait_ge(sem("roped_k"), 1)
            g = g_kT[0]
            B.acquire(pe, g)
            for t in range(T):
                ins = pe.transpose(B.at(g)[:, t * P:(t + 1) * P], ak[:, t].rearrange("p h d -> p (h d)"), ident)
            B.filled(ins, g)

        def heads_drain(eng):
            for i, g in enumerate(g_qT):
                drain(eng, g, qT_at[:, i, :], B.at(g), HD ** -0.5)
            drain(eng, g_kT[0], kT_at, B.at(g_kT[0]))

        def heads_ready_pe():
            for g in (*g_qT, *g_kT):
                B.drained(pe, g)

        half = lambda h: slice((h // 4) * HD, (h // 4 + 1) * HD)
        attn_pe, attn_act, attn_dve, g_attn_end = attention(
            "attn", [(i, i + 4) for i in range(4)], [S],
            lambda h, qt: qT_at[half(h), h % 4, qt * P:(qt + 1) * P], lambda h, si: kT_at[half(h), :],
            lambda h, kt: av[:, kt, half(h)], HD, p_at, pt_at,
            lambda i, o: dve.tensor_copy(ymixT[:, 4 + i, :], o), [])

        g_out1 = B.take(2 * T)

        def add_product_pe(groups, lhs, rhs, chunks):
            for i, g in enumerate(groups):
                t, n = i // 2, i % 2
                B.acquire(pe, g)
                B.filled(product(g, B.at(g), [(lhs(k)[:, t * P:(t + 1) * P], rhs(k)[:, n * BANK:(n + 1) * BANK])
                                              for k in range(chunks)]), g)

        def add_product_dve(groups):
            for i, g in enumerate(groups):
                t, n = i // 2, i % 2
                o = x_sb[:, t, n * BANK:(n + 1) * BANK]
                B.full(dve, g)
                B.release(dve.tensor_tensor(o, B.at(g), o, ALU.add), g)

        def out1_pe():
            pe.wait_ge(sem("w_out_in"), 16 * 3)
            for g in (*g_pool, *g_mlT, g_attn_end):
                B.drained(pe, g)
            add_product_pe(g_out1, lambda k: ymixT[:, k, :], lambda k: w_out[:, k, :], KD)

        hn_mem = sem("hn_mem")
        norm2_act_, norm2_dve = rms_rows(x_sb, hn, T, D, hn_mem)
        g_h2 = B.take(KD)
        g_qca = B.take(CA_H)

        def norm2_act():
            for g in g_out1:
                B.drained(act, g)
            norm2_act_()

        def qca_pe():
            pe.wait_ge(sem("ca_wq_in"), 16)
            for g in g_h2:
                B.drained(pe, g)
            for h, g in enumerate(g_qca):
                B.acquire(pe, g)
                B.filled(product(g, B.at(g), [(ca_wq[:, k, h * CA_HD:(h + 1) * CA_HD], hT[:, k, :]) for k in range(KD)]), g)

        def qca_drain(eng):
            for h, g in enumerate(g_qca):
                drain(eng, g, qT_ca[:, h, :], B.at(g), CA_HD ** -0.5)

        ca_pe, ca_act, ca_dve, g_ca_end = attention(
            "ca", [(h,) for h in range(CA_H)], [N_MEM],
            lambda h, qt: qT_ca[:, h, qt * P:(qt + 1) * P], lambda h, si: kT_ca[:, h, :],
            lambda h, kt: v_ca[:, kt, h * CA_HD:(h + 1) * CA_HD], CA_HD, p_ca, pt_ca,
            lambda i, o: dve.tensor_copy(oT_ca[:, i, :], o), [])
        g_out2 = B.take(2 * T)

        def ca_all_pe():
            for g in g_qca:
                B.drained(pe, g)
            ca_pe()
            pe.wait_ge(sem("ca_wo_in"), 16)
            B.drained(pe, g_ca_end)
            add_product_pe(g_out2, lambda k: oT_ca[:, k, :], lambda k: ca_wo[:, k, :], CA_H)

        hn_ffn = sem("hn_ffn")
        norm3_act_, norm3_dve = rms_rows(x_sb, hn, T, D, hn_ffn)
        g_h3 = B.take(KD)
        g_logit = B.take(1)
        g_affT = B.take(1)
        g_slots = B.take(1)

        def norm3_act():
            for g in g_out2:
                B.drained(act, g)
            norm3_act_()

        def route_pe():
            for g in g_h3:
                B.drained(pe, g)
            g = g_logit[0]
            B.acquire(pe, g)
            for t in range(T):
                ins = product(g, B.at(g)[:, t * N_EXP:(t + 1) * N_EXP],
                              [(hT[:, k, t * P:(t + 1) * P], router_w[:, k, :]) for k in range(KD)])
            B.filled(ins, g)
            pe.wait_ge(sem("aff"), 1)
            g = g_affT[0]
            B.acquire(pe, g)
            for t in range(T):
                ins = pe.transpose(B.at(g)[0:N_EXP, t * P:(t + 1) * P], aff[:, t, :], ident)
            B.filled(ins, g)
            pe.wait_ge(sem("slot_rows"), 1)
            g = g_slots[0]
            B.acquire(pe, g)
            for t in range(T):
                ins = pe.transpose(B.at(g)[:, t * N_EXP:(t + 1) * N_EXP], slotT[:, t * P:(t + 1) * P], ident[0:N_EXP, 0:N_EXP])
            B.filled(ins, g)

        def route_act():
            B.drained(act, g_logit[0])
            act.activation(aff, aff, ACT.Exp).then_inc(sem("exp_logits"), 1)

        def route_dve():
            g = g_logit[0]
            B.full(dve, g)
            v = B.at(g)[:, 0:T * N_EXP].rearrange("p (t e) -> p t e", t=T)
            link(dve.tensor_reduce(stat[:, 32:36], v, AX, ALU.max))
            B.release(dve.tensor_tensor(aff, v, stat[:, 32:36].unsqueeze(2).to_broadcast([P, T, N_EXP]), ALU.subtract), g)
            dve.wait_ge(sem("exp_logits"), 1)
            link(dve.tensor_reduce(stat[:, 36:40], aff, AX, ALU.add))
            link(dve.reciprocal(stat[:, 40:44], stat[:, 36:40]))
            dve.tensor_tensor(aff, aff, stat[:, 40:44].unsqueeze(2).to_broadcast([P, T, N_EXP]), ALU.mult).then_inc(sem("aff"), 1)
            g = g_affT[0]
            B.full(dve, g)
            B.release(dve.tensor_copy(affT, B.at(g)[0:N_EXP, :]), g)
            B.drained(dve, g)
            link(dve.tensor_copy(left, affT))
            for r in range(CAP // 8):
                eight = top8[:, 8 * r:8 * r + 8]
                link(dve.max(eight, left))
                link(dve.match_replace(left, eight, left, -1.0))
            link(dve.tensor_tensor(left, left, affT, ALU.not_equal))
            link(dve.memset(zero16, 1.0))
            link(dve.tensor_tensor_scan(slotT, zero16, left, 0.0, ALU.mult, ALU.add))
            link(dve.tensor_tensor(slotT, slotT, left, ALU.mult))
            dve.tensor_scalar(slotT, slotT, 1.0, None, ALU.subtract).then_inc(sem("slot_rows"), 1)
            g = g_slots[0]
            B.full(dve, g)
            B.release(dve.tensor_copy(slot_of, B.at(g)[:, 0:T * N_EXP].rearrange("p (t e) -> p t e", t=T)), g)
            B.drained(dve, g)

        PAIRS, PIECES = N_EXP // 2, 24
        AHEAD = NSLOT
        xsT_full, xsT_sb = sem("xsT_full"), [sem("xsT_sb_act"), sem("xsT_sb_dve")]
        sel_ready, selgT_full, selgT_sb = sem("sel_ready"), sem("selgT_full"), sem("selgT_sb")
        silu_ready, hid_ready = sem("silu_ready"), sem("hid_ready")
        hidT_full, hidT_sb = sem("hidT_full"), [sem("hidT_sb_act"), sem("hidT_sb_dve")]
        y_sb = sem("y_sb")
        added_full, added = sem("added_full"), sem("added")
        posc_ready = sem("posc_ready")
        w_gu, w_down = a["expert_w_gu"][0], a["expert_w_down"][0]

        def piece_source(expert, i):
            if i < KD:
                return w_gu[bass.ds(expert, 1), i * P:(i + 1) * P, :].rearrange("e p f -> p (e f)")
            q = i - KD
            return w_down[bass.ds(expert, 1), q * 512:(q + 1) * 512, :].rearrange("e (j p) d -> p (e j) d", p=P)

        def piece_target(s, i):
            return slot(s) if i < KD else slot(s).rearrange("p (j d) -> p j d", j=4)

        def load_piece(expert, i, s):
            sp.dma_start(piece_target(s, i), piece_source(expert, i)).then_inc(slot_loaded[s], 16)

        def experts_sp():
            for i in range(AHEAD):
                if i == 0:
                    B.full(sp, g_out1[-1])
                if i == 2:
                    B.full(sp, g_qca[-1])
                if i == 3:
                    B.full(sp, g_out2[-1])
                if i == 7:
                    B.full(sp, g_slots[-1])
                load_piece(0, i, i)
            with sp.Fori(0, PAIRS - 1) as p:
                for n in range(AHEAD, PIECES + AHEAD):
                    e, i = n // 12, n % 12
                    sp.wait_ge(slot_free[n % NSLOT], 3 * p + n // NSLOT)
                    load_piece(2 * p + e, i, n % NSLOT)
            for n in range(AHEAD, PIECES):
                e, i = n // 12, n % 12
                sp.wait_ge(slot_free[n % NSLOT], 3 * (PAIRS - 1) + n // NSLOT)
                load_piece(2 * (PAIRS - 1) + e, i, n % NSLOT)

        GATHER, TURN = (4, 5), (4, 5)
        ADD_BANKS = (7, 4, 5, 0, 1, 2, 3, 6)

        def piece(n, p):
            s = n % NSLOT
            pe.wait_ge(slot_loaded[s], 48 * p + 16 * (n // NSLOT + 1))
            return slot(s)

        before_experts = range(B.next - NBANK, B.next)

        def experts_pe():
            for g in before_experts:
                B.drained(pe, g)
            with pe.Fori(0, PAIRS) as p:
                pe.wait_ge(sel_ready, p + 1)
                pe.wait_ge(added, 2 * T * p + 1)
                for k in range(KD):
                    for t in range(T):
                        ins = pe.matmul(psum[:, GATHER[k // 4], (k % 4) * P:(k % 4 + 1) * P], hn[:, t, k * P:(k + 1) * P],
                                        sel[:, t, :], start=(t == 0), stop=(t == T - 1))
                    if k % 4 == 3:
                        ins.then_inc(xsT_full, 1)
                for t in range(T):
                    ins = pe.transpose(psum[:, 7, t * P:(t + 1) * P], selg[:, t, :], ident)
                ins.then_inc(selgT_full, 1)
                pe.wait_ge(xsT_sb[0], p + 1)
                pe.wait_ge(xsT_sb[1], p + 1)
                for e in range(2):
                    for k in range(KD):
                        w = piece(12 * e + k, p)
                        for c in range(4):
                            for h in range(2):
                                ins = pe.matmul(psum[h * 64:(h + 1) * 64, c, :], xsT[:, k, e * CAP:(e + 1) * CAP],
                                                w[:, (2 * c + h) * BANK:(2 * c + h + 1) * BANK],
                                                start=(k == 0), stop=(k == KD - 1), skip_group_check=True)
                        ins.then_inc(slot_free[(12 * e + k) % NSLOT], 1)
                    for b in range(2):
                        pe.wait_ge(hid_ready, 4 * p + 2 * e + b + 1)
                        for j in range(4):
                            ins = pe.transpose(psum[:, TURN[b], j * P:(j + 1) * P], hid[:, b, j * P:(j + 1) * P], ident)
                        ins.then_inc(hidT_full, 1)
                    for q in range(4):
                        b, h = q // 2, q % 2
                        if h == 0:
                            pe.wait_ge(hidT_sb[b], 2 * p + e + 1)
                        if q == 0 and e == 1:
                            pe.wait_ge(y_sb, 4 * p + 2)
                        w = piece(12 * e + KD + q, p).rearrange("p (j d) -> p j d", j=4)
                        for j in range(4):
                            for n in range(2):
                                ins = pe.matmul(psum[n * 64:(n + 1) * 64, 6, :], hidT[b][:, j, h, :],
                                                w[:, j, n * BANK:(n + 1) * BANK], start=(q == 0 and j == 0),
                                                stop=(q == 3 and j == 3), skip_group_check=True)
                        ins.then_inc(slot_free[(12 * e + KD + q) % NSLOT], 1)
                pe.wait_ge(selgT_sb, p + 1)
                pe.wait_ge(y_sb, 4 * p + 4)
                for i, bank in enumerate(ADD_BANKS):
                    t, n = i // 2, i % 2
                    pe.matmul(psum[:, bank, :], selgT[:, t * P:(t + 1) * P], ypair[:, n * BANK:(n + 1) * BANK],
                              start=True, stop=True).then_inc(added_full, 1)
            pe.wait_ge(added, 2 * T * PAIRS + 1)

        def gu_done(eng, p, e):
            n = 12 * e + KD - 1
            eng.wait_ge(slot_free[n % NSLOT], 3 * p + n // NSLOT + 1)

        def y_done(eng, p, e):
            n = 12 * e + 11
            eng.wait_ge(slot_free[n % NSLOT], 3 * p + n // NSLOT + 1)

        def experts_act():
            with act.Fori(0, PAIRS) as p:
                act.wait_ge(xsT_full, 2 * p + 1)
                v = psum[:, GATHER[0], :].rearrange("p (k c) -> p k c", k=4)
                for k in range(4):
                    ins = act.activation(xsT[:, k, :], v[:, k, :], ACT.Identity, scale=gain["norm_ffn_g"][:, k:k + 1])
                ins.then_inc(xsT_sb[0], 1)
                for e in range(2):
                    gu_done(act, p, e)
                    for b in range(2):
                        act.activation(silu_g[:, b, :], psum[:, b, :], ACT.Silu).then_inc(silu_ready, 1)
                    act.wait_ge(hidT_full, 4 * p + 2 * e + 1)
                    act.activation(hidT[0].rearrange("p j h c -> p (j h c)"), psum[:, TURN[0], :],
                                   ACT.Identity).then_inc(hidT_sb[0], 1)
                    y_done(act, p, e)
                    for n in range(2):
                        act.activation(ypair[e * 64:(e + 1) * 64, n * BANK:(n + 1) * BANK], psum[n * 64:(n + 1) * 64, 6, :],
                                       ACT.Identity).then_inc(y_sb, 1)

        def experts_dve():
            link(dve.memset(stat[:, 0:1], 0.0))
            dve.memset(stat[:, 1:2], 0.0).then_inc(added, 1)
            iota = const[:, C_IOTA:C_IOTA + CAP]
            with dve.Fori(0, PAIRS) as p:
                dve.tensor_copy(posc, slot_of[:, :, bass.ds(2 * p, 2)]).then_inc(posc_ready, 1)
                dve.tensor_copy(gatec, aff[:, :, bass.ds(2 * p, 2)]).then_inc(posc_ready, 1)
                dve.wait_ge(posc_ready, 2 * p + 2)
                for t in range(T):
                    for e in range(2):
                        o = slice(e * CAP, (e + 1) * CAP)
                        dve.tensor_scalar(selg[:, t, o], iota, posc[:, t, e:e + 1], gatec[:, t, e:e + 1],
                                          ALU.is_equal, ALU.mult)
                        ins = dve.tensor_scalar(sel[:, t, o], iota, posc[:, t, e:e + 1], None, ALU.is_equal)
                ins.then_inc(sel_ready, 1)
                dve.wait_ge(xsT_full, 2 * p + 2)
                v = psum[:, GATHER[1], :].rearrange("p (k c) -> p k c", k=4)
                for k in range(4):
                    ins = dve.tensor_scalar(xsT[:, 4 + k, :], v[:, k, :], gain["norm_ffn_g"][:, 4 + k:5 + k], None, ALU.mult)
                ins.then_inc(xsT_sb[1], 1)
                dve.wait_ge(selgT_full, p + 1)
                dve.tensor_copy(selgT, psum[:, 7, :]).then_inc(selgT_sb, 1)
                for e in range(2):
                    for b in range(2):
                        dve.wait_ge(silu_ready, 4 * p + 2 * e + b + 1)
                        dve.tensor_tensor(hid[:, b, :], psum[:, 2 + b, :], silu_g[:, b, :], ALU.mult).then_inc(hid_ready, 1)
                    dve.wait_ge(hidT_full, 4 * p + 2 * e + 2)
                    dve.tensor_copy(hidT[1].rearrange("p j h c -> p (j h c)"), psum[:, TURN[1], :]).then_inc(hidT_sb[1], 1)
                for i, bank in enumerate(ADD_BANKS):
                    t, n = i // 2, i % 2
                    o = x_sb[:, t, n * BANK:(n + 1) * BANK]
                    dve.wait_ge(added_full, 2 * T * p + i + 1)
                    dve.tensor_tensor(o, psum[:, bank, :], o, ALU.add).then_inc(added, 1)

        w2, wm = a["w_in_2"][0], a["w_mod_2"][0]
        blocks = [(wm, j * BANK, BANK) for j in range(4)]
        blocks += [(w2, C2["ckv"], 160), (w2, C2["cq"], Q_LORA), (w2, C2["za"], BANK)]
        blocks += [(wm, j * BANK, BANK) for j in (4, 5)]
        blocks += [(w2, C2[n], BANK) for n in ("kb", "vb", "qb", "zb")]
        blocks += [(w2, C2[n] + j * BANK, BANK) for j in range(2) for n in ("ga", "gb")]
        BLOCK = dict(mod=0, ckv=4, cq=5, za=6, gate=7, kb=9, vb=10, qb=11, zb=12, g=13)
        block_loaded = [sem("block_loaded0"), sem("block_loaded1")]

        def block_view(b):
            n = blocks[b][2]
            return blk[b % 2][:, 0:KD * n].rearrange("p (k c) -> p k c", k=KD)

        def block_in(b):
            pe.wait_ge(block_loaded[b % 2], 16 * (b // 2 + 1))
            return block_view(b)

        last_of_block = {}

        def load_blocks(lo, hi):
            for b in range(lo, hi):
                src, c0, n = blocks[b]
                if b >= 2:
                    B.full(sp, last_of_block[b - 2])
                sp.dma_start(block_view(b), src[:, c0:c0 + n].rearrange("(k p) c -> p k c", p=P)).then_inc(block_loaded[b % 2], 16)

        g_mod = B.take(4)
        last_of_block.update({j: g_mod[j] for j in range(4)})

        def silu_c_act():
            act.wait_ge(sem("columns_in"), 16 * N_COLUMNS)
            act.activation(c_col, c_col, ACT.Silu).then_inc(sem("silu_c"), 1)

        def mod_pe():
            pe.wait_ge(sem("silu_c"), 1)
            for j, g in enumerate(g_mod):
                w = block_in(j)
                B.acquire(pe, g)
                for m in range(4):
                    ins = product(g, B.at(g)[:, 2 * m:2 * m + 2], [(w[:, k, m * P:(m + 1) * P], c_col[:, k, :]) for k in range(KD)])
                B.filled(ins, g)

        def mod_dve():
            for j, g in enumerate(g_mod):
                B.full(dve, g)
                v = mod[:, 4 * j:4 * j + 4, :]
                B.release(dve.tensor_tensor(v, B.at(g)[:, 0:8].rearrange("p (m v) -> p m v", m=4),
                                            b_mod_col[:, 4 * j:4 * j + 4].unsqueeze(2).to_broadcast([P, 4, 2]), ALU.add), g)
            B.drained(dve, g_mod[-1])
            link(dve.tensor_scalar(mod[:, KD:, :], mod[:, KD:, :], 1.0, None, ALU.add))
            dve.tensor_tensor(mod[:, KD:, :], mod[:, KD:, :], gain["norm_g_2"].unsqueeze(2).to_broadcast([P, KD, 2]),
                              ALU.mult).then_inc(sem("mod"), 1)

        hn_fin, hn_x2, hn_ctx = sem("hn_fin"), sem("hn_x2"), sem("hn_ctx")
        norm4_act_, norm4_dve_ = rms_rows(x_sb, hn, T, D, hn_fin)
        norm5_act_, norm5_dve = rms_rows(x_sb, hn, T, D, hn_x2)
        normc_act_, normc_dve = rms_rows(ctx_t, ctx_n, 2, D, hn_ctx)
        g_x2 = B.take(KD)
        g_ctx = B.take(4)

        def norms_act():
            act.wait_ge(added, 2 * T * PAIRS + 1)
            norm4_act_()
            act.wait_ge(sem("x_mid"), T)
            norm5_act_()
            act.wait_ge(sem("ctx_in"), 16)
            normc_act_()

        def norms_dve():
            norm4_dve_()
            dve.wait_ge(sem("g_row_in"), 16)
            for t in range(T):
                dve.wait_ge(hn_fin, t + 1)
                dve.tensor_tensor(x_sb[:, t, :], hn[:, t, :], g_row, ALU.mult).then_inc(sem("x_mid"), 1)
            norm5_dve()
            normc_dve()

        def turn2_pe():
            pe.wait_ge(hn_x2, T)
            transpose_rows(g_x2, hn, T)
            pe.wait_ge(hn_ctx, 2)
            transpose_rows(g_ctx, ctx_n, 2)

        def turn2_drain(eng):
            eng.wait_ge(sem("mod"), 1)
            drain_rows(eng, g_x2, T, h2T, mod[:, KD:, 0], mod[:, 0:KD, 0])
            drain_rows(eng, g_ctx, 2, hcT, mod[:, KD:, 1], mod[:, 0:KD, 1])

        def tokens(t, k):
            return h2T[:, k, t * P:(t + 1) * P] if t < T else hcT[:, k, (t - T) * P:(t - T + 1) * P]

        g_ckv = B.take(KT2)
        g_cq = B.take(T)
        g_za = B.take(4)
        last_of_block.update({4: g_ckv[-1], 5: g_cq[-1], 6: g_za[-1]})

        def mla_in_pe():
            for g in (*g_x2, *g_ctx):
                B.drained(pe, g)
            w = block_in(BLOCK["ckv"])
            for t, g in enumerate(g_ckv):
                B.acquire(pe, g)
                B.filled(product(g, B.at(g)[:, 0:160], [(tokens(t, k), w[:, k, :]) for k in range(KD)]), g)
            w = block_in(BLOCK["cq"])
            for t, g in enumerate(g_cq):
                B.acquire(pe, g)
                B.filled(product(g, B.at(g)[:, 0:Q_LORA], [(tokens(t, k), w[:, k, :]) for k in range(KD)]), g)
            w = block_in(BLOCK["za"])
            for c, g in enumerate(g_za):
                B.acquire(pe, g)
                B.filled(product(g, B.at(g), [(w[:, k, c * P:(c + 1) * P], h2T[:, k, :]) for k in range(KD)]), g)

        norm_kv_act, norm_kv_dve = rms_rows(ckv[:, :, 0:KV_LORA], ckv[:, :, 0:KV_LORA], KT2, KV_LORA, sem("ckv_n"))
        norm_q_act, norm_q_dve = rms_rows(cq, cq, T, Q_LORA, sem("cq_n"))

        def mla_in_act():
            for t, g in enumerate(g_ckv):
                B.full(act, g)
                B.release(copy(act, ckv[:, t, :], B.at(g)[:, 0:160]), g)
            for g in g_ckv:
                B.drained(act, g)
            norm_kv_act(junk=cut(ring, R2 + 17408 - 1024, KT2, KV_LORA))
            for t, g in enumerate(g_cq):
                B.full(act, g)
                B.release(copy(act, cq[:, t, :], B.at(g)[:, 0:Q_LORA]), g)
            for g in g_cq:
                B.drained(act, g)
            norm_q_act(junk=cut(ring, R2 + 14336, T, Q_LORA))
            for c, g in enumerate(g_za):
                B.full(act, g)
                B.release(act.activation(oaT[:, c, :], B.at(g), ACT.Silu), g)

        def rotate_halves(v, cos, sin, done=None):
            x1, x2 = v[:, :, :, 0, :], v[:, :, :, 1, :]
            n = v.shape[1]
            t0, t1 = (r[:, 0:n] for r in rope2_t)
            link(dve.tensor_tensor(t0, x1, sin, ALU.mult))
            link(dve.tensor_tensor(t1, x2, sin, ALU.mult))
            link(dve.tensor_tensor(x1, x1, cos, ALU.mult))
            link(dve.tensor_tensor(x2, x2, cos, ALU.mult))
            link(dve.tensor_tensor(x1, x1, t1, ALU.subtract))
            return dve.tensor_tensor(x2, x2, t0, ALU.add)

        cos2, sin2 = (const[:, c:c + 64].rearrange("p (t a f) -> p t a f", t=T, a=2) for c in (C_COS2, C_SIN2))

        def mla_in_dve():
            norm_kv_dve()
            kr = ckv[:, 0:T, KV_LORA:].rearrange("p t (a x f) -> p t a x f", a=2, x=2)
            rotate_halves(kr, cos2, sin2).then_inc(sem("kr"), 1)
            norm_q_dve()

        g_ckvT = B.take(2)
        g_krT = B.take(2)
        g_cqT = B.take(2)
        g_q = B.take(2 * T)
        g_kn = B.take(2 * MLA_H)
        g_va = B.take(KT2)
        g_qT2 = B.take(MLA_H)
        KEY_SEGS = ((0, S), (S, NTOK))

        def mla_up_pe():
            pe.wait_ge(sem("ckv_n"), KT2)
            pe.wait_ge(sem("kr"), 1)
            for groups, c0, n in ((g_ckvT, 0, KV_LORA), (g_krT, KV_LORA, ROPE)):
                for i, g in enumerate(groups):
                    B.acquire(pe, g)
                    for t in range(T * i, min(T * i + T, KT2)):
                        ins = pe.transpose(B.at(g)[0:n, (t % T) * P:(t % T + 1) * P], ckv[:, t, c0:c0 + n], ident)
                    B.filled(ins, g)
            pe.wait_ge(sem("cq_n"), T)
            for c, g in enumerate(g_cqT):
                B.acquire(pe, g)
                for t in range(T):
                    ins = pe.transpose(B.at(g)[:, t * P:(t + 1) * P], cq[:, t, c * P:(c + 1) * P], ident)
                B.filled(ins, g)
            pe.wait_ge(sem("uq_in"), 16)
            pe.wait_ge(sem("ukv_in"), 16)
            for g in (*g_ckvT, *g_cqT):
                B.drained(pe, g)
            for i, g in enumerate(g_q):
                t, n = i // 2, i % 2
                B.acquire(pe, g)
                B.filled(product(g, B.at(g)[:, 0:384], [(cqT[:, c, t * P:(t + 1) * P], uq[:, c, n * 384:(n + 1) * 384])
                                                       for c in range(2)]), g)
            for i, g in enumerate(g_kn):
                h, (lo, hi) = i // 2, KEY_SEGS[i % 2]
                B.acquire(pe, g)
                B.filled(product(g, B.at(g)[0:NOPE, 0:hi - lo], [(ukv[:, h, 0:NOPE], ckvT[:, lo:hi])]), g)
            for t, g in enumerate(g_va):
                B.acquire(pe, g)
                B.filled(product(g, B.at(g).rearrange("p (h d) -> p h d", h=MLA_H),
                                 [(ckvT[:, t * P:(t + 1) * P], ukv[:, :, NOPE:])]), g)
            pe.wait_ge(sem("q_rot"), T)
            for h, g in enumerate(g_qT2):
                B.acquire(pe, g)
                for t in range(T):
                    ins = pe.transpose(B.at(g)[0:QK_MLA, t * P:(t + 1) * P], q_tok[:, t, h, :], ident)
                B.filled(ins, g)

        def mla_up_act():
            act.wait_ge(sem("columns_in"), 16 * N_COLUMNS)
            for g, (lo, hi) in zip(g_ckvT, KEY_SEGS):
                B.full(act, g)
                B.release(copy(act, ckvT[:, lo:hi], B.at(g)[:, 0:hi - lo], g_ckv_col), g)
            for c, g in enumerate(g_cqT):
                B.full(act, g)
                B.release(copy(act, cqT[:, c, :], B.at(g), g_cq_col[:, c:c + 1]), g)
            for i, g in enumerate(g_q):
                t, n = i // 2, i % 2
                B.full(act, g)
                B.release(copy(act, q_tok[:, t, 4 * n:4 * n + 4, :], B.at(g)[:, 0:384].rearrange("p (h c) -> p h c", h=4),
                               QK_MLA ** -0.5), g)
            for i, g in enumerate(g_kn):
                h, (lo, hi) = i // 2, KEY_SEGS[i % 2]
                B.full(act, g)
                B.release(copy(act, kT_mla[0:NOPE, h, lo:hi], B.at(g)[0:NOPE, 0:hi - lo]), g)
            for h, g in enumerate(g_qT2):
                if h % 2 == 0:
                    B.full(act, g)
                    B.release(copy(act, qT_mla[:, h, :], B.at(g)[0:QK_MLA, :]), g)

        def mla_up_dve():
            for g, (lo, hi) in zip(g_krT, KEY_SEGS):
                B.full(dve, g)
                B.release(dve.tensor_copy(kT_mla[NOPE:QK_MLA, :, lo:hi],
                                          B.at(g)[0:ROPE, 0:hi - lo].unsqueeze(1).to_broadcast([ROPE, MLA_H, hi - lo])), g)
            for t in range(T):
                for g in g_q[2 * t:2 * t + 2]:
                    B.drained(dve, g)
                v = q_tok[:, t, :, NOPE:].rearrange("p h (a x f) -> p h a x f", a=2, x=2)
                c, s = (r[:, t].unsqueeze(1).to_broadcast([P, MLA_H, 2, 8]) for r in (cos2, sin2))
                rotate_halves(v, c, s).then_inc(sem("q_rot"), 1)
                dve.wait_ge(sem("q_rot"), t + 1)
            for t, g in enumerate(g_va):
                B.full(dve, g)
                B.release(dve.tensor_copy(va[:, t, :], B.at(g)), g)
            for h, g in enumerate(g_qT2):
                if h % 2 == 1:
                    B.full(dve, g)
                    B.release(dve.tensor_copy(qT_mla[:, h, :], B.at(g)[0:QK_MLA, :]), g)

        def mla_ready_pe():
            for g in (*g_krT, *g_kn, *g_va, *g_qT2, *g_za):
                B.drained(pe, g)

        SEG2 = [S, CTX]
        seg2 = lambda si: slice(*KEY_SEGS[si])
        pairs2 = [(2 * i, 2 * i + 1) for i in range(4)]
        mla_pe, mla_act, mla_dve, g_mla_end = attention(
            "mla", pairs2, SEG2, lambda h, qt: qT_mla[:, h, qt * P:(qt + 1) * P], lambda h, si: kT_mla[:, h, seg2(si)],
            lambda h, kt: va[:, kt, h * HD:(h + 1) * HD], HD, p2b, pt2,
            lambda i, o: dve.tensor_tensor(oaT[:, i, :], o, oaT[:, i, :], ALU.mult), [])

        g_gate2 = B.take(2)
        last_of_block.update({7: g_gate2[0], 8: g_gate2[1]})

        def gate2_pe():
            pe.wait_ge(sem("sc_rep"), KD)
            for j, g in enumerate(g_gate2):
                w = block_in(BLOCK["gate"] + j)
                B.acquire(pe, g)
                B.filled(product(g, B.at(g), [(sc_rep[:, k, :], w[:, k, :]) for k in range(KD)]), g)

        def sc_rep_dve():
            dve.wait_ge(sem("silu_c"), 1)
            for k in range(KD):
                dve.tensor_scalar(sc_rep[:, k, :], ones, c_col[:, k, 0:1], None, ALU.mult).then_inc(sem("sc_rep"), 1)

        def gate2_dve():
            dve.wait_ge(sem("gate_row_in"), 16)
            for j, g in enumerate(g_gate2):
                o = gate_row[:, j * BANK:(j + 1) * BANK]
                B.full(dve, g)
                B.release(dve.tensor_tensor(o, B.at(g), o, ALU.add), g)

        g_kb = B.take(4 + 4)
        g_vb = B.take(KT2)
        g_qb = B.take(4)
        g_zb = B.take(4)
        last_of_block.update({9: g_kb[-1], 10: g_vb[-1], 11: g_qb[-1], 12: g_zb[-1]})

        def na_in_pe():
            w = block_in(BLOCK["kb"])
            for i, g in enumerate(g_kb):
                c, src, n = i % 4, (h2T, hcT)[i // 4], (S, CTX)[i // 4]
                B.acquire(pe, g)
                B.filled(product(g, B.at(g)[:, 0:n], [(w[:, k, c * P:(c + 1) * P], src[:, k, :]) for k in range(KD)]), g)
            w = block_in(BLOCK["vb"])
            for t, g in enumerate(g_vb):
                B.acquire(pe, g)
                B.filled(product(g, B.at(g), [(tokens(t, k), w[:, k, :]) for k in range(KD)]), g)
            for name, groups in (("qb", g_qb), ("zb", g_zb)):
                w = block_in(BLOCK[name])
                for c, g in enumerate(groups):
                    B.acquire(pe, g)
                    B.filled(product(g, B.at(g), [(w[:, k, c * P:(c + 1) * P], h2T[:, k, :]) for k in range(KD)]), g)

        def na_in_drain(eng):
            for i, g in enumerate(g_kb):
                lo, hi = KEY_SEGS[i // 4]
                drain(eng, g, kbT[:, i % 4, lo:hi], B.at(g)[:, 0:hi - lo])
            for t, g in enumerate(g_vb):
                drain(eng, g, vb[:, t, :], B.at(g))
            for c, g in enumerate(g_qb):
                drain(eng, g, qbT[:, c, :], B.at(g), HD ** -0.5)
            if eng is act:
                for c, g in enumerate(g_zb):
                    B.full(act, g)
                    B.release(act.activation(obT[:, c, :], B.at(g), ACT.Silu), g)

        def na_ready_pe():
            for g in (*g_kb, *g_vb, *g_qb, *g_zb):
                B.drained(pe, g)

        odd = lambda h: slice((h % 2) * HD, (h % 2 + 1) * HD)

        def na_bias(h, qt):
            o = 6 - 2 * qt
            return na_table[:, h, o * GRID_W:(o + GRID_H) * GRID_W]

        na_pe, na_act, na_dve, g_na_end = attention(
            "na", pairs2, SEG2, lambda h, qt: qbT[odd(h), h // 2, qt * P:(qt + 1) * P],
            lambda h, si: kbT[odd(h), h // 2, seg2(si)], lambda h, kt: vb[:, kt, h * HD:(h + 1) * HD], HD, p2b, pt2,
            lambda i, o: dve.tensor_tensor(obT[:, i, :], o, obT[:, i, :], ALU.mult), [], bias=na_bias)

        g_y = [B.take(4) for _ in range(KD)]
        last_of_block.update({13: g_y[3][0], 14: g_y[3][1], 15: g_y[7][0], 16: g_y[7][1]})
        g_out3 = B.take(2 * T)

        def y_pe():
            B.drained(pe, g_na_end)
            B.drained(pe, g_mla_end)
            for j in range(KD):
                b = BLOCK["g"] + 2 * (j // 4)
                gs = g_y[j]
                for i in range(2):
                    w = block_in(b + i)
                    B.acquire(pe, gs[i])
                    B.filled(product(gs[i], B.at(gs[i]), [(w[:, k, (j % 4) * P:(j % 4 + 1) * P], h2T[:, k, :])
                                                         for k in range(KD)]), gs[i])
                if j == 0:
                    pe.wait_ge(sem("woa_in"), 16)
                    pe.wait_ge(sem("wob_in"), 16)
                for i, (w, o) in enumerate(((woa, oaT), (wob, obT))):
                    g = gs[2 + i]
                    B.acquire(pe, g)
                    B.filled(product(g, B.at(g), [(w[:, k, j * P:(j + 1) * P], o[:, k, :]) for k in range(4)]), g)
            pe.wait_ge(sem("w_out2_in"), 32)
            pe.wait_ge(sem("yT"), KD)
            add_product_pe(g_out3, lambda k: yT[:, k, :], lambda k: w_out2[k // 4][:, k % 4, :], KD)

        def y_act():
            for j in range(KD):
                for i in range(2):
                    if j >= 2:
                        act.wait_ge(sem("yT"), j - 1)
                    B.full(act, g_y[j][i])
                    B.release(act.activation(sg[2 * (j % 2) + i], B.at(g_y[j][i]), ACT.Sigmoid), g_y[j][i])

        def y_dve():
            for j in range(KD):
                for i in range(2):
                    B.drained(dve, g_y[j][i])
                    g = g_y[j][2 + i]
                    B.full(dve, g)
                    B.release(dve.tensor_tensor(sg[2 * (j % 2) + i], B.at(g), sg[2 * (j % 2) + i], ALU.mult), g)
                    B.drained(dve, g)
                dve.tensor_tensor(yT[:, j, :], sg[2 * (j % 2)], sg[2 * (j % 2) + 1], ALU.add).then_inc(sem("yT"), 1)
            for i, g in enumerate(g_out3):
                t, n = i // 2, i % 2
                c = slice(n * BANK, (n + 1) * BANK)
                B.full(dve, g)
                if i >= 2:
                    dve.wait_ge(sem("x_last"), i - 1)
                B.release(dve.tensor_tensor(ysum[i % 2], B.at(g), gate_row[:, c], ALU.mult), g)
                B.drained(dve, g)
                dve.tensor_tensor(x_sb[:, t, c], ysum[i % 2], x_sb[:, t, c], ALU.add).then_inc(sem("x_last"), 1)

        hn_last = sem("hn_last")
        norm6_act_, norm6_dve_ = rms_rows(x_sb, hn, T, D, hn_last)

        def last_act():
            act.wait_ge(sem("x_last"), 2 * T)
            norm6_act_()

        def last_dve():
            norm6_dve_()
            dve.wait_ge(sem("g_fin_in"), 16)
            for t in range(T):
                dve.wait_ge(hn_last, t + 1)
                dve.tensor_tensor(x_sb[:, t, :], hn[:, t, :], g_fin, ALU.mult).then_inc(sem("result"), 1)

        def row_of(v, n):
            return v.unsqueeze(0).to_broadcast([P, n]) if len(v.shape) == 1 else v.to_broadcast([P, n])

        def first_loads():
            sp.dma_start(const[:], a["shape_const"]).then_inc(sem("const_in"), 16)
            sp.dma_start(mem, a["mem"][0].rearrange("(t p) d -> p t d", p=P)).then_inc(sem("mem_in"), 16)
            sp.dma_start(x_sb, a["x"][0].rearrange("(t p) d -> p t d", p=P)).then_inc(sem("x_in"), 16)
            sp.dma_start(ca_wkv, a["ca_wkv"][0].rearrange("(k p) c -> p k c", p=P)).then_inc(sem("ca_wkv_in"), 16)
            w = a["w_in"][0].rearrange("(k p) c -> p k c", p=P)
            sp.dma_start(w_gate, w[:, :, GATE0:GATE1]).then_inc(sem("w_gate_in"), 16)
            for k in range(0, KD, 2):
                sp.dma_start(w_in[:, k:k + 2, 0:GATE0], w[:, k:k + 2, 0:GATE0]).then_inc(sem("w_in_in"), 16)
                sp.dma_start(w_in[:, k:k + 2, GATE0:], w[:, k:k + 2, GATE1:]).then_inc(sem("w_in_in"), 16)
            B.full(sp, g_vca[-1])
            sp.dma_start(pool_w, a["pool_w"][0].rearrange("(c g) i e -> (g i) c e", c=2)).then_inc(sem("pool_w_in"), 16)
            sp.dma_start(ml_g, row_of(a["mlstm_norm_g"], ML_H * HD)).then_inc(sem("rows_in"), 16)
            sp.dma_start(qg, row_of(a["q_norm_g"], HD)).then_inc(sem("rows_in"), 16)
            sp.dma_start(kg, row_of(a["k_norm_g"], HD)).then_inc(sem("rows_in"), 16)
            B.full(sp, g_gate[-1])
            sp.dma_start(inv_n, a["shape_inv"].rearrange("p (c s) -> p c s", c=2)).then_inc(sem("inv_n_in"), 16)
            B.full(sp, g_akv[-1])
            w = a["w_out"][0]
            sp.dma_start(w_out[:, 0:4, :], w[0:512].rearrange("(k p) c -> p k c", p=P)).then_inc(sem("w_out_in"), 16)
            for h in range(2):
                sp.dma_start(w_out[h * HD:(h + 1) * HD, 4:8, :],
                             w[512 + h * 256:768 + h * 256].rearrange("(k p) c -> p k c", p=HD)).then_inc(sem("w_out_in"), 16)
            sp.dma_start(ca_wq, a["ca_wq"][0].rearrange("(k p) c -> p k c", p=P)).then_inc(sem("ca_wq_in"), 16)
            sp.dma_start(ca_wo, a["ca_wo"][0].rearrange("(k p) c -> p k c", p=P)).then_inc(sem("ca_wo_in"), 16)

        ctx.enter_context(nc.allow_non_contiguous_dma(reason="a few KB of gains and biases, one column per chunk"))

        def column_loads():
            cols = lambda v: v.rearrange("o (k p) -> p (o k)", p=P)
            for name in gain:
                act.dma_start(gain[name], cols(a[name])).then_inc(sem("columns_in"), 16)
            act.dma_start(c_col[:, :, 0], cols(a["c_2"])).then_inc(sem("columns_in"), 16)
            act.dma_start(c_col[:, :, 1], a["c_ctx_2"].rearrange("(k p) -> p k", p=P)).then_inc(sem("columns_in"), 16)
            act.dma_start(b_mod_col, cols(a["b_mod_2"][:, 0:2 * D])).then_inc(sem("columns_in"), 16)
            act.dma_start(pool_scale, cols(a["pool_scale"])).then_inc(sem("columns_in"), 16)
            for c in range(4):
                act.dma_start(conv_w[:, c, :], a["mlstm_conv_w"][0, :, c * P:(c + 1) * P].rearrange("w p -> p w")).then_inc(sem("columns_in"), 16)
            act.dma_start(gate_i, a["mlstm_gate_b"][:, 0:8].rearrange("o p -> p o")).then_inc(sem("columns_in"), 16)
            act.dma_start(gate_f, a["mlstm_gate_b"][:, 8:16].rearrange("o p -> p o")).then_inc(sem("columns_in"), 16)
            act.dma_start(g_cq_col, cols(a["g_cq_2"])).then_inc(sem("columns_in"), 16)
            act.dma_start(g_ckv_col, cols(a["g_ckv_2"])).then_inc(sem("columns_in"), 16)
            act.dma_start(router_w, a["router_w"][0].rearrange("(k p) e -> p k e", p=P)).then_inc(sem("columns_in"), 16)
            act.wait_ge(sem("fill"), 1)
            flat = na_dram.rearrange("a w c -> (a w c)").rearrange("(p r f) -> p r f", p=P, f=240)
            act.dma_start(flat, fill[:].unsqueeze(1).to_broadcast([P, 16, 240])).then_inc(sem("na_filled"), 16)
            act.wait_ge(sem("na_filled"), 16)
            rpb = a["rpb_2"][0].rearrange("h r c -> (h r) c")
            mid = GRID_W - NA_KC + NA_KC // 2
            n_hr = NA_H * (2 * NA_KR - 1)
            cell, row = GRID_W, 2 * NA_KC - 1
            act.dma_start(bass.AP(na_dram.tensor, 8 * cell, [[cell * cell, n_hr], [cell + 1, mid - 7], [1, NA_KC]]),
                          bass.AP(rpb.tensor, 7, [[row, n_hr], [0, mid - 7], [1, NA_KC]])).then_inc(sem("na_cells"), 16)
            for w in (*range(8), *range(mid + 1, GRID_W)):
                start = min(max(w - NA_KC // 2, 0), GRID_W - NA_KC)
                act.dma_start(na_dram[:, w, start:start + NA_KC],
                              rpb[:, start - w + NA_KC - 1:start - w + 2 * NA_KC - 1]).then_inc(sem("na_cells"), 16)

        N_CELLS = 1 + 8 + 7

        def second_loads():
            for s in (0, 1):
                sp.wait_ge(slot_free[s], 3 * PAIRS)
                load_blocks(s, s + 1)
            sp.wait_ge(added, 2 * T * PAIRS + 1)
            sp.dma_start(ctx_t, a["ctx_2"][0].rearrange("(t p) d -> p t d", p=P)).then_inc(sem("ctx_in"), 16)
            sp.dma_start(g_row, row_of(a["final_norm_g"], D)).then_inc(sem("g_row_in"), 16)
            sp.dma_start(uq, a["w_uq_2"][0].rearrange("(k p) c -> p k c", p=P)).then_inc(sem("uq_in"), 16)
            sp.dma_start(ukv, a["w_ukv_2"][0].rearrange("p (h c) -> p h c", h=MLA_H)).then_inc(sem("ukv_in"), 16)
            load_blocks(2, 9)
            B.full(sp, g_mla_end)
            sp.dma_start(gate_row, row_of(a["b_mod_2"][:, 2 * D:], D)).then_inc(sem("gate_row_in"), 16)
            load_blocks(9, 11)
            sp.wait_ge(sem("na_cells"), 16 * N_CELLS)
            v = na_dram.rearrange("(h r) w c -> w h r c", h=NA_H)
            for i in range(2):
                for h in range(NA_H):
                    sp.dma_start(na_table[i * 64:(i + 1) * 64, h, :].rearrange("p (r c) -> p r c", r=14),
                                 v[:, h, 1 - i:15 - i, :]).then_inc(sem("na_table_in"), 16)
            load_blocks(11, 15)
            B.full(sp, g_na_end)
            sp.dma_start(woa, a["w_oa_2"][0].rearrange("(k p) c -> p k c", p=P)).then_inc(sem("woa_in"), 16)
            sp.dma_start(wob, a["w_ob_2"][0].rearrange("(k p) c -> p k c", p=P)).then_inc(sem("wob_in"), 16)
            w = a["w_out_2"][0]
            for i in range(2):
                sp.dma_start(w_out2[i], w[i * 512:(i + 1) * 512].rearrange("(k p) c -> p k c", p=P)).then_inc(sem("w_out2_in"), 16)
            sp.dma_start(g_fin, row_of(a["final_g_2"], D)).then_inc(sem("g_fin_in"), 16)
            load_blocks(15, 17)

        block = ctx.enter_context(nc.Block())

        @block.sync
        def _(_):
            first_loads()
            experts_sp()
            second_loads()
            for t in range(T):
                sp.wait_ge(sem("result"), t + 1)
                sp.dma_start(out[0, t * P:(t + 1) * P, :], x_sb[:, t, :]).then_inc(sem("stored"), 16)
            sp.wait_ge(sem("stored"), 16 * T)

        @block.gpsimd
        def _(_):
            pool.memset(fill[:], NEG).then_inc(sem("fill"), 1)
            B.full(pool, g_vca[-1])
            pool.memset(upad, 0.0).then_inc(sem("pads"), 1)
            pool.memset(qkpad, 0.0).then_inc(sem("pads"), 1)
            pool.memset(v_aug[:, :, :, HD:], 1.0).then_inc(sem("pads"), 1)

        @block.tensor
        def _(_):
            memory_pe()
            pe.wait_ge(hn_mix, T)
            transpose_rows(g_h1, hn, T)
            project_pe()
            gates_pe()
            pool_pe()
            mlstm_pe()
            mlstm_out_pe()
            heads_pe()
            heads_ready_pe()
            attn_pe()
            out1_pe()
            pe.wait_ge(hn_mem, T)
            transpose_rows(g_h2, hn, T)
            qca_pe()
            ca_all_pe()
            pe.wait_ge(hn_ffn, T)
            transpose_rows(g_h3, hn, T)
            route_pe()
            experts_pe()
            mod_pe()
            turn2_pe()
            mla_in_pe()
            mla_up_pe()
            mla_ready_pe()
            mla_pe()
            gate2_pe()
            na_in_pe()
            na_ready_pe()
            na_pe()
            y_pe()

        @block.scalar
        def _(_):
            column_loads()
            act.wait_ge(sem("x_in"), 16)
            norm1_act()
            memory_drain(act)
            silu_c_act()
            drain_rows(act, g_h1, T, hT, gain["norm_mix_g"])
            project_act()
            conv_act()
            gates_act()
            pool_act()
            mlstm_act()
            mlstm_norm_act()
            mlstm_out_drain(act)
            heads_act()
            heads_drain(act)
            attn_act()
            norm2_act()
            drain_rows(act, g_h2, T, hT, gain["norm_mem_g"])
            qca_drain(act)
            ca_act()
            norm3_act()
            drain_rows(act, g_h3, T, hT, gain["norm_ffn_g"])
            route_act()
            experts_act()
            norms_act()
            turn2_drain(act)
            mla_in_act()
            mla_up_act()
            mla_act()
            na_in_drain(act)
            na_act()
            y_act()
            last_act()

        @block.vector
        def _(_):
            norm1_dve()
            memory_drain(dve)
            dve.wait_ge(sem("columns_in"), 16 * N_COLUMNS)
            drain_rows(dve, g_h1, T, hT, gain["norm_mix_g"])
            conv_dve()
            gates_dve()
            pool_dve()
            mlstm_dve()
            mlstm_out_drain(dve)
            heads_dve()
            heads_drain(dve)
            attn_dve()
            add_product_dve(g_out1)
            norm2_dve()
            drain_rows(dve, g_h2, T, hT, gain["norm_mem_g"])
            qca_drain(dve)
            ca_dve()
            add_product_dve(g_out2)
            norm3_dve()
            drain_rows(dve, g_h3, T, hT, gain["norm_ffn_g"])
            route_dve()
            experts_dve()
            norms_dve()
            mod_dve()
            turn2_drain(dve)
            sc_rep_dve()
            mla_in_dve()
            mla_up_dve()
            mla_dve()
            gate2_dve()
            na_in_drain(dve)
            dve.wait_ge(sem("na_table_in"), 16 * 2 * NA_H)
            na_dve()
            y_dve()
            last_dve()


_INPUTS = ["x", "mem", "norm_mix_g", "w_in", "pool_w", "pool_scale", "mlstm_conv_w", "mlstm_gate_b", "mlstm_norm_g",
           "q_norm_g", "k_norm_g", "w_out", "norm_mem_g", "ca_wq", "ca_wkv", "ca_wo", "norm_ffn_g", "router_w",
           "expert_w_gu", "expert_w_down", "final_norm_g", "c_2", "ctx_2", "c_ctx_2", "w_mod_2", "b_mod_2", "norm_g_2",
           "w_in_2", "g_cq_2", "w_uq_2", "g_ckv_2", "w_ukv_2", "rpb_2", "w_oa_2", "w_ob_2", "w_out_2", "final_g_2"]


def kernel(**inputs):
    import concourse.bacc as bacc
    from concourse.bass_utils import run_bass_kernel_spmd

    nc = bacc.Bacc("TRN2", target_bir_lowering=False, num_devices=1)
    arrays = {f"in_{n}": np.ascontiguousarray(inputs[n]) for n in _INPUTS}
    arrays["in_shape_const"], arrays["in_shape_inv"] = shape_constants()
    aps = {n[3:]: nc.dram_tensor(n, v.shape, F32, kind="ExternalInput").ap() for n, v in arrays.items()}
    out = nc.dram_tensor("out", (1, S, D), F32, kind="ExternalOutput").ap()
    build(nc, aps, out)
    return run_bass_kernel_spmd(nc, [arrays], core_ids=[0]).results[0]["out"]
```

```python
import math
from contextlib import ExitStack

import numpy as np

import concourse.bass as bass
from concourse import mybir

F32 = mybir.dt.float32
F32R = mybir.dt.float32r
ACT = mybir.ActivationFunctionType
ALU = mybir.AluOpType
AX = mybir.AxisListType.X

P = 128
D = 1024
KD = D // P
S = 512
T = S // P
N_MEM = 256
HD = 64
GRID_W = 64
GRID_H = S // GRID_W
POOL_WINDOWS = (2, 4, 8, 16)
POOL_G = 64
PADL = 8
UP = S + 2 * PADL
ML_H = 4
ML_CONV = 5
QKP = S + ML_CONV - 1
AT_H = 8
CA_H, CA_HD = 4, 128
N_EXP = 16
CAP = 2 * S // N_EXP
FF = 2 * D
EPS = 1e-6
CTX = 256
NTOK = S + CTX
KT2 = NTOK // P
MLA_H, NOPE, ROPE = 8, 64, 32
QK_MLA = NOPE + ROPE
Q_LORA, KV_LORA = 256, 128
NA_H, NA_KR, NA_KC = 8, 8, 16
ROPE_THETA = 10000.0
BANK = 512
NBANK = 8
SLOT = 4096
NSLOT = 8
NEG = -1e30
SMALL = 700

GATE0, GATE1 = 1280, 1296
IN_COLS = 2064
MAIN = IN_COLS - 16
C2 = {"ckv": 0, "kb": 160, "vb": 672, "cq": 1184, "za": 1440, "qb": 1952, "zb": 2464, "ga": 2976, "gb": 4000}

C_ID, C_MF, C_MB, C_COS, C_SIN, C_IOTA, C_COS2, C_SIN2, C_ONE, C_END = np.cumsum(
    [0, 128, 128, 128, 128, 128, 64, 64, 64, 128]).tolist()


def shape_constants():
    c = np.zeros((P, C_END), np.float32)
    i = np.arange(P)
    c[:, C_ID:C_ID + P] = np.eye(P)
    c[:, C_MF:C_MF + P] = np.where(i[:, None] <= i[None, :], 0, NEG)
    c[:, C_MB:C_MB + P] = np.where(i[:, None] >= i[None, :], 0, NEG)
    tok = np.arange(S)
    row, col = (tok // GRID_W).astype(np.float32), (tok % GRID_W).astype(np.float32)

    def angles(n):
        f = (np.float32(ROPE_THETA) ** (-np.arange(n, dtype=np.float32) / np.float32(n))).astype(np.float32)
        return np.concatenate([row[:, None] * f, col[:, None] * f], axis=-1).astype(np.float32)

    def by_tile(a):
        return a.reshape(T, P, -1).transpose(1, 0, 2).reshape(P, -1)

    a = angles(HD // 4)
    c[:, C_COS:C_COS + 128], c[:, C_SIN:C_SIN + 128] = by_tile(np.cos(a)), by_tile(np.sin(a))
    a = angles(ROPE // 4)
    c[:, C_COS2:C_COS2 + 64], c[:, C_SIN2:C_SIN2 + 64] = by_tile(np.cos(a)), by_tile(np.sin(a))
    c[:, C_IOTA:C_IOTA + CAP] = np.arange(CAP)
    c[:, C_ONE:C_ONE + P] = 1.0
    inv = np.zeros((P, 2, S), np.float32)
    for g, w in enumerate(POOL_WINDOWS):
        n = np.clip(tok + w // 2, 0, S) - np.clip(tok - w // 2, 0, S)
        inv[(g % 2) * 64:(g % 2) * 64 + 64, g // 2] = (1.0 / n).astype(np.float32)
    return c, inv.reshape(P, 2 * S)


class Banks:

    def __init__(self, nc, ctx, psum):
        self.psum = psum
        self.full_sem = [ctx.enter_context(nc.semaphore(f"bank_full{b}")) for b in range(NBANK)]
        self.free_sem = [ctx.enter_context(nc.semaphore(f"bank_free{b}")) for b in range(NBANK)]
        self.next = 0

    def take(self, n):
        g = self.next
        self.next += n
        return range(g, g + n)

    def at(self, g):
        return self.psum[:, g % NBANK, :]

    def acquire(self, pe, g):
        if g >= NBANK:
            pe.wait_ge(self.free_sem[g % NBANK], g // NBANK)

    def filled(self, ins, g):
        ins.then_inc(self.full_sem[g % NBANK], 1)

    def full(self, eng, g):
        eng.wait_ge(self.full_sem[g % NBANK], g // NBANK + 1)

    def release(self, ins, g):
        ins.then_inc(self.free_sem[g % NBANK], 1)

    def drained(self, eng, g):
        eng.wait_ge(self.free_sem[g % NBANK], g // NBANK + 1)


def build(nc, a, out):
    ctx = ExitStack()
    pe, act, dve, pool, sp = nc.tensor, nc.scalar, nc.vector, nc.gpsimd, nc.sync
    with ctx:
        sems = {}

        def sem(name):
            if name not in sems:
                sems[name] = ctx.enter_context(nc.semaphore(name))
            return sems[name]

        def sb(name, cols, parts=P):
            return ctx.enter_context(nc.sbuf_tensor(name, [parts, cols], F32))

        psum = ctx.enter_context(nc.psum_tensor("psum", [P, NBANK, BANK], F32))
        B = Banks(nc, ctx, psum)

        ring_at = -(-nc.sbuf_base // 32) * 32
        ring = sb("ring", NSLOT * SLOT)

        def rounded(name, o, *dims):
            return nc.alloc_sbuf_tensor_at(name, [P, *dims], F32R, offset=ring_at + 4 * o)

        x_flat = sb("x_res", T * D)
        hn_flat = sb("hn", T * D)
        W = sb("work_area", 10272)
        const = sb("const_sb", C_END)
        fill = sb("fill", 240)
        small = sb("small", SMALL)
        x_sb = x_flat[:].rearrange("p (t d) -> p t d", t=T)
        hn = hn_flat[:].rearrange("p (t d) -> p t d", t=T)
        taken = [0]

        def sm(n, parts=P):
            o = taken[0]
            taken[0] += n
            assert taken[0] <= SMALL
            return small[0:parts, o:o + n]

        def cut(base, o, *dims, parts=P):
            n = int(np.prod(dims))
            v = base[0:parts, o:o + n]
            if len(dims) == 2:
                v = v.rearrange("p (a b) -> p a b", a=dims[0])
            if len(dims) == 3:
                v = v.rearrange("p (a b c) -> p a b c", a=dims[0], b=dims[1])
            return v

        def slot(s):
            return ring[:, s * SLOT:(s + 1) * SLOT]

        ident = const[:, C_ID:C_ID + P]
        ones = const[:, C_ONE:C_ONE + P]
        ROWS, n_rows = {}, 0
        for name, n in (("norm_mix_g", KD), ("norm_mem_g", KD), ("norm_ffn_g", KD), ("norm_g_2", KD), ("c_2", KD),
                        ("c_ctx_2", KD), ("b_mod_2", 2 * KD), ("pool_scale", 2), ("g_cq_2", 2), ("g_ckv_2", 1),
                        ("mlstm_conv_w", 4 * ML_CONV)):
            ROWS[name] = (n_rows, n_rows + n)
            n_rows += n
        columns = sm(n_rows)
        column = {name: columns[:, lo:hi] for name, (lo, hi) in ROWS.items()}
        gain = {n: column[n] for n in ("norm_mix_g", "norm_mem_g", "norm_ffn_g", "norm_g_2")}
        b_mod_col, pool_scale = column["b_mod_2"], column["pool_scale"]
        conv_w = column["mlstm_conv_w"].rearrange("p (w c) -> p c w", w=ML_CONV)
        gate_bias = sm(2, 2 * ML_H)
        g_cq_col, g_ckv_col = column["g_cq_2"], column["g_ckv_2"]
        stat = sm(64)
        mod = sm(2 * KD * 2).rearrange("p (j v) -> p j v", v=2)
        router_w = sm(KD * N_EXP).rearrange("p (k e) -> p k e", k=KD)
        aff = sm(T * N_EXP).rearrange("p (t e) -> p t e", t=T)
        slot_of = sm(T * N_EXP).rearrange("p (t e) -> p t e", t=T)
        gcols = sm(P).rearrange("p (k t r) -> p k t r", k=4, t=T)
        posc = sm(T * 2).rearrange("p (t e) -> p t e", t=T)
        gatec = sm(T * 2).rearrange("p (t e) -> p t e", t=T)
        ml_stat = sm(3 * T).rearrange("p (i t) -> p i t", i=3)

        slot_free = [sem(f"slot_free{s}") for s in range(NSLOT)]
        slot_loaded = [sem(f"slot_loaded{s}") for s in range(NSLOT)]
        dve_step = sem("dve_step")
        n_dve = [0]

        def link(ins):
            n_dve[0] += 1
            ins.then_inc(dve_step, 1)
            dve.wait_ge(dve_step, n_dve[0])

        w_in = [cut(slot(i), 0, KD, BANK) for i in range(4)]
        W_IN_COLS = (((0, 512),), ((512, 768), (1808, 2064)), ((768, 1280),), ((1296, 1808),))
        w_gate = cut(W, 9232, KD, 16)
        ca_wkv = ring[:, 4 * SLOT:6 * SLOT].rearrange("p (k c) -> p k c", k=KD)
        mem = cut(slot(6), 0, 2, D)
        memT = cut(slot(6), 2048, KD, N_MEM)
        kT_ca = cut(W, 0, CA_H, N_MEM)
        v_ca = cut(W, 1024, 2, CA_H * CA_HD)
        hT = cut(slot(7), 0, KD, S)
        four = 4 * SLOT
        qkpad = cut(ring, four, 4, QKP)
        sig_o = cut(ring, four + 2064, T, ML_H * HD)
        aq = cut(ring, four + 3088, T, AT_H, HD)
        ak = cut(ring, four + 5136, T, 2, HD)
        av = cut(ring, four + 5648, T, 2 * HD)
        qT_at = cut(ring, four, 4, S)
        kT_at = ring[:, four + 6160:four + 6672]
        pool_w = cut(ring, four + 6672, 2, POOL_G)
        ml_g = ring[:, four + 6800:four + 7056]
        qg = ring[:, four + 7056:four + 7120]
        kg = ring[:, four + 7120:four + 7184]
        c_pad = cut(ring, four + 7184, KD, 32)
        mod_rows = ring[:, four + 7440:four + 7952]
        rows = W[0:n_rows, 2048:2048 + P]
        gate_b_rows = W[0:2, 2176:2176 + 2 * ML_H]
        upad = cut(slot(6), 0, 2, UP)
        p1 = cut(slot(6), 1056, 2, UP)
        p2 = cut(slot(6), 2112, 2, UP)
        p3 = slot(6)[:, 3168:3168 + UP]
        inv_n = cut(W, 9232, 2, S)
        d_pool = cut(hn_flat, 2048, 2, S)
        ymixT = cut(hn_flat, 0, KD, S)
        grow = [W[0:2 * ML_H, 2048 + i * S:2048 + (i + 1) * S] for i in range(8)]
        qkT = cut(W, 6144, 4, S)
        v_aug = cut(W, 8192, T, ML_H, HD + 1)
        hsum = cut(slot(6), 0, T, ML_H, HD)
        htmp = cut(slot(6), 1024, T, ML_H, HD)
        Pt = [[cut(slot(7), 0, T, S), cut(slot(7), 2048, T, S)], [cut(hn_flat, 2048, T, S), cut(slot(6), 2048, T, S)]]
        gate_row = W[:, 9232:9232 + D]
        gate_lin = [grow[2][0:1], grow[4][0:1]]
        w_mod = [cut(slot(i), 0, 2, 2 * D) for i in (0, 3, 1, 2)]
        w_modg = [cut(slot(i), 0, 4, D) for i in (2, 3)]
        sq_q = cut(ring, four, T, AT_H, HD)
        w_out = ring[:, 0:2 * SLOT].rearrange("p (k c) -> p k c", k=KD)
        ca_wq = cut(slot(2), 0, KD, CA_H * CA_HD)
        ca_wo = cut(slot(3), 0, CA_H, D)
        rope_t = [cut(W, 9232 + i * 256, AT_H, HD // 2) for i in range(2)]
        p_at = [slot(6)[:, 2048 + i * S:2048 + (i + 1) * S] for i in range(4)]
        pt_at = [cut(slot(7), i * 2048, T, S) for i in range(2)]
        hn_ca = cut(ring, four, T, D)
        qT_ca = cut(W, 2048, CA_H, S)
        oT_ca = cut(W, 4096, CA_H, S)
        p_ca = [W[:, 6144 + i * N_MEM:6144 + (i + 1) * N_MEM] for i in range(4)]
        pt_ca = [cut(W, 7168, 2, S), cut(W, 8192, 2, S)]
        affT, left, slotT, zero16 = (W[0:N_EXP, 2048 + i * S:2048 + (i + 1) * S] for i in range(4))
        top8 = W[0:N_EXP, 4096:4096 + CAP]
        ctx_n = cut(W, 4160, 2, D)
        hcT = cut(W, 6656, KD, CTX)

        xsT = cut(W, 0, KD, P)
        silu_g = cut(W, 1024, 2, BANK)
        hid = cut(W, 2048, 2, BANK)
        hidT = [cut(W, 3072 + b * 512, 4, 2, CAP) for b in range(2)]
        sel = cut(W, 4096, T, P)
        selg = cut(W, 4608, T, P)
        selgT = W[:, 5120:5632]
        ypair = W[:, 5632:6656]

        blk = [slot(0), slot(1)]
        blk_lo = [rounded(f"block_lo{i}", i * SLOT, SLOT) for i in range(2)]
        w_hi = rounded("w_hi", 2 * SLOT, KD, BANK)
        h2T, h2_lo = cut(slot(3), 0, KD, S), rounded("h2_lo", 3 * SLOT, KD, S)
        h2_hi = rounded("h2_hi", 4 * SLOT, KD, S)
        hc_lo = rounded("hc_lo", 5 * SLOT, KD, CTX)
        hc_hi = rounded("hc_hi", 5 * SLOT + 2048, KD, CTX)
        square_junk, dve_junk = slot(6)[:, 0:D], slot(6)[:, D:2 * D]
        g_row = slot(6)[:, 2048:2048 + D]
        oaT = cut(slot(6), 0, 4, S)
        kT_mla = cut(ring, 6 * SLOT + 2048, MLA_H, NTOK, parts=QK_MLA)
        q_tok = cut(slot(2), 0, T, MLA_H, QK_MLA)
        ckv = cut(hn_flat, 0, KT2, KV_LORA + ROPE)
        qT_mla = cut(hn_flat, 0, MLA_H, S, parts=QK_MLA)
        va = cut(W, 0, KT2, MLA_H * HD)
        ckvT = W[:, 3072:3840]
        uq = cut(W, 4096, 2, MLA_H * QK_MLA)
        ukv = cut(W, 5632, MLA_H, NOPE + HD)
        cq = cut(W, 6656, T, Q_LORA)
        cqT = cut(W, 7680, 2, S)
        rope2_t = [cut(W, 8704 + i * 128, MLA_H, 2, 8) for i in range(2)]
        pt_mla = [cut(W, 3072, KT2, S), cut(slot(2), 0, KT2, S)]
        p_mla = [W[:, 6144 + i * NTOK:6144 + (i + 1) * NTOK] for i in range(3)]
        qbT = cut(hn_flat, 0, 4, S)
        obT = cut(hn_flat, 2048, 4, S)
        kbT = cut(ring, 6 * SLOT + 2048, 4, NTOK)
        vb = cut(ring, 6 * SLOT + 5120, KT2, NA_H * HD)
        na_table = cut(W, 2048, NA_H, 14 * GRID_W)
        pt_na = [cut(slot(5), 0, KT2, S), cut(slot(2), 0, KT2, S)]
        p_na = [W[:, 0:NTOK], W[:, NTOK:2 * NTOK], slot(5)[:, 3072:3072 + NTOK]]
        woa = cut(ring, 6 * SLOT + 2048, 4, D)
        wob = cut(slot(5), 0, 4, D)
        yT = cut(W, 2048, KD, S)
        w_out2_a, w_out2_b = cut(slot(7), 2048, 2, D), W[:, 0:D]
        w_out2 = [w_out2_a[:, 0], w_out2_a[:, 1], w_out2_b, *(cut(slot(0), 0, 4, D)[:, i] for i in range(4)), slot(1)[:, 0:D]]
        sg = [W[:, 6144 + i * S:6144 + (i + 1) * S] for i in range(4)]
        ysum = [W[:, 8192 + i * S:8192 + (i + 1) * S] for i in range(2)]
        g_fin = W[:, D:2 * D]

        na_dram = nc.dram_tensor("na_scratch", [NA_H * (2 * NA_KR - 1), GRID_W, GRID_W], F32, kind="Internal").ap()

        def copy(eng, o, i, scale=None, bias=None):
            if eng is act:
                kw = {}
                if scale is not None:
                    kw["scale"] = scale
                if bias is not None:
                    kw["bias"] = bias
                return act.activation(o, i, ACT.Identity, **kw)
            if scale is None and bias is None:
                return dve.tensor_copy(o, i)
            if scale is None:
                return dve.tensor_scalar(o, i, bias, None, ALU.add)
            if bias is None:
                return dve.tensor_scalar(o, i, scale, None, ALU.mult)
            return dve.tensor_scalar(o, i, scale, bias, ALU.mult, ALU.add)

        norms = [0, 0]

        def rms_rows(src, dst, tiles, width, mark):
            ss, ms, rt, rs = (stat[:, i * 8:i * 8 + tiles] for i in range(4))
            squared, mean_ready, root_ready = sem("rows_squared"), sem("mean_ready"), sem("root_ready")
            norms[0] += 1
            norms[1] += tiles
            turn, rows = norms

            def on_act(junk=None):
                for t in range(tiles):
                    act.activation((junk or dst)[:, t, :], src[:, t, :], ACT.Square,
                                   accum_out=ss[:, t:t + 1]).then_inc(squared, 1)
                act.wait_ge(mean_ready, turn)
                act.activation(rt, ms, ACT.Sqrt).then_inc(root_ready, 1)

            def on_dve():
                dve.wait_ge(squared, rows)
                dve.tensor_scalar(ms, ss, 1.0 / width, EPS, ALU.mult, ALU.add).then_inc(mean_ready, 1)
                dve.wait_ge(root_ready, turn)
                link(dve.reciprocal(rs, rt))
                for t in range(tiles):
                    dve.tensor_scalar(dst[:, t, :], src[:, t, :], rs[:, t:t + 1], None, ALU.mult).then_inc(mark, 1)

            return on_act, on_dve

        def add_norm(groups, src, dst, mark, arrived=None):
            squared, mean_ready, root_ready = sem("rows_squared"), sem("mean_ready"), sem("root_ready")
            turn = list(norms)
            norms[0] += T
            norms[1] += T
            ss, ms, rt, rs = (stat[:, i * 8:i * 8 + T] for i in range(4))

            def on_act():
                if arrived:
                    act.wait_ge(arrived, 16)
                for t in range(T):
                    for g in groups[2 * t:2 * t + 2]:
                        B.drained(act, g)
                    act.activation(dst[:, t, :], src[:, t, :], ACT.Square, accum_out=ss[:, t:t + 1]).then_inc(squared, 1)
                    act.wait_ge(mean_ready, turn[0] + t + 1)
                    act.activation(rt[:, t:t + 1], ms[:, t:t + 1], ACT.Sqrt).then_inc(root_ready, 1)

            def on_dve():
                for t in range(T):
                    for n, g in enumerate(groups[2 * t:2 * t + 2]):
                        o = x_sb[:, t, n * BANK:(n + 1) * BANK]
                        B.full(dve, g)
                        B.release(dve.tensor_tensor(o, B.at(g), o, ALU.add), g)
                    dve.wait_ge(squared, turn[1] + t + 1)
                    dve.tensor_scalar(ms[:, t:t + 1], ss[:, t:t + 1], 1.0 / D, EPS, ALU.mult, ALU.add).then_inc(mean_ready, 1)
                    dve.wait_ge(root_ready, turn[0] + t + 1)
                    link(dve.reciprocal(rs[:, t:t + 1], rt[:, t:t + 1]))
                    dve.tensor_scalar(dst[:, t, :], src[:, t, :], rs[:, t:t + 1], None, ALU.mult).then_inc(mark, 1)

            return on_act, on_dve

        def turn_tiles(groups, src, mark):
            for i, g in enumerate(groups):
                t, half = i // 2, i % 2
                pe.wait_ge(mark, t + 1)
                B.acquire(pe, g)
                for k in range(4):
                    ins = pe.transpose(B.at(g)[:, k * P:(k + 1) * P], src[:, t, (4 * half + k) * P:(4 * half + k + 1) * P], ident)
                B.filled(ins, g)

        def drain_tiles(eng, groups, dst, scale, bias=None):
            for i, g in enumerate(groups):
                t, half = i // 2, i % 2
                if (half == 0) == (eng is act):
                    B.full(eng, g)
                    for k in range(4 * half, 4 * half + 4):
                        ins = copy(eng, dst[:, k, t * P:(t + 1) * P], B.at(g)[:, (k % 4) * P:(k % 4 + 1) * P],
                                   scale[:, k:k + 1], None if bias is None else bias[:, k:k + 1])
                    B.release(ins, g)

        def product(g, o, pairs):
            for i, (l, r) in enumerate(pairs):
                ins = pe.matmul(o, l, r, start=(i == 0), stop=(i == len(pairs) - 1))
            return ins

        def transpose_rows(groups, src, tiles):
            per = BANK // (tiles * P)
            for i, g in enumerate(groups):
                B.acquire(pe, g)
                for k in range(i * per, (i + 1) * per):
                    for t in range(tiles):
                        o = ((k - i * per) * tiles + t) * P
                        ins = pe.transpose(B.at(g)[:, o:o + P], src[:, t, k * P:(k + 1) * P], ident)
                B.filled(ins, g)

        def drain_rows(eng, groups, tiles, dst, scale=None, bias=None):
            per = BANK // (tiles * P)
            for i, g in enumerate(groups):
                if (g % 2 == 0) == (eng is act):
                    B.full(eng, g)
                    for k in range(i * per, (i + 1) * per):
                        o = (k - i * per) * tiles * P
                        ins = copy(eng, dst[:, k, :], B.at(g)[:, o:o + tiles * P],
                                   None if scale is None else scale[:, k:k + 1],
                                   None if bias is None else bias[:, k:k + 1])
                    B.release(ins, g)

        def drain(eng, g, o, i, scale=None, bias=None):
            if (g % 2 == 0) == (eng is act):
                B.full(eng, g)
                B.release(copy(eng, o, i, scale, bias), g)

        def plan_attention(name, heads, segs, nkt):
            units = [(c, qt, j) for c in range(len(heads)) for qt in range(T) for j in range(len(heads[c]))]
            per, lag, order = len(heads[0]) * T, 2, []
            for i in range(len(units) + lag + 1):
                if i < len(units):
                    order.append(("S", i))
                if 0 <= i - lag < len(units):
                    order.append(("T", i - lag))
                if i - lag >= 1 and (i - lag) % per == 0:
                    order.append(("O", (i - lag) // per - 1))
            size = {"S": len(segs), "T": -(-nkt // 4), "O": 1}
            return units, order, {(kind, i): list(B.take(size[kind])) for kind, i in order}

        def attention(name, heads, segs, q_at, k_at, v_at, dv, pbuf, ptbuf, o_out, ready, bias=None):
            nkt, nseg, np_ = sum(segs) // P, len(segs), len(pbuf)
            units, order, gid = plan_attention(name, heads, segs, nkt)
            sets = len(ptbuf) // len(heads[0])
            per = len(heads[0]) * T
            maxed, normed = sem(name + "_max"), sem(name + "_weights")
            exp_biased = sem(name + "_exp") if bias is not None else None
            tmp_max = lambda i: stat[:, 32 + 2 * (i % 4):34 + 2 * (i % 4)]
            neg_max = lambda i: stat[:, 40 + i % 4:41 + i % 4]
            sums = lambda i: stat[:, 44 + 2 * (i % 4):46 + 2 * (i % 4)]
            recip = lambda i: stat[:, 52 + 2 * (i % 4):54 + 2 * (i % 4)]
            turned = lambda c, j: ptbuf[(c % sets) * len(heads[0]) + j]
            last_out = gid["O", len(heads) - 1][0]

            def on_pe():
                for s, n in ready:
                    pe.wait_ge(s, n)
                for kind, i in order:
                    gs = gid[kind, i]
                    if kind == "S":
                        c, qt, j = units[i]
                        for si, g in enumerate(gs):
                            B.acquire(pe, g)
                            B.filled(product(g, B.at(g)[:, 0:segs[si]], [(q_at(heads[c][j], qt), k_at(heads[c][j], si))]), g)
                    elif kind == "T":
                        pe.wait_ge(normed, i + 1)
                        for n, g in enumerate(gs):
                            B.acquire(pe, g)
                            for kt in range(4 * n, min(4 * n + 4, nkt)):
                                ins = pe.transpose(B.at(g)[:, (kt % 4) * P:(kt % 4 + 1) * P],
                                                   pbuf[i % np_][:, kt * P:(kt + 1) * P], ident)
                            B.filled(ins, g)
                    else:
                        g = gs[0]
                        B.acquire(pe, g)
                        for u in range(i * per, (i + 1) * per):
                            for gt in gid["T", u]:
                                B.drained(pe, gt)
                        for kt in range(nkt):
                            for j, h in enumerate(heads[i]):
                                ins = pe.matmul(B.at(g)[j * dv:(j + 1) * dv, :], v_at(h, kt), turned(i, j)[:, kt, :],
                                                start=(kt == 0), stop=(kt == nkt - 1), skip_group_check=True)
                        B.filled(ins, g)

            def on_act():
                for kind, i in order:
                    gs = gid[kind, i]
                    if kind == "S":
                        act.wait_ge(maxed, i + 1)
                        if i >= np_ and bias is None:
                            B.full(act, gid["T", i - np_][-1])
                        o = 0
                        for n, g in enumerate(gs):
                            dst = pbuf[i % np_][:, o:o + segs[n]]
                            o += segs[n]
                            if bias is not None and n == 0:
                                act.activation(dst, dst, ACT.Exp, bias=neg_max(i),
                                               accum_out=sums(i)[:, 0:1]).then_inc(exp_biased, 1)
                            else:
                                B.release(act.activation(dst, B.at(g)[:, 0:segs[n]], ACT.Exp, bias=neg_max(i),
                                                         accum_out=sums(i)[:, n:n + 1]), g)
                    elif kind == "T":
                        c, qt, j = units[i]
                        if qt == 0 and j == 0 and c >= sets:
                            B.full(act, gid["O", c - sets][0])
                        for n, g in enumerate(gs):
                            m = min(4, nkt - 4 * n)
                            B.full(act, g)
                            B.release(act.activation(turned(c, j)[:, 4 * n:4 * n + m, qt * P:(qt + 1) * P],
                                                     B.at(g)[:, 0:m * P].rearrange("p (k q) -> p k q", k=m),
                                                     ACT.Identity), g)

            def on_dve():
                def divide(i):
                    if bias is not None:
                        dve.wait_ge(exp_biased, i + 1)
                    for g in gid["S", i][1 if bias is not None else 0:]:
                        B.drained(dve, g)
                    s = sums(i)[:, 0:1]
                    if nseg == 2:
                        link(dve.tensor_tensor(recip(i)[:, 0:1], sums(i)[:, 0:1], sums(i)[:, 1:2], ALU.add))
                        s = recip(i)[:, 0:1]
                    link(dve.reciprocal(recip(i)[:, 1:2], s))
                    dve.tensor_scalar(pbuf[i % np_], pbuf[i % np_], recip(i)[:, 1:2], None, ALU.mult).then_inc(normed, 1)

                for kind, i in order:
                    gs = gid[kind, i]
                    if kind == "S":
                        c, qt, j = units[i]
                        for n, g in enumerate(gs):
                            B.full(dve, g)
                            if bias is not None and n == 0:
                                if i >= np_:
                                    B.full(dve, gid["T", i - np_][-1])
                                B.release(dve.tensor_tensor_reduce(
                                    out=pbuf[i % np_][:, 0:segs[0]], in0=B.at(g)[:, 0:segs[0]],
                                    in1=bias(heads[c][j], qt), scale=1.0, scalar=NEG * 2, op0=ALU.add, op1=ALU.max,
                                    accum_out=tmp_max(i)[:, 0:1]), g)
                                B.drained(dve, g)
                            elif nseg == 1:
                                dve.tensor_reduce(neg_max(i), B.at(g)[:, 0:segs[0]], AX, ALU.max,
                                                  negate=True).then_inc(maxed, 1)
                            else:
                                link(dve.tensor_reduce(tmp_max(i)[:, n:n + 1], B.at(g)[:, 0:segs[n]], AX, ALU.max))
                        if nseg == 2:
                            dve.tensor_reduce(neg_max(i), tmp_max(i), AX, ALU.max, negate=True).then_inc(maxed, 1)
                        if i >= 1:
                            divide(i - 1)
                        if i == len(units) - 1:
                            divide(i)
                    elif kind == "O":
                        B.full(dve, gs[0])
                        B.release(o_out(i, B.at(gs[0])), gs[0])

            return on_pe, on_act, on_dve, last_out

        g_memT = B.take(4)
        g_columns = B.take(1)
        hn_mix = sem("hn_mix")
        norm1_act, norm1_dve = add_norm([], x_sb, hn, hn_mix, arrived=sem("x_in"))
        g_h1 = B.take(2 * T)
        g_kca = B.take(2)
        g_vca = B.take(2)

        def first_turns_pe():
            pe.wait_ge(sem("const_in"), 16)
            pe.wait_ge(sem("mem_in"), 16)
            transpose_rows(g_memT, mem, 2)
            pe.wait_ge(sem("rows_in"), 16 * N_ROW_LOADS)
            g = g_columns[0]
            B.acquire(pe, g)
            pe.transpose(B.at(g)[:, 0:n_rows], rows, ident[0:n_rows, 0:n_rows])
            B.filled(pe.transpose(B.at(g)[0:2 * ML_H, P:P + 2], gate_b_rows, ident[0:2, 0:2]), g)
            turn_tiles(g_h1, hn, hn_mix)

        def columns_act():
            g = g_columns[0]
            B.full(act, g)
            act.activation(columns, B.at(g)[:, 0:n_rows], ACT.Identity).then_inc(sem("columns"), 1)
            B.release(act.activation(gate_bias, B.at(g)[0:2 * ML_H, P:P + 2], ACT.Identity), g)

        def memory_pe():
            pe.wait_ge(sem("ca_wkv_in"), 16)
            for g in g_memT:
                B.drained(pe, g)
            for i, g in enumerate(g_kca):
                B.acquire(pe, g)
                for h in (2 * i, 2 * i + 1):
                    ins = product(g, B.at(g)[:, (h % 2) * N_MEM:(h % 2 + 1) * N_MEM],
                                  [(ca_wkv[:, k, h * CA_HD:(h + 1) * CA_HD], memT[:, k, :]) for k in range(KD)])
                B.filled(ins, g)
            for m, g in enumerate(g_vca):
                B.acquire(pe, g)
                B.filled(product(g, B.at(g), [(memT[:, k, m * P:(m + 1) * P], ca_wkv[:, k, BANK:]) for k in range(KD)]), g)

        def memory_drain(eng):
            for i, g in enumerate(g_kca):
                drain(eng, g, kT_ca[:, 2 * i:2 * i + 2, :], B.at(g).rearrange("p (h m) -> p h m", h=2))
            for m, g in enumerate(g_vca):
                drain(eng, g, v_ca[:, m, :], B.at(g))

        g_chan = B.take(6)
        g_gate = B.take(1)
        g_aq = B.take(T)
        g_akv = B.take(T)
        g_cols = B.take(1)
        g_vo = B.take(T)
        g_pool = B.take(2)

        def project_pe():
            for g in g_h1:
                B.drained(pe, g)
            for c, g in enumerate(g_chan):
                if c % 4 == 0:
                    pe.wait_ge(w_in_loaded[c // 4], 16 * len(W_IN_COLS[c // 4]))
                B.acquire(pe, g)
                B.filled(product(g, B.at(g), [(w_in[c // 4][:, k, (c % 4) * P:(c % 4 + 1) * P], hT[:, k, :])
                                             for k in range(KD)]), g)
            pe.wait_ge(sem("w_gate_in"), 16)
            g = g_gate[0]
            B.acquire(pe, g)
            for k in range(KD):
                for i in range(2):
                    ins = pe.matmul(B.at(g)[64 * i:64 * i + 8, :], w_gate[:, k, 8 * i:8 * i + 8], hT[:, k, :],
                                    start=(k == 0), stop=(k == KD - 1), skip_group_check=True)
            B.filled(ins, g)
            project_tokens_pe(g_aq, 3, 0, 512)
            project_tokens_pe(g_akv, 1, 256, 256)

        def project_tokens_pe(groups, i, c0, n):
            pe.wait_ge(w_in_loaded[i], 16 * len(W_IN_COLS[i]))
            for t, g in enumerate(groups):
                B.acquire(pe, g)
                B.filled(product(g, B.at(g)[:, 0:n], [(hT[:, k, t * P:(t + 1) * P], w_in[i][:, k, c0:c0 + n])
                                                     for k in range(KD)]), g)

        def project_act():
            for c, g in enumerate(g_chan):
                B.full(act, g)
                if c == 0:
                    act.wait_ge(sem("pads"), 2)
                dst = upad[:, c, PADL:PADL + S] if c < 2 else qkpad[:, c - 2, 2:2 + S]
                B.release(copy(act, dst, B.at(g)), g)
            g = g_gate[0]
            B.full(act, g)
            B.drained(act, g_columns[0])
            act.activation(gi, B.at(g)[0:8, :], ACT.Identity, bias=gate_bias[:, 0:1]).then_inc(sem("gate_i"), 1)
            B.release(copy(act, gf, B.at(g)[64:72, :], None, gate_bias[:, 1:2]), g)
            gates_act()
            for t, g in enumerate(g_aq):
                B.full(act, g)
                B.release(copy(act, aq[:, t].rearrange("p (i g) d -> p g i d", g=2),
                               B.at(g).rearrange("p (g i d) -> p g i d", g=2, i=4)), g)
            for t, g in enumerate(g_akv):
                B.full(act, g)
                act.activation(ak[:, t], B.at(g)[:, 0:128].rearrange("p (h d) -> p h d", h=2),
                               ACT.Identity).then_inc(sem("ak"), 1)
                B.release(copy(act, av[:, t, :], B.at(g)[:, 128:256]), g)

        def project_vo_act():
            for t, g in enumerate(g_vo):
                B.full(act, g)
                if t == 0:
                    act.wait_ge(sem("pads"), 3)
                act.activation(sig_o[:, t, :], B.at(g)[:, 256:512], ACT.Sigmoid).then_inc(sem("sig_o"), 1)
                B.release(copy(act, v_aug[:, t, :, 0:HD], B.at(g)[:, 0:256].rearrange("p (h d) -> p h d", h=ML_H)), g)

        def pool_dve():
            for g in g_chan[0:2]:
                B.drained(dve, g)
            L = UP
            link(dve.tensor_tensor(p1[:, :, 1:L], upad[:, :, 0:L - 1], upad[:, :, 1:L], ALU.add))
            link(dve.tensor_tensor(p2[:, :, 2:L - 1], p1[:, :, 1:L - 2], p1[:, :, 3:L], ALU.add))
            link(dve.tensor_tensor(p3[:, 4:L - 3], p2[:, 1, 2:L - 5], p2[:, 1, 6:L - 1], ALU.add))
            link(dve.tensor_tensor(p1[64:128, 1, 8:L - 7], p3[64:128, 4:L - 11], p3[64:128, 12:L - 3], ALU.add))
            dve.wait_ge(sem("inv_n_in"), 16)
            B.full(dve, g_h1[-1])
            w = slice(PADL, PADL + S)
            for c, lo, hi, s in ((0, 0, 64, p1[0:64, 0, w]), (0, 64, 128, p2[64:128, 0, w]),
                                 (1, 0, 64, p3[0:64, w]), (1, 64, 128, p1[64:128, 1, w])):
                link(dve.tensor_tensor(d_pool[lo:hi, c, :], s, inv_n[lo:hi, c, :], ALU.mult))
                dve.tensor_tensor(d_pool[lo:hi, c, :], d_pool[lo:hi, c, :], upad[lo:hi, c, w],
                                  ALU.subtract).then_inc(sem("pooled"), 1)

        def pool_pe():
            pe.wait_ge(sem("pooled"), 4)
            pe.wait_ge(sem("pool_w_in"), 16)
            for c, g in enumerate(g_pool):
                B.acquire(pe, g)
                for lo in (0, 64):
                    ins = pe.matmul(B.at(g)[lo:lo + 64, :], pool_w[lo:lo + 64, c, :], d_pool[lo:lo + 64, c, :],
                                    start=True, stop=True)
                B.filled(ins, g)

        def pool_act():
            for c, g in enumerate(g_pool):
                B.full(act, g)
                B.release(copy(act, ymixT[:, c, :], B.at(g), pool_scale[:, c:c + 1]), g)

        def conv_dve():
            for g in g_chan[2:6]:
                B.drained(dve, g)
            for c in range(4):
                link(dve.tensor_scalar(qkT[:, c, :], qkpad[:, c, 0:S], conv_w[:, c, 0:1], None, ALU.mult))
                for w in range(1, ML_CONV):
                    ins = dve.scalar_tensor_tensor(out=qkT[:, c, :], in0=qkpad[:, c, w:w + S], scalar=conv_w[:, c, w:w + 1],
                                                   in1=qkT[:, c, :], op0=ALU.mult, op1=ALU.add)
                    if w < ML_CONV - 1:
                        link(ins)
                    else:
                        ins.then_inc(sem("conv"), 1)

        def conv_act():
            for c in range(4):
                act.wait_ge(sem("conv"), c + 1)
                act.activation(qkT[:, c, :], qkT[:, c, :], ACT.Silu).then_inc(sem("qk_silu"), 1)

        gi, gf, e_f, l_f, bsum, arow, mrow, bm = grow
        arow2, mrow2, bm2 = gi, l_f, gf
        rows_f, rows_b = sem("gate_rows_f"), sem("gate_rows_b")

        def gates_dve():
            B.drained(dve, g_gate[0])
            dve.scalar_tensor_tensor(out=e_f, in0=gf, scalar=-1.0, in1=gf, op0=ALU.mult, op1=ALU.min).then_inc(sem("neg_abs_f"), 1)
            dve.wait_ge(sem("log_f"), 1)
            link(dve.scalar_tensor_tensor(out=e_f, in0=gf, scalar=0.0, in1=l_f, op0=ALU.min, op1=ALU.subtract))
            ones8 = const[0:8, C_ONE:C_ONE + 1].to_broadcast([8, S])
            link(dve.tensor_tensor_scan(bsum, ones8, e_f, 0.0, ALU.mult, ALU.add))
            link(dve.tensor_tensor(arow, gi, bsum, ALU.subtract))
            link(dve.tensor_tensor_scan(mrow, arow, arow, 0.0, ALU.max, ALU.max))
            link(dve.tensor_tensor(bm, bsum, mrow, ALU.add))
            dve.tensor_scalar(mrow, mrow, -1.0, None, ALU.mult).then_inc(rows_f, 1)
            link(dve.tensor_tensor_scan(bsum[:, ::-1], ones8, e_f[:, ::-1], 0.0, ALU.mult, ALU.add))
            link(dve.tensor_tensor(arow2, gi, bsum, ALU.subtract))
            link(dve.tensor_tensor_scan(mrow2[:, ::-1], arow2[:, ::-1], arow2[:, ::-1], 0.0, ALU.max, ALU.max))
            link(dve.tensor_tensor(bm2, bsum, mrow2, ALU.add))
            dve.tensor_scalar(mrow2, mrow2, -1.0, None, ALU.mult).then_inc(rows_b, 1)

        def gates_act():
            act.wait_ge(sem("neg_abs_f"), 1)
            act.activation(e_f, e_f, ACT.Exp).then_inc(sem("exp_f"), 1)
            act.wait_ge(sem("exp_f"), 1)
            act.activation(l_f, e_f, ACT.Ln, bias=1.0).then_inc(sem("log_f"), 1)

        def gate_columns_act():
            g = g_cols[0]
            B.full(act, g)
            v = B.at(g)[:, 0:P].rearrange("p (k t r) -> p k t r", k=4, t=T)
            act.activation(gcols[:, 0:2], v[:, 0:2], ACT.Identity).then_inc(sem("gate_columns"), 1)
            B.release(act.activation(gcols[:, 2:4], v[:, 2:4], ACT.Exp, scale=-1.0), g)

        def gates_pe():
            pe.wait_ge(rows_f, 1)
            pe.wait_ge(rows_b, 1)
            g = g_cols[0]
            B.acquire(pe, g)
            for k, r in enumerate((arow, arow2, bm, bm2)):
                for t in range(T):
                    ins = pe.transpose(B.at(g)[:, (k * T + t) * 8:(k * T + t) * 8 + 8], r[:, t * P:(t + 1) * P], ident[0:8, 0:8])
            B.filled(ins, g)

        def silu_c_act():
            B.drained(act, g_columns[0])
            act.wait_ge(sem("pads"), 4)
            for v, name in enumerate(("c_2", "c_ctx_2")):
                act.activation(c_pad[:, :, v], column[name], ACT.Silu).then_inc(sem("silu_c"), 1)

        def mod_pe():
            pe.wait_ge(sem("silu_c"), 2)
            g = g_mod[0]
            B.acquire(pe, g)
            for k in range(KD):
                if k % 2 == 0:
                    pe.wait_ge(w_mod_loaded[k // 2], 16)
                for j in range(4):
                    ins = pe.matmul(B.at(g)[32 * j:32 * j + 32, :], c_pad[:, k, :],
                                    w_mod[k // 2][:, k % 2, j * BANK:(j + 1) * BANK],
                                    start=(k == 0), stop=(k == KD - 1), skip_group_check=True)
            B.filled(ins, g)

        def mod_dve():
            g = g_mod[0]
            B.full(dve, g)
            B.release(dve.tensor_copy(mod_rows, B.at(g)), g)

        def mod_turn_pe():
            B.drained(pe, g_mod[0])
            g = g_modT[0]
            B.acquire(pe, g)
            for m in range(4):
                ins = pe.transpose(B.at(g)[:, m * P:(m + 1) * P], mod_rows[:, m * P:(m + 1) * P], ident)
            B.filled(ins, g)

        def mod_turn_dve():
            g = g_modT[0]
            B.full(dve, g)
            v = B.at(g).rearrange("p (m j r) -> p j m r", m=4, j=4)
            for j in range(4):
                ins = dve.tensor_tensor(mod[:, 4 * j:4 * j + 4, :], v[:, j, :, 0:2],
                                        b_mod_col[:, 4 * j:4 * j + 4].unsqueeze(2).to_broadcast([P, 4, 2]), ALU.add)
                if j < 3:
                    link(ins)
            B.release(ins, g)
            B.drained(dve, g)
            link(dve.tensor_scalar(mod[:, KD:, :], mod[:, KD:, :], 1.0, None, ALU.add))
            link(dve.tensor_tensor(mod[:, KD:, :], mod[:, KD:, :], gain["norm_g_2"].unsqueeze(2).to_broadcast([P, KD, 2]),
                                   ALU.mult))

        def gate2_pe():
            g = g_gate2[0]
            B.acquire(pe, g)
            for k in range(KD):
                if k % 4 == 0:
                    pe.wait_ge(w_modg_loaded[k // 4], 16)
                for j in range(2):
                    ins = pe.matmul(B.at(g)[32 * j:32 * j + 32, :], c_pad[:, k, :],
                                    w_modg[k // 4][:, k % 4, j * BANK:(j + 1) * BANK],
                                    start=(k == 0), stop=(k == KD - 1), skip_group_check=True)
            B.filled(ins, g)
            B.drained(pe, g)
            for j, g in enumerate(g_gate_row):
                B.acquire(pe, g)
                B.filled(product(g, B.at(g), [(ones[0:1, :], gate_lin[j])]), g)

        def gate2_dve():
            dve.wait_ge(sem("gate_lin_in"), 16 * 2)
            g = g_gate2[0]
            B.full(dve, g)
            dve.tensor_tensor(gate_lin[0], B.at(g)[0:1, :], gate_lin[0], ALU.add).then_inc(sem("gate_half"), 1)
            dve.wait_ge(sem("gate_half"), 1)
            B.release(dve.tensor_tensor(gate_lin[1], B.at(g)[32:33, :], gate_lin[1], ALU.add), g)

        def gate_row_act():
            for j, g in enumerate(g_gate_row):
                B.full(act, g)
                B.release(copy(act, gate_row[:, j * BANK:(j + 1) * BANK], B.at(g)), g)

        g_mm, g_ms, g_mo = {}, {}, {}
        g_mm[0], g_ms[0] = B.take(2), B.take(T)
        g_mod = B.take(1)
        for h in range(ML_H):
            if h + 1 < ML_H:
                g_mm[h + 1] = B.take(2)
            g_mo[h] = B.take(2)
            if h + 1 < ML_H:
                g_ms[h + 1] = B.take(T)
            if h == 0:
                g_modT = B.take(1)
        g_qT = B.take(4)
        g_kT = B.take(1)
        g_gate2 = B.take(1)
        g_gate_row = B.take(2)

        def mlstm_max_pe(h):
            for d, m in ((0, mrow), (1, mrow2)):
                g, r = g_mm[h][d], d * ML_H + h
                B.acquire(pe, g)
                B.filled(product(g, B.at(g), [(ident[0:8, r:r + 1].to_broadcast([8, P]), m)]), g)

        def mlstm_scores_pe(h):
            lo, c = (h % 2) * HD, h // 2
            for i, g in enumerate(g_ms[h]):
                B.acquire(pe, g)
                B.filled(product(g, B.at(g), [(qkT[lo:lo + HD, 2 + c, i * P:(i + 1) * P], qkT[lo:lo + HD, c, :])]), g)

        def mlstm_values_pe(h):
            for d, g in enumerate(g_mo[h]):
                B.acquire(pe, g)
                if d == 0:
                    pe.wait_ge(sem("ml_weights0"), T * (h + 1))
                else:
                    for gs in g_ms[h]:
                        B.drained(pe, gs)
                for j in range(T):
                    tiles = range(0, j + 1) if d == 0 else range(j, T)
                    ins = product(g, B.at(g)[:, j * (HD + 1):(j + 1) * (HD + 1)],
                                  [(Pt[h % 2][d][:, i, j * P:(j + 1) * P], v_aug[:, i, h, :]) for i in tiles])
                B.filled(ins, g)

        def mlstm_pe():
            for g in g_vo:
                B.drained(pe, g)
            mlstm_max_pe(0)
            pe.wait_ge(sem("qk_silu"), 4)
            mlstm_scores_pe(0)
            mod_pe()
            for h in range(ML_H):
                if h + 1 < ML_H:
                    mlstm_max_pe(h + 1)
                mlstm_values_pe(h)
                if h + 1 < ML_H:
                    mlstm_scores_pe(h + 1)
                if h == 0:
                    mod_turn_pe()

        def mlstm_act():
            act.wait_ge(sem("gate_columns"), 1)
            for h in range(ML_H):
                for d, g in enumerate(g_mm[h]):
                    r = d * ML_H + h
                    if h >= 2:
                        B.full(act, g_mo[h - 2][d])
                    B.full(act, g)
                    if h == 1 and d == 0:
                        B.full(act, g_pool[-1])
                    for i in range(T):
                        o = slice(i * P, S) if d == 0 else slice(0, (i + 1) * P)
                        ins = act.activation(Pt[h % 2][d][:, i, o], B.at(g)[:, o], ACT.Exp, bias=gcols[:, d, i, r:r + 1])
                    B.release(ins, g)

        def diagonal(pt):
            v = pt.rearrange("p i (j q) -> p (i j) q", q=P)
            return v[:, 0::T + 1, :]

        def mlstm_pool():
            for h in range(ML_H):
                for d in range(2):
                    B.drained(pool, g_mm[h][d])
                    v = diagonal(Pt[h % 2][d])
                    sign = 1 if d == 0 else -1
                    pool.affine_select(out=v, in_=v, pattern=[[0, T], [sign, P]], compare_op=ALU.is_ge, fill=0.0,
                                       base=0, channel_multiplier=-sign).then_inc(sem(f"ml_masked{d}"), 1)

        def mlstm_weights_dve(h):
            for d in range(2):
                dve.wait_ge(sem(f"ml_masked{d}"), h + 1)
                for i, g in enumerate(g_ms[h]):
                    o = slice(i * P, S) if d == 0 else slice(0, (i + 1) * P)
                    pt = Pt[h % 2][d][:, i, o]
                    B.full(dve, g)
                    ins = dve.scalar_tensor_tensor(out=pt, in0=B.at(g)[:, o], scalar=HD ** -0.5, in1=pt,
                                                   op0=ALU.mult, op1=ALU.mult)
                    if d == 0:
                        ins.then_inc(sem("ml_weights0"), 1)
                    else:
                        B.release(ins, g)

        def mlstm_values_dve(h):
            for d, g in enumerate(g_mo[h]):
                r = d * ML_H + h
                B.full(dve, g)
                v = B.at(g)[:, 0:T * (HD + 1)].rearrange("p (t e) -> p t e", t=T)
                link(dve.tensor_copy(ml_stat[:, 1, :], v[:, :, HD]))
                link(dve.scalar_tensor_tensor(out=ml_stat[:, 0, :], in0=ml_stat[:, 1, :], scalar=-1.0,
                                              in1=ml_stat[:, 1, :], op0=ALU.mult, op1=ALU.max))
                link(dve.tensor_tensor(ml_stat[:, 1, :], ml_stat[:, 0, :], gcols[:, 2 + d, :, r], ALU.max))
                link(dve.reciprocal(ml_stat[:, 2, :], ml_stat[:, 1, :]))
                w = ml_stat[:, 2, :].unsqueeze(2).to_broadcast([P, T, HD])
                if d == 0:
                    B.release(dve.tensor_tensor(hsum[:, :, h, :], v[:, :, 0:HD], w, ALU.mult), g)
                else:
                    B.release(dve.tensor_tensor(htmp[:, :, h, :], v[:, :, 0:HD], w, ALU.mult), g)
                    B.drained(dve, g)
                    link(dve.tensor_tensor(hsum[:, :, h, :], hsum[:, :, h, :], htmp[:, :, h, :], ALU.add))

        def mlstm_dve():
            B.drained(dve, g_cols[0])
            mlstm_weights_dve(0)
            mod_dve()
            for h in range(ML_H):
                mlstm_values_dve(h)
                if h + 1 < ML_H:
                    mlstm_weights_dve(h + 1)
                if h == 0:
                    mod_turn_dve()

        def mlstm_norm_dve():
            link(dve.tensor_tensor(htmp, hsum, hsum, ALU.mult))
            link(dve.tensor_reduce(stat[:, 0:16].rearrange("p (t h) -> p t h", t=T), htmp, AX, ALU.add))
            dve.tensor_scalar(stat[:, 16:32], stat[:, 0:16], 1.0 / HD, EPS, ALU.mult, ALU.add).then_inc(sem("ml_mean"), 1)
            dve.wait_ge(sem("ml_root"), 1)
            link(dve.reciprocal(stat[:, 16:32], stat[:, 0:16]))
            rs = stat[:, 16:32].rearrange("p (t h) -> p t h", t=T).unsqueeze(3).to_broadcast([P, T, ML_H, HD])
            link(dve.tensor_tensor(hsum, hsum, rs, ALU.mult))
            dve.wait_ge(sem("head_rows_in"), 16 * 3)
            flat = hsum.rearrange("p t h d -> p t (h d)")
            link(dve.tensor_tensor(flat, flat, ml_g.unsqueeze(1).to_broadcast([P, T, ML_H * HD]), ALU.mult))
            dve.wait_ge(sem("sig_o"), T)
            dve.tensor_tensor(flat, flat, sig_o, ALU.mult).then_inc(sem("y_mlstm"), 1)

        def mlstm_norm_act():
            act.wait_ge(sem("ml_mean"), 1)
            act.activation(stat[:, 0:16], stat[:, 16:32], ACT.Sqrt).then_inc(sem("ml_root"), 1)

        def mlstm_out_pe():
            pe.wait_ge(sem("y_mlstm"), 1)
            transpose_rows(g_mlT, hsum.rearrange("p t h d -> p t (h d)"), T)

        def mlstm_out_drain(eng):
            drain_rows(eng, g_mlT, T, ymixT[:, 2:4, :])

        def rope_pairs(v, heads):
            even, odd = v[:, :, :, 0::2], v[:, :, :, 1::2]
            cos, sin = (const[:, c:c + 128].rearrange("p (t f) -> p t f", t=T).unsqueeze(2).to_broadcast([P, T, heads, 32])
                        for c in (C_COS, C_SIN))
            t0, t1 = (r[:, 0:heads, :] for r in rope_t)
            for t in range(T):
                link(dve.tensor_tensor(t0, even[:, t], sin[:, t], ALU.mult))
                link(dve.tensor_tensor(t1, odd[:, t], sin[:, t], ALU.mult))
                link(dve.tensor_tensor(even[:, t], even[:, t], cos[:, t], ALU.mult))
                link(dve.tensor_tensor(odd[:, t], odd[:, t], cos[:, t], ALU.mult))
                link(dve.tensor_tensor(even[:, t], even[:, t], t1, ALU.subtract))
                ins = dve.tensor_tensor(odd[:, t], odd[:, t], t0, ALU.add)
                if t < T - 1:
                    link(ins)
            return ins

        head_groups = ((aq, AT_H, qg, 0, "q"), (ak, 2, kg, T * AT_H, "k"))
        N_HEAD_ROWS = T * (AT_H + 2)

        def heads_dve():
            for g in (*g_aq, *g_akv):
                B.drained(dve, g)
            dve.wait_ge(sem("ak"), T)
            for v, heads, gn, o, name in head_groups:
                sq = sq_q[:, :, 0:heads, :]
                link(dve.tensor_tensor(sq, v, v, ALU.mult))
                link(dve.tensor_reduce(stat[:, o:o + T * heads].rearrange("p (t h) -> p t h", t=T), sq, AX, ALU.add))
            means = stat[:, 0:N_HEAD_ROWS]
            dve.tensor_scalar(means, means, 1.0 / HD, EPS, ALU.mult, ALU.add).then_inc(sem("head_means"), 1)
            dve.wait_ge(sem("head_roots"), 1)
            link(dve.reciprocal(means, means))
            dve.wait_ge(sem("head_rows_in"), 16 * 3)
            for v, heads, gn, o, name in head_groups:
                rs = stat[:, o:o + T * heads].rearrange("p (t h) -> p t h", t=T).unsqueeze(3).to_broadcast([P, T, heads, HD])
                link(dve.tensor_tensor(v, v, rs, ALU.mult))
                flat = v.rearrange("p t h d -> p (t h) d")
                link(dve.tensor_tensor(flat, flat, gn.unsqueeze(1).to_broadcast([P, T * heads, HD]), ALU.mult))
                rope_pairs(v, heads).then_inc(sem(f"roped_{name}"), 1)
                if name == "q":
                    dve.wait_ge(sem("roped_q"), 1)

        def heads_act():
            act.wait_ge(sem("head_means"), 1)
            means = stat[:, 0:N_HEAD_ROWS]
            act.activation(means, means, ACT.Sqrt).then_inc(sem("head_roots"), 1)

        def heads_pe():
            pe.wait_ge(sem("roped_q"), 1)
            for i, g in enumerate(g_qT):
                B.acquire(pe, g)
                for t in range(T):
                    ins = pe.transpose(B.at(g)[:, t * P:(t + 1) * P], aq[:, t, 2 * i:2 * i + 2, :].rearrange("p g d -> p (g d)"), ident)
                B.filled(ins, g)
            pe.wait_ge(sem("roped_k"), 1)
            g = g_kT[0]
            B.acquire(pe, g)
            for t in range(T):
                ins = pe.transpose(B.at(g)[:, t * P:(t + 1) * P], ak[:, t].rearrange("p h d -> p (h d)"), ident)
            B.filled(ins, g)

        def heads_drain(eng):
            for i, g in enumerate(g_qT):
                drain(eng, g, qT_at[:, i, :], B.at(g), HD ** -0.5)
            drain(eng, g_kT[0], kT_at, B.at(g_kT[0]))

        def heads_ready_pe():
            for g in (*g_qT, *g_kT):
                B.drained(pe, g)

        half = lambda h: slice((h // 4) * HD, (h // 4 + 1) * HD)
        attn_pe, attn_act, attn_dve, g_attn_end = attention(
            "attn", [(i, i + 4) for i in range(4)], [S],
            lambda h, qt: qT_at[half(h), h % 4, qt * P:(qt + 1) * P], lambda h, si: kT_at[half(h), :],
            lambda h, kt: av[:, kt, half(h)], HD, p_at, pt_at,
            lambda i, o: dve.tensor_copy(ymixT[:, 4 + i, :], o), [])
        g_mlT = B.take(2)

        g_out1 = B.take(2 * T)

        def add_product_pe(groups, lhs, rhs, chunks):
            for i, g in enumerate(groups):
                t, n = i // 2, i % 2
                B.acquire(pe, g)
                B.filled(product(g, B.at(g), [(lhs(k)[:, t * P:(t + 1) * P], rhs(k)[:, n * BANK:(n + 1) * BANK])
                                              for k in range(chunks)]), g)

        def out1_pe():
            pe.wait_ge(sem("w_out_in"), 16 * 3)
            for g in (*g_pool, *g_mlT, g_attn_end):
                B.drained(pe, g)
            add_product_pe(g_out1, lambda k: ymixT[:, k, :], lambda k: w_out[:, k, :], KD)

        hn_mem = sem("hn_mem")
        norm2_act, norm2_dve = add_norm(g_out1, x_sb, hn_ca, hn_mem)
        g_h2 = B.take(KD)
        g_qca = B.take(CA_H)

        def qca_pe():
            pe.wait_ge(sem("ca_wq_in"), 16)
            for g in g_h2:
                B.drained(pe, g)
            for h, g in enumerate(g_qca):
                B.acquire(pe, g)
                B.filled(product(g, B.at(g), [(ca_wq[:, k, h * CA_HD:(h + 1) * CA_HD], hT[:, k, :]) for k in range(KD)]), g)

        def qca_drain(eng):
            for h, g in enumerate(g_qca):
                drain(eng, g, qT_ca[:, h, :], B.at(g), CA_HD ** -0.5)

        ca_pe, ca_act, ca_dve, g_ca_end = attention(
            "ca", [(h,) for h in range(CA_H)], [N_MEM],
            lambda h, qt: qT_ca[:, h, qt * P:(qt + 1) * P], lambda h, si: kT_ca[:, h, :],
            lambda h, kt: v_ca[:, kt, h * CA_HD:(h + 1) * CA_HD], CA_HD, p_ca, pt_ca,
            lambda i, o: dve.tensor_copy(oT_ca[:, i, :], o), [])
        g_out2 = B.take(2 * T)

        def ca_all_pe():
            for g in g_qca:
                B.drained(pe, g)
            ca_pe()
            pe.wait_ge(sem("ca_wo_in"), 16)
            B.drained(pe, g_ca_end)
            add_product_pe(g_out2, lambda k: oT_ca[:, k, :], lambda k: ca_wo[:, k, :], CA_H)

        hn_ffn = sem("hn_ffn")
        norm3_act, norm3_dve = add_norm(g_out2, x_sb, hn, hn_ffn)
        g_h3 = B.take(KD)
        hn_ctx = sem("hn_ctx")
        normc_act, normc_dve = rms_rows(ctx_n, ctx_n, 2, D, hn_ctx)
        hT_junk = cut(W, 6656, 2, D)
        g_logit = B.take(1)
        g_affT = B.take(1)
        g_ctx = B.take(4)
        g_slots = B.take(1)

        def route_pe():
            for g in g_h3:
                B.drained(pe, g)
            pe.wait_ge(sem("router_in"), 16)
            g = g_logit[0]
            B.acquire(pe, g)
            for t in range(T):
                ins = product(g, B.at(g)[:, t * N_EXP:(t + 1) * N_EXP],
                              [(hT[:, k, t * P:(t + 1) * P], router_w[:, k, :]) for k in range(KD)])
            B.filled(ins, g)
            pe.wait_ge(sem("aff"), 1)
            g = g_affT[0]
            B.acquire(pe, g)
            for t in range(T):
                ins = pe.transpose(B.at(g)[0:N_EXP, t * P:(t + 1) * P], aff[:, t, :], ident)
            B.filled(ins, g)
            ctx_pe()
            pe.wait_ge(sem("slot_rows"), 1)
            g = g_slots[0]
            B.acquire(pe, g)
            for t in range(T):
                ins = pe.transpose(B.at(g)[:, t * N_EXP:(t + 1) * N_EXP], slotT[:, t * P:(t + 1) * P], ident[0:N_EXP, 0:N_EXP])
            B.filled(ins, g)

        def ctx_norm_act():
            act.wait_ge(sem("ctx_in"), 16)
            normc_act(junk=hT_junk)

        def ctx_pe():
            pe.wait_ge(hn_ctx, 2)
            transpose_rows(g_ctx, ctx_n, 2)

        def ctx_drain_act():
            for i, g in enumerate(g_ctx):
                B.full(act, g)
                for k in (2 * i, 2 * i + 1):
                    ins = copy(act, hcT[:, k, :], B.at(g)[:, (k % 2) * CTX:(k % 2 + 1) * CTX], mod[:, KD + k, 1:2], mod[:, k, 1:2])
                B.release(ins, g)

        def route_act():
            B.drained(act, g_logit[0])
            act.activation(aff, aff, ACT.Exp).then_inc(sem("exp_logits"), 1)

        def route_dve():
            g = g_logit[0]
            B.full(dve, g)
            v = B.at(g)[:, 0:T * N_EXP].rearrange("p (t e) -> p t e", t=T)
            link(dve.tensor_reduce(stat[:, 32:36], v, AX, ALU.max))
            B.release(dve.tensor_tensor(aff, v, stat[:, 32:36].unsqueeze(2).to_broadcast([P, T, N_EXP]), ALU.subtract), g)
            dve.wait_ge(sem("exp_logits"), 1)
            link(dve.tensor_reduce(stat[:, 36:40], aff, AX, ALU.add))
            link(dve.reciprocal(stat[:, 40:44], stat[:, 36:40]))
            dve.tensor_tensor(aff, aff, stat[:, 40:44].unsqueeze(2).to_broadcast([P, T, N_EXP]), ALU.mult).then_inc(sem("aff"), 1)
            g = g_affT[0]
            B.full(dve, g)
            B.release(dve.tensor_copy(affT, B.at(g)[0:N_EXP, :]), g)
            B.drained(dve, g)
            link(dve.tensor_copy(left, affT))
            for r in range(CAP // 8):
                eight = top8[:, 8 * r:8 * r + 8]
                link(dve.max(eight, left))
                link(dve.match_replace(left, eight, left, -1.0))
            link(dve.tensor_tensor(left, left, affT, ALU.not_equal))
            link(dve.memset(zero16, 1.0))
            link(dve.tensor_tensor_scan(slotT, zero16, left, 0.0, ALU.mult, ALU.add))
            link(dve.tensor_tensor(slotT, slotT, left, ALU.mult))
            dve.tensor_scalar(slotT, slotT, 1.0, None, ALU.subtract).then_inc(sem("slot_rows"), 1)
            g = g_slots[0]
            B.full(dve, g)
            B.release(dve.tensor_copy(slot_of, B.at(g)[:, 0:T * N_EXP].rearrange("p (t e) -> p t e", t=T)), g)
            B.drained(dve, g)

        PAIRS, PIECES = N_EXP // 2, 24
        AHEAD = NSLOT
        xsT_full, xsT_sb = sem("xsT_full"), [sem("xsT_sb_act"), sem("xsT_sb_dve")]
        sel_ready, selgT_full, selgT_sb = sem("sel_ready"), sem("selgT_full"), sem("selgT_sb")
        silu_ready, hid_ready = sem("silu_ready"), sem("hid_ready")
        hidT_full, hidT_sb = sem("hidT_full"), [sem("hidT_sb_act"), sem("hidT_sb_dve")]
        y_sb = sem("y_sb")
        added_full, added = sem("added_full"), sem("added")
        posc_ready = sem("posc_ready")
        w_gu, w_down = a["expert_w_gu"][0], a["expert_w_down"][0]

        def piece_source(expert, i):
            if i < KD:
                return w_gu[bass.ds(expert, 1), i * P:(i + 1) * P, :].rearrange("e p f -> p (e f)")
            q = i - KD
            return w_down[bass.ds(expert, 1), q * 512:(q + 1) * 512, :].rearrange("e (j p) d -> p (e j) d", p=P)

        def piece_target(s, i):
            return slot(s) if i < KD else slot(s).rearrange("p (j d) -> p j d", j=4)

        def load_piece(expert, i, s):
            sp.dma_start(piece_target(s, i), piece_source(expert, i)).then_inc(slot_loaded[s], 16)

        def experts_sp():
            for i in range(AHEAD):
                if i == 0:
                    B.full(sp, g_out1[-1])
                if i == 2:
                    B.full(sp, g_qca[-1])
                if i == 3:
                    B.full(sp, g_out2[-1])
                    sp.dma_start(ctx_n, a["ctx_2"][0].rearrange("(t p) d -> p t d", p=P)).then_inc(sem("ctx_in"), 16)
                if i == 7:
                    B.full(sp, g_slots[-1])
                load_piece(0, i, i)
            with sp.Fori(0, PAIRS - 1) as p:
                for n in range(AHEAD, PIECES + AHEAD):
                    e, i = n // 12, n % 12
                    sp.wait_ge(slot_free[n % NSLOT], 3 * p + n // NSLOT)
                    load_piece(2 * p + e, i, n % NSLOT)
            for n in range(AHEAD, PIECES):
                e, i = n // 12, n % 12
                sp.wait_ge(slot_free[n % NSLOT], 3 * (PAIRS - 1) + n // NSLOT)
                load_piece(2 * (PAIRS - 1) + e, i, n % NSLOT)

        GATHER, TURN = (4, 5), (4, 5)
        ADD_BANKS = (7, 4, 5, 0, 1, 2, 3, 6)

        def piece(n, p):
            s = n % NSLOT
            pe.wait_ge(slot_loaded[s], 48 * p + 16 * (n // NSLOT + 1))
            return slot(s)

        before_experts = range(B.next - NBANK, B.next)

        def experts_pe():
            for g in before_experts:
                B.drained(pe, g)
            with pe.Fori(0, PAIRS) as p:
                pe.wait_ge(sel_ready, p + 1)
                pe.wait_ge(added, 2 * T * p + 1)
                for k in range(KD):
                    for t in range(T):
                        ins = pe.matmul(psum[:, GATHER[k // 4], (k % 4) * P:(k % 4 + 1) * P], hn[:, t, k * P:(k + 1) * P],
                                        sel[:, t, :], start=(t == 0), stop=(t == T - 1))
                    if k % 4 == 3:
                        ins.then_inc(xsT_full, 1)
                for t in range(T):
                    ins = pe.transpose(psum[:, 7, t * P:(t + 1) * P], selg[:, t, :], ident)
                ins.then_inc(selgT_full, 1)
                pe.wait_ge(xsT_sb[0], p + 1)
                pe.wait_ge(xsT_sb[1], p + 1)
                for e in range(2):
                    for k in range(KD):
                        w = piece(12 * e + k, p)
                        for c in range(4):
                            for h in range(2):
                                ins = pe.matmul(psum[h * 64:(h + 1) * 64, c, :], xsT[:, k, e * CAP:(e + 1) * CAP],
                                                w[:, (2 * c + h) * BANK:(2 * c + h + 1) * BANK],
                                                start=(k == 0), stop=(k == KD - 1), skip_group_check=True)
                        ins.then_inc(slot_free[(12 * e + k) % NSLOT], 1)
                    for b in range(2):
                        pe.wait_ge(hid_ready, 4 * p + 2 * e + b + 1)
                        for j in range(4):
                            ins = pe.transpose(psum[:, TURN[b], j * P:(j + 1) * P], hid[:, b, j * P:(j + 1) * P], ident)
                        ins.then_inc(hidT_full, 1)
                    for q in range(4):
                        b, h = q // 2, q % 2
                        if h == 0:
                            pe.wait_ge(hidT_sb[b], 2 * p + e + 1)
                        if q == 0 and e == 1:
                            pe.wait_ge(y_sb, 4 * p + 2)
                        w = piece(12 * e + KD + q, p).rearrange("p (j d) -> p j d", j=4)
                        for j in range(4):
                            for n in range(2):
                                ins = pe.matmul(psum[n * 64:(n + 1) * 64, 6, :], hidT[b][:, j, h, :],
                                                w[:, j, n * BANK:(n + 1) * BANK], start=(q == 0 and j == 0),
                                                stop=(q == 3 and j == 3), skip_group_check=True)
                        ins.then_inc(slot_free[(12 * e + KD + q) % NSLOT], 1)
                pe.wait_ge(selgT_sb, p + 1)
                pe.wait_ge(y_sb, 4 * p + 4)
                for i, bank in enumerate(ADD_BANKS):
                    t, n = i // 2, i % 2
                    pe.matmul(psum[:, bank, :], selgT[:, t * P:(t + 1) * P], ypair[:, n * BANK:(n + 1) * BANK],
                              start=True, stop=True).then_inc(added_full, 1)
            pe.wait_ge(added, 2 * T * PAIRS + 1)

        def gu_done(eng, p, e):
            n = 12 * e + KD - 1
            eng.wait_ge(slot_free[n % NSLOT], 3 * p + n // NSLOT + 1)

        def y_done(eng, p, e):
            n = 12 * e + 11
            eng.wait_ge(slot_free[n % NSLOT], 3 * p + n // NSLOT + 1)

        def experts_act():
            with act.Fori(0, PAIRS) as p:
                act.wait_ge(xsT_full, 2 * p + 1)
                v = psum[:, GATHER[0], :].rearrange("p (k c) -> p k c", k=4)
                for k in range(4):
                    ins = act.activation(xsT[:, k, :], v[:, k, :], ACT.Identity, scale=gain["norm_ffn_g"][:, k:k + 1])
                ins.then_inc(xsT_sb[0], 1)
                for e in range(2):
                    gu_done(act, p, e)
                    for b in range(2):
                        act.activation(silu_g[:, b, :], psum[:, b, :], ACT.Silu).then_inc(silu_ready, 1)
                    act.wait_ge(hidT_full, 4 * p + 2 * e + 1)
                    act.activation(hidT[0].rearrange("p j h c -> p (j h c)"), psum[:, TURN[0], :],
                                   ACT.Identity).then_inc(hidT_sb[0], 1)
                    y_done(act, p, e)
                    for n in range(2):
                        act.activation(ypair[e * 64:(e + 1) * 64, n * BANK:(n + 1) * BANK], psum[n * 64:(n + 1) * 64, 6, :],
                                       ACT.Identity).then_inc(y_sb, 1)

        def experts_dve():
            link(dve.memset(stat[:, 0:1], 0.0))
            dve.memset(stat[:, 1:2], 0.0).then_inc(added, 1)
            iota = const[:, C_IOTA:C_IOTA + CAP]
            with dve.Fori(0, PAIRS) as p:
                dve.tensor_copy(posc, slot_of[:, :, bass.ds(2 * p, 2)]).then_inc(posc_ready, 1)
                dve.tensor_copy(gatec, aff[:, :, bass.ds(2 * p, 2)]).then_inc(posc_ready, 1)
                dve.wait_ge(posc_ready, 2 * p + 2)
                for t in range(T):
                    for e in range(2):
                        o = slice(e * CAP, (e + 1) * CAP)
                        dve.tensor_scalar(selg[:, t, o], iota, posc[:, t, e:e + 1], gatec[:, t, e:e + 1],
                                          ALU.is_equal, ALU.mult)
                        ins = dve.tensor_scalar(sel[:, t, o], iota, posc[:, t, e:e + 1], None, ALU.is_equal)
                ins.then_inc(sel_ready, 1)
                dve.wait_ge(xsT_full, 2 * p + 2)
                v = psum[:, GATHER[1], :].rearrange("p (k c) -> p k c", k=4)
                for k in range(4):
                    ins = dve.tensor_scalar(xsT[:, 4 + k, :], v[:, k, :], gain["norm_ffn_g"][:, 4 + k:5 + k], None, ALU.mult)
                ins.then_inc(xsT_sb[1], 1)
                dve.wait_ge(selgT_full, p + 1)
                dve.tensor_copy(selgT, psum[:, 7, :]).then_inc(selgT_sb, 1)
                for e in range(2):
                    for b in range(2):
                        dve.wait_ge(silu_ready, 4 * p + 2 * e + b + 1)
                        dve.tensor_tensor(hid[:, b, :], psum[:, 2 + b, :], silu_g[:, b, :], ALU.mult).then_inc(hid_ready, 1)
                    dve.wait_ge(hidT_full, 4 * p + 2 * e + 2)
                    dve.tensor_copy(hidT[1].rearrange("p j h c -> p (j h c)"), psum[:, TURN[1], :]).then_inc(hidT_sb[1], 1)
                for i, bank in enumerate(ADD_BANKS):
                    t, n = i // 2, i % 2
                    o = x_sb[:, t, n * BANK:(n + 1) * BANK]
                    dve.wait_ge(added_full, 2 * T * p + i + 1)
                    dve.tensor_tensor(o, psum[:, bank, :], o, ALU.add).then_inc(added, 1)

        w2 = a["w_in_2"][0]
        blocks = [(w2, C2["ckv"], 160), (w2, C2["cq"], Q_LORA), (w2, C2["za"], BANK)]
        blocks += [(w2, C2[n], BANK) for n in ("kb", "qb", "zb", "vb")]
        blocks += [(w2, C2[n] + j * BANK, BANK) for j in range(2) for n in ("ga", "gb")]
        BLOCK = dict(ckv=0, cq=1, za=2, kb=3, qb=4, zb=5, vb=6, g=7)
        block_loaded = [sem("block_loaded0"), sem("block_loaded1")]

        def block_view(b):
            n = blocks[b][2]
            return blk[b % 2][:, 0:KD * n].rearrange("p (k c) -> p k c", k=KD)

        def block_lo(b):
            n = blocks[b][2]
            return blk_lo[b % 2][:, 0:KD * n].rearrange("p (k c) -> p k c", k=KD)

        parts = [(BLOCK["ckv"], 0, 160, 0), (BLOCK["cq"], 0, Q_LORA, 256)]
        parts += [(BLOCK[n], c * P, P, c * P) for n in ("za", "kb", "qb", "zb", "vb") for c in range(4)]
        parts += [(BLOCK["g"] + 2 * (j // 4) + i, (j % 4) * P, P, (2 * (j % 2) + i) * P) for j in range(KD) for i in range(2)]
        PART = dict(ckv=0, cq=1, za=2, kb=6, qb=10, zb=14, vb=18, g=22)
        w_rounded, w_split = sem("w_rounded"), sem("w_split")

        def round_part(i, used=None):
            b, c, n, o = parts[i]
            act.wait_ge(block_loaded[b % 2], 16 * (b // 2 + 1))
            if used is not None:
                B.full(act, used)
            act.activation(w_hi[:, :, o:o + n], block_view(b)[:, :, c:c + n], ACT.Identity).then_inc(w_rounded, 1)

        def rest_of_parts(lo, hi):
            for i in range(lo, hi):
                b, c, n, o = parts[i]
                pool.wait_ge(w_rounded, i + 1)
                pool.tensor_tensor(block_lo(b)[:, :, c:c + n], block_view(b)[:, :, c:c + n],
                                   w_hi[:, :, o:o + n].bitcast(F32), ALU.subtract).then_inc(w_split, 1)

        def part(i):
            b, c, n, o = parts[i]
            pe.wait_ge(w_split, i + 1)
            return w_hi[:, :, o:o + n], block_lo(b)[:, :, c:c + n]

        def three_passes(g, o, w, x, weights_move=False):
            pairs = []
            for k in range(KD):
                (wh, wl), (xh, xl) = ([half[:, k, :] for half in v] for v in (w, x))
                for a_, b_ in ((wh, xh), (wh, xl), (wl, xh)):
                    pairs.append((b_, a_) if weights_move else (a_, b_))
            B.filled(product(g, o, pairs), g)

        last_of_block = {}

        def load_blocks(lo, hi):
            for b in range(lo, hi):
                src, c0, n = blocks[b]
                if b >= 2:
                    B.full(sp, last_of_block[b - 2])
                sp.dma_start(block_view(b), src[:, c0:c0 + n].rearrange("(k p) c -> p k c", p=P)).then_inc(block_loaded[b % 2], 16)

        hn_x2 = sem("hn_x2")
        g_x2 = B.take(2 * T)
        sums2, means2, roots2, recips2 = (stat[:, 32 + 8 * i:40 + 8 * i] for i in range(4))

        def two_norms_act():
            for t in range(T):
                act.wait_ge(added, 2 * T * (PAIRS - 1) + 2 * t + 3)
                act.activation(square_junk, x_sb[:, t, :], ACT.Square, accum_out=sums2[:, t:t + 1]).then_inc(sem("x_squared"), 1)
                act.wait_ge(sem("x_squared"), t + 1)
            for t in range(2):
                act.wait_ge(sem("xg"), t + 1)
                act.activation(square_junk, hn[:, t, :], ACT.Square, accum_out=sums2[:, T + t:T + t + 1]).then_inc(sem("x_squared"), 1)
                act.wait_ge(sem("x_squared"), T + t + 1)
            act.wait_ge(sem("x_means"), 1)
            act.activation(roots2, means2, ACT.Sqrt).then_inc(sem("x_roots"), 1)

        def two_norms_pool():
            pool.wait_ge(sem("g_row_in"), 16)
            for t in range(2):
                pool.wait_ge(added, 2 * T * (PAIRS - 1) + 2 * t + 3)
                pool.tensor_tensor(hn[:, t, :], x_sb[:, t, :], g_row, ALU.mult).then_inc(sem("xg"), 1)

        def two_norms_dve():
            dve.wait_ge(sem("g_row_in"), 16)
            dve.wait_ge(added, 2 * T * PAIRS + 1)
            for t in range(2, T):
                link(dve.tensor_tensor(hn[:, t, :], x_sb[:, t, :], g_row, ALU.mult))
                link(dve.tensor_tensor_reduce(out=dve_junk, in0=hn[:, t, :], in1=hn[:, t, :], scale=1.0, scalar=0.0,
                                              op0=ALU.mult, op1=ALU.add, accum_out=sums2[:, T + t:T + t + 1]))
            dve.wait_ge(sem("x_squared"), T + 2)
            link(dve.tensor_scalar(means2[:, 0:T], sums2[:, 0:T], 1.0 / D, EPS, ALU.mult, ALU.add))
            link(dve.reciprocal(recips2[:, 0:T], means2[:, 0:T]))
            link(dve.tensor_tensor(means2[:, T:], sums2[:, T:], recips2[:, 0:T], ALU.mult))
            dve.tensor_scalar(means2[:, T:], means2[:, T:], 1.0 / D, EPS, ALU.mult, ALU.add).then_inc(sem("x_means"), 1)
            dve.wait_ge(sem("x_roots"), 1)
            link(dve.reciprocal(recips2, roots2))
            for t in range(T):
                dve.tensor_scalar(hn[:, t, :], hn[:, t, :], recips2[:, t:t + 1], recips2[:, T + t:T + t + 1],
                                  ALU.mult, ALU.mult).then_inc(hn_x2, 1)

        def x_mid_dve():
            for t in range(T):
                dve.scalar_tensor_tensor(out=x_sb[:, t, :], in0=x_sb[:, t, :], scalar=recips2[:, t:t + 1], in1=g_row,
                                         op0=ALU.mult, op1=ALU.mult).then_inc(sem("x_mid"), 1)

        def turn2_pe():
            turn_tiles(g_x2, hn, hn_x2)

        h2_rounded, h2_split = sem("h2_rounded"), sem("h2_split")

        def ctx_split(eng):
            if eng is act:
                act.activation(hc_hi[:], hcT, ACT.Identity).then_inc(sem("hc_rounded"), 1)
            else:
                eng.wait_ge(sem("hc_rounded"), 1)
                eng.tensor_tensor(hc_lo[:], hcT, hc_hi[:].bitcast(F32), ALU.subtract).then_inc(sem("hc_split"), 1)

        def x2_split(eng):
            tile = lambda v, t: v[:, :, t * P:(t + 1) * P]
            for t in range(T + 1):
                if t < T:
                    drain_tiles(eng, g_x2[2 * t:2 * t + 2], tile(h2T, t), mod[:, KD:, 0], mod[:, 0:KD, 0])
                    if eng is act:
                        for g in g_x2[2 * t:2 * t + 2]:
                            B.drained(act, g)
                        act.activation(tile(h2_hi, t), tile(h2T, t), ACT.Identity).then_inc(h2_rounded, 1)
                if eng is dve and t >= 1:
                    dve.wait_ge(h2_rounded, t)
                    dve.tensor_tensor(tile(h2_lo, t - 1), tile(h2T, t - 1), tile(h2_hi, t - 1).bitcast(F32),
                                      ALU.subtract).then_inc(h2_split, 1)

        h2 = (h2_hi, h2_lo)

        def tokens(t):
            halves, t = (h2, t) if t < T else ((hc_hi, hc_lo), t - T)
            return [v[:, :, t * P:(t + 1) * P] for v in halves]

        g_ckv = B.take(KT2)
        g_cq = B.take(T)
        g_za = B.take(4)
        last_of_block.update({BLOCK["ckv"]: g_ckv[-1], BLOCK["cq"]: g_cq[-1], BLOCK["za"]: g_za[-1]})

        def mla_in_pe():
            for i, (name, groups, n) in enumerate((("ckv", g_ckv, 160), ("cq", g_cq, Q_LORA))):
                w = part(PART[name])
                for t, g in enumerate(groups):
                    pe.wait_ge(*((h2_split, t + 1) if t < T else (sem("hc_split"), 1)))
                    B.acquire(pe, g)
                    three_passes(g, B.at(g)[:, 0:n], w, tokens(t), weights_move=True)
            channels_pe("za", g_za)

        def channels_pe(name, groups):
            for c, g in enumerate(groups):
                w = part(PART[name] + c)
                B.acquire(pe, g)
                three_passes(g, B.at(g), w, h2)

        norm_kv_act, norm_kv_dve = rms_rows(ckv[:, :, 0:KV_LORA], ckv[:, :, 0:KV_LORA], KT2, KV_LORA, sem("ckv_n"))
        norm_q_act, norm_q_dve = rms_rows(cq, cq, T, Q_LORA, sem("cq_n"))

        def mla_in_act():
            for t, g in enumerate(g_ckv):
                B.full(act, g)
                B.release(copy(act, ckv[:, t, :], B.at(g)[:, 0:160]), g)
            for c in range(2):
                round_part(PART["za"] + c, g_ckv[-1])
            for g in g_ckv:
                B.drained(act, g)
            norm_kv_act(junk=cut(hn_flat, 1024, KT2, KV_LORA))
            for t, g in enumerate(g_cq):
                B.full(act, g)
                B.release(copy(act, cq[:, t, :], B.at(g)[:, 0:Q_LORA]), g)
            for c in range(2, 4):
                round_part(PART["za"] + c, g_cq[-1])
            for g in g_cq:
                B.drained(act, g)
            norm_q_act(junk=cut(hn_flat, 2048, T, Q_LORA))
            for c, g in enumerate(g_za):
                B.full(act, g)
                B.release(act.activation(oaT[:, c, :], B.at(g), ACT.Silu), g)

        def rotate_halves(v, cos, sin, done=None):
            x1, x2 = v[:, :, :, 0, :], v[:, :, :, 1, :]
            n = v.shape[1]
            t0, t1 = (r[:, 0:n] for r in rope2_t)
            link(dve.tensor_tensor(t0, x1, sin, ALU.mult))
            link(dve.tensor_tensor(t1, x2, sin, ALU.mult))
            link(dve.tensor_tensor(x1, x1, cos, ALU.mult))
            link(dve.tensor_tensor(x2, x2, cos, ALU.mult))
            link(dve.tensor_tensor(x1, x1, t1, ALU.subtract))
            return dve.tensor_tensor(x2, x2, t0, ALU.add)

        cos2, sin2 = (const[:, c:c + 64].rearrange("p (t a f) -> p t a f", t=T, a=2) for c in (C_COS2, C_SIN2))

        def mla_in_dve():
            norm_kv_dve()
            kr = ckv[:, 0:T, KV_LORA:].rearrange("p t (a x f) -> p t a x f", a=2, x=2)
            rotate_halves(kr, cos2, sin2).then_inc(sem("kr"), 1)
            norm_q_dve()

        g_ckvT = B.take(2)
        g_krT = B.take(2)
        g_cqT = B.take(2)
        g_q = B.take(2 * T)
        g_kn = B.take(2 * MLA_H)
        g_va = B.take(KT2)
        g_qT2 = B.take(MLA_H)
        KEY_SEGS = ((0, S), (S, NTOK))

        def mla_up_pe():
            pe.wait_ge(sem("ckv_n"), KT2)
            pe.wait_ge(sem("kr"), 1)
            for groups, c0, n in ((g_ckvT, 0, KV_LORA), (g_krT, KV_LORA, ROPE)):
                for i, g in enumerate(groups):
                    B.acquire(pe, g)
                    for t in range(T * i, min(T * i + T, KT2)):
                        ins = pe.transpose(B.at(g)[0:n, (t % T) * P:(t % T + 1) * P], ckv[:, t, c0:c0 + n], ident)
                    B.filled(ins, g)
            pe.wait_ge(sem("cq_n"), T)
            for c, g in enumerate(g_cqT):
                B.acquire(pe, g)
                for t in range(T):
                    ins = pe.transpose(B.at(g)[:, t * P:(t + 1) * P], cq[:, t, c * P:(c + 1) * P], ident)
                B.filled(ins, g)
            pe.wait_ge(sem("uq_in"), 16)
            pe.wait_ge(sem("ukv_in"), 16)
            for g in (*g_ckvT, *g_cqT):
                B.drained(pe, g)
            for i, g in enumerate(g_q):
                t, n = i // 2, i % 2
                B.acquire(pe, g)
                B.filled(product(g, B.at(g)[:, 0:384], [(cqT[:, c, t * P:(t + 1) * P], uq[:, c, n * 384:(n + 1) * 384])
                                                       for c in range(2)]), g)
            for i, g in enumerate(g_kn):
                h, (lo, hi) = i // 2, KEY_SEGS[i % 2]
                B.acquire(pe, g)
                B.filled(product(g, B.at(g)[0:NOPE, 0:hi - lo], [(ukv[:, h, 0:NOPE], ckvT[:, lo:hi])]), g)
            for t, g in enumerate(g_va):
                B.acquire(pe, g)
                B.filled(product(g, B.at(g).rearrange("p (h d) -> p h d", h=MLA_H),
                                 [(ckvT[:, t * P:(t + 1) * P], ukv[:, :, NOPE:])]), g)
            pe.wait_ge(sem("q_rot"), T)
            for h, g in enumerate(g_qT2):
                B.acquire(pe, g)
                for t in range(T):
                    ins = pe.transpose(B.at(g)[0:QK_MLA, t * P:(t + 1) * P], q_tok[:, t, h, :], ident)
                B.filled(ins, g)

        def mla_up_act():
            for g, (lo, hi) in zip(g_ckvT, KEY_SEGS):
                B.full(act, g)
                B.release(copy(act, ckvT[:, lo:hi], B.at(g)[:, 0:hi - lo], g_ckv_col), g)
            for c, g in enumerate(g_cqT):
                B.full(act, g)
                B.release(copy(act, cqT[:, c, :], B.at(g), g_cq_col[:, c:c + 1]), g)
            for i, g in enumerate(g_q):
                t, n = i // 2, i % 2
                B.full(act, g)
                B.release(copy(act, q_tok[:, t, 4 * n:4 * n + 4, :], B.at(g)[:, 0:384].rearrange("p (h c) -> p h c", h=4),
                               QK_MLA ** -0.5), g)
            for i, g in enumerate(g_kn):
                h, (lo, hi) = i // 2, KEY_SEGS[i % 2]
                B.full(act, g)
                B.release(copy(act, kT_mla[0:NOPE, h, lo:hi], B.at(g)[0:NOPE, 0:hi - lo]), g)
            for h, g in enumerate(g_qT2):
                if h % 2 == 0:
                    B.full(act, g)
                    B.release(copy(act, qT_mla[:, h, :], B.at(g)[0:QK_MLA, :]), g)

        def mla_up_dve():
            for g, (lo, hi) in zip(g_krT, KEY_SEGS):
                B.full(dve, g)
                B.release(dve.tensor_copy(kT_mla[NOPE:QK_MLA, :, lo:hi],
                                          B.at(g)[0:ROPE, 0:hi - lo].unsqueeze(1).to_broadcast([ROPE, MLA_H, hi - lo])), g)
            for t in range(T):
                for g in g_q[2 * t:2 * t + 2]:
                    B.drained(dve, g)
                v = q_tok[:, t, :, NOPE:].rearrange("p h (a x f) -> p h a x f", a=2, x=2)
                c, s = (r[:, t].unsqueeze(1).to_broadcast([P, MLA_H, 2, 8]) for r in (cos2, sin2))
                rotate_halves(v, c, s).then_inc(sem("q_rot"), 1)
                dve.wait_ge(sem("q_rot"), t + 1)
            for t, g in enumerate(g_va):
                B.full(dve, g)
                B.release(dve.tensor_copy(va[:, t, :], B.at(g)), g)
            for h, g in enumerate(g_qT2):
                if h % 2 == 1:
                    B.full(dve, g)
                    B.release(dve.tensor_copy(qT_mla[:, h, :], B.at(g)[0:QK_MLA, :]), g)

        def mla_ready_pe():
            for g in (*g_krT, *g_kn, *g_va, *g_qT2, *g_za):
                B.drained(pe, g)

        SEG2 = [S, CTX]
        seg2 = lambda si: slice(*KEY_SEGS[si])
        pairs2 = [(2 * i, 2 * i + 1) for i in range(4)]
        mla_pe, mla_act, mla_dve, g_mla_end = attention(
            "mla", pairs2, SEG2, lambda h, qt: qT_mla[:, h, qt * P:(qt + 1) * P], lambda h, si: kT_mla[:, h, seg2(si)],
            lambda h, kt: va[:, kt, h * HD:(h + 1) * HD], HD, p_mla, pt_mla,
            lambda i, o: dve.tensor_tensor(oaT[:, i, :], o, oaT[:, i, :], ALU.mult), [])

        g_kb = B.take(4 + 4)
        g_qb = B.take(4)
        g_zb = B.take(4)
        g_vb = B.take(KT2)
        last_of_block.update({BLOCK["kb"]: g_kb[-1], BLOCK["vb"]: g_vb[-1], BLOCK["qb"]: g_qb[-1], BLOCK["zb"]: g_zb[-1]})

        def na_in_pe():
            for c in range(4):
                w = part(PART["kb"] + c)
                for g, x in zip(g_kb[2 * c:2 * c + 2], (h2, (hc_hi, hc_lo))):
                    B.acquire(pe, g)
                    three_passes(g, B.at(g)[:, 0:x[0].shape[2]], w, x)
            channels_pe("qb", g_qb)
            channels_pe("zb", g_zb)
            for c in range(4):
                part(PART["vb"] + c)
            for t, g in enumerate(g_vb):
                B.acquire(pe, g)
                three_passes(g, B.at(g), (w_hi, block_lo(BLOCK["vb"])), tokens(t), weights_move=True)

        def na_in_drain(eng):
            if eng is act:
                for c in range(4):
                    round_part(PART["kb"] + c, g_mla_end)
            for c in range(4):
                for g, (lo, hi) in zip(g_kb[2 * c:2 * c + 2], KEY_SEGS):
                    drain(eng, g, kbT[:, c, lo:hi], B.at(g)[:, 0:hi - lo])
                if eng is act:
                    round_part(PART["qb"] + c, g_kb[2 * c + 1])
            for c, g in enumerate(g_qb):
                drain(eng, g, qbT[:, c, :], B.at(g), HD ** -0.5)
                if eng is act:
                    round_part(PART["zb"] + c, g)
            if eng is act:
                for c, g in enumerate(g_zb):
                    B.full(act, g)
                    B.release(act.activation(obT[:, c, :], B.at(g), ACT.Silu), g)
                    round_part(PART["vb"] + c, g)
            for t, g in enumerate(g_vb):
                drain(eng, g, vb[:, t, :], B.at(g))

        def na_ready_pe():
            for g in (*g_kb, *g_vb, *g_qb, *g_zb):
                B.drained(pe, g)

        odd = lambda h: slice((h % 2) * HD, (h % 2 + 1) * HD)

        def na_bias(h, qt):
            o = 6 - 2 * qt
            return na_table[:, h, o * GRID_W:(o + GRID_H) * GRID_W]

        na_pe, na_act, na_dve, g_na_end = attention(
            "na", pairs2, SEG2, lambda h, qt: qbT[odd(h), h // 2, qt * P:(qt + 1) * P],
            lambda h, si: kbT[odd(h), h // 2, seg2(si)], lambda h, kt: vb[:, kt, h * HD:(h + 1) * HD], HD, p_na, pt_na,
            lambda i, o: dve.tensor_tensor(obT[:, i, :], o, obT[:, i, :], ALU.mult), [], bias=na_bias)

        g_y = [B.take(4) for _ in range(KD)]
        last_of_block.update({BLOCK["g"] + 2 * n + i: g_y[4 * n + 3][i] for n in range(2) for i in range(2)})
        g_out3 = B.take(2 * T)

        def y_pe():
            B.drained(pe, g_na_end)
            B.drained(pe, g_mla_end)
            for j in range(KD):
                gs = g_y[j]
                for i in range(2):
                    w = part(PART["g"] + 2 * j + i)
                    B.acquire(pe, gs[i])
                    three_passes(gs[i], B.at(gs[i]), w, h2)
                if j == 0:
                    pe.wait_ge(sem("woa_in"), 16)
                    pe.wait_ge(sem("wob_in"), 16)
                for i, (w, o) in enumerate(((woa, oaT), (wob, obT))):
                    g = gs[2 + i]
                    B.acquire(pe, g)
                    B.filled(product(g, B.at(g), [(w[:, k, j * P:(j + 1) * P], o[:, k, :]) for k in range(4)]), g)
            pe.wait_ge(sem("w_out2_in"), 16 * 4)
            pe.wait_ge(sem("yT"), KD)
            add_product_pe(g_out3, lambda k: yT[:, k, :], lambda k: w_out2[k], KD)

        def y_act():
            for j in range(2):
                for i in range(2):
                    round_part(PART["g"] + 2 * j + i, g_na_end)
            for j in range(KD):
                for i in range(2):
                    if j >= 2:
                        act.wait_ge(sem("yT"), j - 1)
                    B.full(act, g_y[j][i])
                    B.release(act.activation(sg[2 * (j % 2) + i], B.at(g_y[j][i]), ACT.Sigmoid), g_y[j][i])
                    if j + 2 < KD:
                        round_part(PART["g"] + 2 * (j + 2) + i, g_y[j][i])

        def y_dve():
            for j in range(KD):
                for i in range(2):
                    B.drained(dve, g_y[j][i])
                    g = g_y[j][2 + i]
                    B.full(dve, g)
                    B.release(dve.tensor_tensor(sg[2 * (j % 2) + i], B.at(g), sg[2 * (j % 2) + i], ALU.mult), g)
                    B.drained(dve, g)
                dve.tensor_tensor(yT[:, j, :], sg[2 * (j % 2)], sg[2 * (j % 2) + 1], ALU.add).then_inc(sem("yT"), 1)
            for i, g in enumerate(g_out3):
                t, n = i // 2, i % 2
                c = slice(n * BANK, (n + 1) * BANK)
                B.full(dve, g)
                if i >= 2:
                    dve.wait_ge(sem("x_last"), i - 1)
                B.release(dve.tensor_tensor(ysum[i % 2], B.at(g), gate_row[:, c], ALU.mult), g)
                B.drained(dve, g)
                dve.tensor_tensor(x_sb[:, t, c], ysum[i % 2], x_sb[:, t, c], ALU.add).then_inc(sem("x_last"), 1)
                if n == 1:
                    last_norm_dve(t)

        last_stat = stat[:, 0:2 * T].rearrange("p (t i) -> p t i", i=2)

        def last_norm_act():
            for t in range(T):
                act.wait_ge(sem("x_last"), 2 * t + 2)
                act.activation(hn[:, t, :], x_sb[:, t, :], ACT.Square, accum_out=last_stat[:, t, 0:1]).then_inc(sem("last_squared"), 1)
                act.wait_ge(sem("last_mean"), t + 1)
                act.activation(last_stat[:, t, 0:1], last_stat[:, t, 1:2], ACT.Sqrt).then_inc(sem("last_root"), 1)

        def last_norm_dve(t):
            if t == 0:
                dve.wait_ge(sem("g_fin_in"), 16)
            dve.wait_ge(sem("last_squared"), t + 1)
            dve.tensor_scalar(last_stat[:, t, 1:2], last_stat[:, t, 0:1], 1.0 / D, EPS, ALU.mult, ALU.add).then_inc(sem("last_mean"), 1)
            dve.wait_ge(sem("last_root"), t + 1)
            link(dve.reciprocal(last_stat[:, t, 1:2], last_stat[:, t, 0:1]))
            dve.scalar_tensor_tensor(out=x_sb[:, t, :], in0=x_sb[:, t, :], scalar=last_stat[:, t, 1:2], in1=g_fin,
                                     op0=ALU.mult, op1=ALU.mult).then_inc(sem("result"), 1)

        def row_of(v, n):
            return v.unsqueeze(0).to_broadcast([P, n]) if len(v.shape) == 1 else v.to_broadcast([P, n])

        w_in_loaded = [sem(f"w_in_loaded{i}") for i in range(4)]
        w_mod_loaded = [sem(f"w_mod_loaded{i}") for i in range(4)]
        w_modg_loaded = [sem(f"w_modg_loaded{i}") for i in range(2)]

        def first_loads():
            sp.dma_start(const[:], a["shape_const"]).then_inc(sem("const_in"), 16)
            sp.dma_start(mem, a["mem"][0].rearrange("(t p) d -> p t d", p=P)).then_inc(sem("mem_in"), 16)
            for dst, src in row_loads:
                sp.dma_start(dst, src).then_inc(sem("rows_in"), 16)
            sp.dma_start(x_sb, a["x"][0].rearrange("(t p) d -> p t d", p=P)).then_inc(sem("x_in"), 16)
            sp.dma_start(ca_wkv, a["ca_wkv"][0].rearrange("(k p) c -> p k c", p=P)).then_inc(sem("ca_wkv_in"), 16)
            w = a["w_in"][0].rearrange("(k p) c -> p k c", p=P)
            for i in (0, 1, 3, 2):
                o = 0
                for lo, hi in W_IN_COLS[i]:
                    sp.dma_start(w_in[i][:, :, o:o + hi - lo], w[:, :, lo:hi]).then_inc(w_in_loaded[i], 16)
                    o += hi - lo
                if i == 1:
                    sp.dma_start(w_gate, w[:, :, GATE0:GATE1]).then_inc(sem("w_gate_in"), 16)
            B.full(sp, g_vca[-1])
            sp.dma_start(pool_w, a["pool_w"][0].rearrange("(c g) i e -> (g i) c e", c=2)).then_inc(sem("pool_w_in"), 16)
            sp.dma_start(ml_g, row_of(a["mlstm_norm_g"], ML_H * HD)).then_inc(sem("head_rows_in"), 16)
            sp.dma_start(qg, row_of(a["q_norm_g"], HD)).then_inc(sem("head_rows_in"), 16)
            sp.dma_start(kg, row_of(a["k_norm_g"], HD)).then_inc(sem("head_rows_in"), 16)
            sp.dma_start(router_w, a["router_w"][0].rearrange("(k p) e -> p k e", p=P)).then_inc(sem("router_in"), 16)
            w = a["w_mod_2"][0].rearrange("(k p) c -> p k c", p=P)
            for i, g in enumerate((g_chan[3], g_aq[-1], g_akv[-1], g_vo[-1])):
                if i == 1:
                    B.full(sp, g_gate[0])
                    sp.dma_start(inv_n, a["shape_inv"].rearrange("p (c s) -> p c s", c=2)).then_inc(sem("inv_n_in"), 16)
                    sp.wait_ge(rows_b, 1)
                    for j in range(2):
                        sp.dma_start(gate_lin[j], a["b_mod_2"][:, 2 * D + j * BANK:2 * D + (j + 1) * BANK]).then_inc(sem("gate_lin_in"), 16)
                B.full(sp, g)
                sp.dma_start(w_mod[i], w[:, 2 * i:2 * i + 2, 0:2 * D]).then_inc(w_mod_loaded[i], 16)
            B.full(sp, g_mod[0])
            for i in range(2):
                sp.dma_start(w_modg[i], w[:, 4 * i:4 * i + 4, 2 * D:]).then_inc(w_modg_loaded[i], 16)
            w = a["w_out"][0]
            sp.dma_start(w_out[:, 0:4, :], w[0:512].rearrange("(k p) c -> p k c", p=P)).then_inc(sem("w_out_in"), 16)
            for h in range(2):
                sp.dma_start(w_out[h * HD:(h + 1) * HD, 4:8, :],
                             w[512 + h * 256:768 + h * 256].rearrange("(k p) c -> p k c", p=HD)).then_inc(sem("w_out_in"), 16)
            B.full(sp, g_gate2[0])
            sp.dma_start(ca_wq, a["ca_wq"][0].rearrange("(k p) c -> p k c", p=P)).then_inc(sem("ca_wq_in"), 16)
            sp.dma_start(ca_wo, a["ca_wo"][0].rearrange("(k p) c -> p k c", p=P)).then_inc(sem("ca_wo_in"), 16)

        row_loads = [(rows[lo:hi, :], a[name].rearrange("(k p) -> k p", p=P) if len(a[name].shape) == 1 else
                      a[name][0].rearrange("w (c p) -> (w c) p", p=P) if len(a[name].shape) == 3 else
                      a[name][:, 0:(hi - lo) * P].rearrange("o (k p) -> (o k) p", p=P)) for name, (lo, hi) in ROWS.items()]
        row_loads.append((gate_b_rows, a["mlstm_gate_b"].rearrange("o (k p) -> (o k) p", k=2)))
        N_ROW_LOADS = len(row_loads)

        ctx.enter_context(nc.allow_non_contiguous_dma(reason="windows of 16 biases, and a few columns of weights"))

        def na_table_build():
            pool.wait_ge(sem("fill"), 1)
            flat = na_dram.rearrange("a w c -> (a w c)").rearrange("(p r f) -> p r f", p=P, f=240)
            pool.dma_start(flat, fill[:].unsqueeze(1).to_broadcast([P, 16, 240])).then_inc(sem("na_filled"), 16)
            pool.wait_ge(sem("na_filled"), 16)
            rpb = a["rpb_2"][0].rearrange("h r c -> (h r) c")
            mid = GRID_W - NA_KC + NA_KC // 2
            n_hr = NA_H * (2 * NA_KR - 1)
            cell, row = GRID_W, 2 * NA_KC - 1
            pool.dma_start(bass.AP(na_dram.tensor, 8 * cell, [[cell * cell, n_hr], [cell + 1, mid - 7], [1, NA_KC]]),
                           bass.AP(rpb.tensor, 7, [[row, n_hr], [0, mid - 7], [1, NA_KC]])).then_inc(sem("na_cells"), 16)
            for w in (*range(8), *range(mid + 1, GRID_W)):
                start = min(max(w - NA_KC // 2, 0), GRID_W - NA_KC)
                pool.dma_start(na_dram[:, w, start:start + NA_KC],
                               rpb[:, start - w + NA_KC - 1:start - w + 2 * NA_KC - 1]).then_inc(sem("na_cells"), 16)

        N_CELLS = 1 + 8 + 7

        def second_loads():
            for s in (0, 1):
                sp.wait_ge(slot_free[s], 3 * PAIRS)
                load_blocks(s, s + 1)
            sp.wait_ge(slot_free[6], 3 * PAIRS)
            sp.dma_start(g_row, row_of(a["final_norm_g"], D)).then_inc(sem("g_row_in"), 16)
            sp.wait_ge(added, 2 * T * PAIRS + 1)
            sp.dma_start(uq, a["w_uq_2"][0].rearrange("(k p) c -> p k c", p=P)).then_inc(sem("uq_in"), 16)
            sp.dma_start(ukv, a["w_ukv_2"][0].rearrange("p (h c) -> p h c", h=MLA_H)).then_inc(sem("ukv_in"), 16)
            load_blocks(2, 5)
            B.full(sp, g_mla_end)
            sp.wait_ge(sem("na_cells"), 16 * N_CELLS)
            v = na_dram.rearrange("(h r) w c -> w h r c", h=NA_H)
            for i in range(2):
                for h in range(NA_H):
                    sp.dma_start(na_table[i * 64:(i + 1) * 64, h, :].rearrange("p (r c) -> p r c", r=14),
                                 v[:, h, 1 - i:15 - i, :]).then_inc(sem("na_table_in"), 16)
            load_blocks(5, 9)
            B.full(sp, g_na_end)
            sp.dma_start(woa, a["w_oa_2"][0].rearrange("(k p) c -> p k c", p=P)).then_inc(sem("woa_in"), 16)
            sp.dma_start(wob, a["w_ob_2"][0].rearrange("(k p) c -> p k c", p=P)).then_inc(sem("wob_in"), 16)
            w = a["w_out_2"][0].rearrange("(k p) c -> p k c", p=P)
            sp.dma_start(w_out2_a, w[:, 0:2, :]).then_inc(sem("w_out2_in"), 16)
            sp.dma_start(w_out2_b, w[:, 2, :]).then_inc(sem("w_out2_in"), 16)
            sp.dma_start(g_fin, row_of(a["final_g_2"], D)).then_inc(sem("g_fin_in"), 16)
            load_blocks(9, 11)
            B.full(sp, g_y[KD - 1][0])
            sp.dma_start(slot(1)[:, 0:D], w[:, 7, :]).then_inc(sem("w_out2_in"), 16)
            B.full(sp, g_y[KD - 1][1])
            sp.dma_start(slot(0).rearrange("p (k c) -> p k c", k=4), w[:, 3:7, :]).then_inc(sem("w_out2_in"), 16)

        block = ctx.enter_context(nc.Block())

        @block.sync
        def _(_):
            first_loads()
            experts_sp()
            second_loads()
            for t in range(T):
                sp.wait_ge(sem("result"), t + 1)
                sp.dma_start(out[0, t * P:(t + 1) * P, :], x_sb[:, t, :]).then_inc(sem("stored"), 16)
            sp.wait_ge(sem("stored"), 16 * T)

        @block.gpsimd
        def _(_):
            pool.memset(fill[:], NEG).then_inc(sem("fill"), 1)
            B.full(pool, g_vca[-1])
            pool.memset(upad, 0.0).then_inc(sem("pads"), 1)
            pool.memset(qkpad, 0.0).then_inc(sem("pads"), 1)
            pool.memset(v_aug[:, :, :, HD:], 1.0).then_inc(sem("pads"), 1)
            pool.memset(c_pad, 0.0).then_inc(sem("pads"), 1)
            mlstm_pool()
            na_table_build()
            rest_of_parts(0, 2)
            two_norms_pool()
            ctx_split(pool)
            rest_of_parts(2, len(parts))

        @block.tensor
        def _(_):
            first_turns_pe()
            memory_pe()
            project_pe()
            gates_pe()
            project_tokens_pe(g_vo, 2, 0, 512)
            pool_pe()
            mlstm_pe()
            heads_pe()
            gate2_pe()
            heads_ready_pe()
            attn_pe()
            mlstm_out_pe()
            out1_pe()
            turn_tiles(g_h2, hn_ca, hn_mem)
            qca_pe()
            ca_all_pe()
            turn_tiles(g_h3, hn, hn_ffn)
            route_pe()
            experts_pe()
            turn2_pe()
            mla_in_pe()
            mla_up_pe()
            mla_ready_pe()
            mla_pe()
            na_in_pe()
            na_ready_pe()
            na_pe()
            y_pe()

        @block.scalar
        def _(_):
            drain_rows(act, g_memT, 2, memT)
            columns_act()
            norm1_act()
            drain_tiles(act, g_h1, hT, gain["norm_mix_g"])
            memory_drain(act)
            project_act()
            gate_columns_act()
            conv_act()
            silu_c_act()
            heads_act()
            project_vo_act()
            pool_act()
            mlstm_act()
            heads_drain(act)
            mlstm_norm_act()
            gate_row_act()
            attn_act()
            mlstm_out_drain(act)
            norm2_act()
            drain_tiles(act, g_h2, hT, gain["norm_mem_g"])
            qca_drain(act)
            ca_act()
            norm3_act()
            drain_tiles(act, g_h3, hT, gain["norm_ffn_g"])
            ctx_norm_act()
            route_act()
            ctx_drain_act()
            experts_act()
            round_part(PART["ckv"])
            round_part(PART["cq"])
            two_norms_act()
            x2_split(act)
            ctx_split(act)
            mla_in_act()
            mla_up_act()
            mla_act()
            na_in_drain(act)
            na_act()
            y_act()
            last_norm_act()

        @block.vector
        def _(_):
            drain_rows(dve, g_memT, 2, memT)
            norm1_dve()
            B.drained(dve, g_columns[0])
            drain_tiles(dve, g_h1, hT, gain["norm_mix_g"])
            memory_drain(dve)
            gates_dve()
            conv_dve()
            pool_dve()
            heads_dve()
            mlstm_dve()
            heads_drain(dve)
            gate2_dve()
            mlstm_norm_dve()
            attn_dve()
            mlstm_out_drain(dve)
            norm2_dve()
            drain_tiles(dve, g_h2, hT, gain["norm_mem_g"])
            qca_drain(dve)
            ca_dve()
            norm3_dve()
            drain_tiles(dve, g_h3, hT, gain["norm_ffn_g"])
            normc_dve()
            route_dve()
            experts_dve()
            two_norms_dve()
            x2_split(dve)
            x_mid_dve()
            mla_in_dve()
            mla_up_dve()
            mla_dve()
            na_in_drain(dve)
            dve.wait_ge(sem("na_table_in"), 16 * 2 * NA_H)
            na_dve()
            y_dve()


_INPUTS = ["x", "mem", "norm_mix_g", "w_in", "pool_w", "pool_scale", "mlstm_conv_w", "mlstm_gate_b", "mlstm_norm_g",
           "q_norm_g", "k_norm_g", "w_out", "norm_mem_g", "ca_wq", "ca_wkv", "ca_wo", "norm_ffn_g", "router_w",
           "expert_w_gu", "expert_w_down", "final_norm_g", "c_2", "ctx_2", "c_ctx_2", "w_mod_2", "b_mod_2", "norm_g_2",
           "w_in_2", "g_cq_2", "w_uq_2", "g_ckv_2", "w_ukv_2", "rpb_2", "w_oa_2", "w_ob_2", "w_out_2", "final_g_2"]


def kernel(**inputs):
    import concourse.bacc as bacc
    from concourse.bass_utils import run_bass_kernel_spmd

    nc = bacc.Bacc("TRN2", target_bir_lowering=False, num_devices=1)
    arrays = {f"in_{n}": np.ascontiguousarray(inputs[n]) for n in _INPUTS}
    arrays["in_shape_const"], arrays["in_shape_inv"] = shape_constants()
    aps = {n[3:]: nc.dram_tensor(n, v.shape, F32, kind="ExternalInput").ap() for n, v in arrays.items()}
    out = nc.dram_tensor("out", (1, S, D), F32, kind="ExternalOutput").ap()
    build(nc, aps, out)
    return run_bass_kernel_spmd(nc, [arrays], core_ids=[0]).results[0]["out"]
```

```python
import math
from contextlib import ExitStack

import numpy as np

import concourse.bass as bass
from concourse import mybir

F32 = mybir.dt.float32
F32R = mybir.dt.float32r
ACT = mybir.ActivationFunctionType
ALU = mybir.AluOpType
AX = mybir.AxisListType.X

P = 128
D = 1024
KD = D // P
S = 512
T = S // P
N_MEM = 256
HD = 64
GRID_W = 64
GRID_H = S // GRID_W
POOL_WINDOWS = (2, 4, 8, 16)
POOL_G = 64
PADL = 8
UP = S + 2 * PADL
ML_H = 4
ML_CONV = 5
V_MOVE = 96
QKP = S + ML_CONV - 1
AT_H = 8
CA_H, CA_HD = 4, 128
N_EXP = 16
CAP = 2 * S // N_EXP
FF = 2 * D
EPS = 1e-6
CTX = 256
NTOK = S + CTX
KT2 = NTOK // P
MLA_H, NOPE, ROPE = 8, 64, 32
QK_MLA = NOPE + ROPE
Q_LORA, KV_LORA = 256, 128
NA_H, NA_KR, NA_KC = 8, 8, 16
ROPE_THETA = 10000.0
BANK = 512
NBANK = 8
SLOT = 4096
NSLOT = 8
NEG = -1e30
SMALL = 672
O_LATER = 3

GATE0, GATE1 = 1280, 1296
IN_COLS = 2064
MAIN = IN_COLS - 16
C2 = {"ckv": 0, "kb": 160, "vb": 672, "cq": 1184, "za": 1440, "qb": 1952, "zb": 2464, "ga": 2976, "gb": 4000}

C_ID, C_ONE, C_COS, C_SIN, C_IOTA, C_COS2, C_SIN2, C_END = np.cumsum([0, 128, 128, 128, 128, 64, 64, 64]).tolist()


def shape_constants():
    c = np.zeros((P, C_END), np.float32)
    c[:, C_ID:C_ID + P] = np.eye(P)
    tok = np.arange(S)
    row, col = (tok // GRID_W).astype(np.float32), (tok % GRID_W).astype(np.float32)

    def angles(n):
        f = (np.float32(ROPE_THETA) ** (-np.arange(n, dtype=np.float32) / np.float32(n))).astype(np.float32)
        return np.concatenate([row[:, None] * f, col[:, None] * f], axis=-1).astype(np.float32)

    def by_tile(a):
        return a.reshape(T, P, -1).transpose(1, 0, 2).reshape(P, -1)

    a = angles(HD // 4)
    c[:, C_COS:C_COS + 128], c[:, C_SIN:C_SIN + 128] = by_tile(np.cos(a)), by_tile(np.sin(a))
    a = angles(ROPE // 4)
    c[:, C_COS2:C_COS2 + 64], c[:, C_SIN2:C_SIN2 + 64] = by_tile(np.cos(a)), by_tile(np.sin(a))
    c[:, C_IOTA:C_IOTA + CAP] = np.arange(CAP)
    c[:, C_ONE:C_ONE + P] = 1.0
    inv = np.zeros((P, 2, S), np.float32)
    for g, w in enumerate(POOL_WINDOWS):
        n = np.clip(tok + w // 2, 0, S) - np.clip(tok - w // 2, 0, S)
        inv[(g % 2) * 64:(g % 2) * 64 + 64, g // 2] = (1.0 / n).astype(np.float32)
    return c, inv.reshape(P, 2 * S)


class Banks:

    def __init__(self, nc, ctx, psum):
        self.psum = psum
        self.full_sem = [ctx.enter_context(nc.semaphore(f"bank_full{b}")) for b in range(NBANK)]
        self.free_sem = [ctx.enter_context(nc.semaphore(f"bank_free{b}")) for b in range(NBANK)]
        self.next = 0

    def take(self, n):
        g = self.next
        self.next += n
        return range(g, g + n)

    def at(self, g):
        return self.psum[:, g % NBANK, :]

    def acquire(self, pe, g):
        if g >= NBANK:
            pe.wait_ge(self.free_sem[g % NBANK], g // NBANK)

    def filled(self, ins, g):
        ins.then_inc(self.full_sem[g % NBANK], 1)

    def full(self, eng, g):
        eng.wait_ge(self.full_sem[g % NBANK], g // NBANK + 1)

    def release(self, ins, g):
        ins.then_inc(self.free_sem[g % NBANK], 1)

    def drained(self, eng, g):
        eng.wait_ge(self.free_sem[g % NBANK], g // NBANK + 1)


def build(nc, a, out):
    ctx = ExitStack()
    pe, act, dve, pool, sp = nc.tensor, nc.scalar, nc.vector, nc.gpsimd, nc.sync
    with ctx:
        sems = {}

        def sem(name):
            if name not in sems:
                sems[name] = ctx.enter_context(nc.semaphore(name))
            return sems[name]

        def sb(name, cols, parts=P):
            return ctx.enter_context(nc.sbuf_tensor(name, [parts, cols], F32))

        psum = ctx.enter_context(nc.psum_tensor("psum", [P, NBANK, BANK], F32))
        B = Banks(nc, ctx, psum)

        ring_at = -(-nc.sbuf_base // 32) * 32
        ring = sb("ring", NSLOT * SLOT)
        x_flat = sb("x_res", T * D)
        hn_flat = sb("hn", T * D)
        W = sb("work_area", 10304)
        x_at = 4 * NSLOT * SLOT + ring_at
        hn_at, W_at = x_at + 4 * T * D, x_at + 8 * T * D

        def rounded(name, o, *dims, base=ring_at):
            return nc.alloc_sbuf_tensor_at(name, [P, *dims], F32R, offset=base + 4 * o)

        const = sb("const_sb", C_COS + NTOK)
        fill = sb("fill", 240)
        small = sb("small", SMALL)
        x_sb = x_flat[:].rearrange("p (t d) -> p t d", t=T)
        hn = hn_flat[:].rearrange("p (t d) -> p t d", t=T)
        taken = [0]

        def sm(n, parts=P):
            o = taken[0]
            taken[0] += n
            assert taken[0] <= SMALL
            return small[0:parts, o:o + n]

        def cut(base, o, *dims, parts=P):
            n = int(np.prod(dims))
            v = base[0:parts, o:o + n]
            if len(dims) == 2:
                v = v.rearrange("p (a b) -> p a b", a=dims[0])
            if len(dims) == 3:
                v = v.rearrange("p (a b c) -> p a b c", a=dims[0], b=dims[1])
            return v

        def slot(s):
            return ring[:, s * SLOT:(s + 1) * SLOT]

        ident = const[:, C_ID:C_ID + P]
        ones = const[:, C_ONE:C_ONE + P]
        ROWS, n_rows = {}, 0
        for name, n in (("norm_mix_g", KD), ("norm_mem_g", KD), ("norm_ffn_g", KD), ("norm_g_2", KD), ("c_2", KD),
                        ("c_ctx_2", KD), ("b_mod_2", 2 * KD), ("pool_scale", 2), ("g_cq_2", 2), ("g_ckv_2", 1),
                        ("mlstm_conv_w", 4 * ML_CONV)):
            ROWS[name] = (n_rows, n_rows + n)
            n_rows += n
        columns = sm(n_rows)
        column = {name: columns[:, lo:hi] for name, (lo, hi) in ROWS.items()}
        gain = {n: column[n] for n in ("norm_mix_g", "norm_mem_g", "norm_ffn_g", "norm_g_2")}
        b_mod_col, pool_scale = column["b_mod_2"], column["pool_scale"]
        conv_w = column["mlstm_conv_w"].rearrange("p (w c) -> p c w", w=ML_CONV)
        gate_bias = sm(2, 2 * ML_H)
        g_cq_col, g_ckv_col = column["g_cq_2"], column["g_ckv_2"]
        stat = sm(64)
        mod = sm(2 * KD * 2).rearrange("p (j v) -> p j v", v=2)
        router_w = sm(KD * N_EXP).rearrange("p (k e) -> p k e", k=KD)
        aff = sm(T * N_EXP).rearrange("p (t e) -> p t e", t=T)
        slot_of = sm(T * N_EXP).rearrange("p (t e) -> p t e", t=T)
        gcols = sm(P).rearrange("p (k t r) -> p k t r", k=4, t=T)
        posc = sm(T * 2).rearrange("p (t e) -> p t e", t=T)
        gatec = sm(T * 2).rearrange("p (t e) -> p t e", t=T)
        ml_den = sm(4 * T * ML_H).rearrange("p (i d t h) -> p i d t h", i=2, d=2, t=T)

        slot_free = [sem(f"slot_free{s}") for s in range(NSLOT)]
        slot_loaded = [sem(f"slot_loaded{s}") for s in range(NSLOT)]
        dve_step = sem("dve_step")
        n_dve = [0]

        def link(ins):
            n_dve[0] += 1
            ins.then_inc(dve_step, 1)
            dve.wait_ge(dve_step, n_dve[0])

        pool_step = sem("pool_step")
        n_pool = [0]

        def pool_link(ins):
            n_pool[0] += 1
            ins.then_inc(pool_step, 1)
            pool.wait_ge(pool_step, n_pool[0])

        blk_lo = [rounded(f"block_lo{i}", i * SLOT, SLOT) for i in range(2)]
        w_hi = rounded("w_hi", 2 * SLOT, KD, BANK)
        w_in = [cut(slot(i), 0, KD, BANK) for i in (0, 1, 1, 0)]
        w_in_lo = [blk_lo[i][:].rearrange("p (k c) -> p k c", k=KD) for i in (0, 1, 1, 0)]
        W_IN_COLS = (((0, 512),), ((512, 768), (1808, 2064)), ((768, 1280),), ((1296, 1808),))
        w_gate = cut(W, 9264, KD, 16)
        ca_wkv = ring[:, 4 * SLOT:6 * SLOT].rearrange("p (k c) -> p k c", k=KD)
        mem = cut(slot(6), 0, 2, D)
        memT = cut(slot(6), 2048, KD, N_MEM)
        kT_ca = cut(W, 0, CA_H, N_MEM)
        v_ca = cut(W, 1024, 2, CA_H * CA_HD)
        hT, hT_lo = cut(slot(7), 0, KD, S), rounded("hT_lo", 7 * SLOT, KD, S)
        hT_hi = rounded("hT_hi", 3 * SLOT, KD, S)
        four = 4 * SLOT
        qkpad = cut(ring, four, 4, QKP)
        sig_o = cut(ring, four + 2064, T, ML_H * HD)
        aq = cut(ring, four + 3088, T, AT_H, HD)
        ak = cut(ring, four + 5136, T, 2, HD)
        av = cut(ring, four + 5648, T, 2 * HD)
        qT_at = cut(ring, four, 4, S)
        kT_at = ring[:, four + 6160:four + 6672]
        pool_w = cut(ring, four + 6672, 2, POOL_G)
        ml_g = ring[:, four + 6800:four + 7056]
        qg = ring[:, four + 7056:four + 7120]
        kg = ring[:, four + 7120:four + 7184]
        mod_c = cut(ring, four + 7184, 2, KD)
        pick = cut(ring, four + 7200, 2, 32)
        mod_rows = ring[:, four + 7440:four + 7952]
        rows = W[0:n_rows, 2048:2048 + P]
        gate_b_rows = W[0:2, 2176:2176 + 2 * ML_H]
        upad = cut(slot(6), 0, 2, UP)
        p1 = cut(slot(6), 1056, 2, UP)
        p2 = cut(slot(6), 2112, 2, UP)
        p3 = slot(6)[:, 3168:3168 + UP]
        inv_n = cut(W, 9264, 2, S)
        d_pool = cut(hn_flat, 2048, 2, S)
        ymixT = cut(hn_flat, 0, KD, S)
        grow = [W[0:2 * ML_H, 2048 + i * S:2048 + (i + 1) * S] for i in range(8)]
        qkT = cut(W, 6144, 4, S)
        v_aug = cut(W, 8192, T, ML_H, HD + 1)
        v_pad = W[:, 8192 + T * ML_H * (HD + 1):9264]

        def v_moving(i, h):
            o = 8192 + (i * ML_H + h) * (HD + 1)
            return W[:, o:o + V_MOVE]

        hsum = cut(slot(6), 0, T, ML_H, HD)
        htmp = cut(slot(6), 1024, T, ML_H, HD)
        Pt = [[cut(slot(7), 0, T, S), cut(slot(7), 2048, T, S)], [cut(hn_flat, 2048, T, S), cut(slot(6), 2048, T, S)]]
        gate_row = W[:, 9264:9264 + D]
        w_mod = [slot(i)[:, 0:3 * D] for i in (0, 1, 2, 3, 2, 3, 2, 3)]
        mod_sum = [W[:, 2048:2048 + 3 * D], W[:, 5120:5120 + 2 * D]]
        gate_lin = [W[0:1, 7168 + j * BANK:7168 + (j + 1) * BANK] for j in range(2)]
        sq_q = cut(ring, four, T, AT_H, HD)
        w_out = ring[:, 0:2 * SLOT].rearrange("p (k c) -> p k c", k=KD)
        ca_wq = cut(slot(2), 0, KD, CA_H * CA_HD)
        ca_wo = cut(slot(3), 0, CA_H, D)
        rope_t = [cut(W, 9264 + i * 256, AT_H, HD // 2) for i in range(2)]
        p_at = [slot(6)[:, 2048 + i * S:2048 + (i + 1) * S] for i in range(4)]
        pt_at = [cut(slot(7), i * 2048, T, S) for i in range(2)]
        hn_ca = cut(ring, four, T, D)
        qT_ca = cut(W, 2048, CA_H, S)
        ca_wo_lo, ca_wo_hi = rounded("ca_wo_lo", 3 * SLOT, CA_H, D), rounded("ca_wo_hi", 6 * SLOT, CA_H, D)
        oT_hi, oT_lo = rounded("oT_hi", 4096, CA_H, S, base=W_at), rounded("oT_lo", 5 * SLOT, CA_H, S)
        p_ca = [W[:, 6144 + i * N_MEM:6144 + (i + 1) * N_MEM] for i in range(4)]
        pt_ca = [cut(W, 7168, 2, S), cut(W, 8192, 2, S)]
        logitsT, left, slotT, ones16 = (W[0:N_EXP, 2048 + i * S:2048 + (i + 1) * S] for i in range(4))
        top8 = W[0:N_EXP, 4096:4096 + CAP]
        ctx_n = cut(W, 4160, 2, D)
        hcT = cut(W, 6656, KD, CTX)

        xsT = cut(W, 0, KD, P)
        silu_g = cut(W, 1024, 2, BANK)
        hid = cut(W, 2048, 2, BANK)
        hidT = [cut(W, 3072 + b * 512, 4, 2, CAP) for b in range(2)]
        sel = cut(W, 4096, T, P)
        selg = cut(W, 4608, T, P)
        selgT = W[:, 5120:5632]
        ypair = W[:, 5632:6656]

        blk = [slot(0), slot(1)]
        h2T, h2_lo = cut(slot(3), 0, KD, S), rounded("h2_lo", 3 * SLOT, KD, S)
        h2_hi = rounded("h2_hi", 4 * SLOT, KD, S)
        hc_lo = rounded("hc_lo", 5 * SLOT, KD, CTX)
        hc_hi = rounded("hc_hi", 5 * SLOT + 2048, KD, CTX)
        ckv_hi = rounded("ckv_hi", 2 * SLOT + 2048, KD, 160)
        cq_hi = rounded("cq_hi", 2 * SLOT, KD, Q_LORA)
        part_hi = rounded("part_hi", 2 * SLOT, 4, KD, P)
        square_junk, dve_junk = slot(6)[:, 0:D], slot(6)[:, D:2 * D]
        g_row = slot(6)[:, 2048:2048 + D]
        oaT = cut(slot(6), 0, 4, S)
        kT_mla = cut(ring, 6 * SLOT + 2048, MLA_H, NTOK, parts=QK_MLA)
        q_tok = cut(slot(2), 0, T, MLA_H, QK_MLA)
        ckv = cut(hn_flat, 0, KT2, KV_LORA + ROPE)
        qT_mla = cut(hn_flat, 0, MLA_H, S, parts=QK_MLA)
        va = cut(W, 0, KT2, MLA_H * HD)
        ckvT = W[:, 3072:3840]
        uq = cut(W, 4096, 2, MLA_H * QK_MLA)
        ukv = cut(W, 5632, MLA_H, NOPE + HD)
        cq = cut(W, 6656, T, Q_LORA)
        cqT = cut(W, 7680, 2, S)
        rope2_t = [cut(W, 8704 + i * 128, MLA_H, 2, 8) for i in range(2)]
        pt_mla = [cut(W, 3072, KT2, S), cut(slot(2), 0, KT2, S)]
        p_mla = [W[:, 6144 + i * NTOK:6144 + (i + 1) * NTOK] for i in range(4)]
        qbT = cut(hn_flat, 0, 4, S)
        obT = cut(hn_flat, 2048, 4, S)
        kbT = cut(ring, 6 * SLOT + 2048, 4, NTOK)
        vb = cut(ring, 6 * SLOT + 5120, KT2, NA_H * HD)
        na_table = cut(W, 2048, NA_H, 14 * GRID_W)
        pt_na = [cut(slot(5), 0, KT2, S), cut(slot(2), 0, KT2, S)]
        p_na = [W[:, 0:NTOK], W[:, NTOK:2 * NTOK], slot(5)[:, 3072:3072 + NTOK], const[:, C_COS:C_COS + NTOK]]
        woa, woa_lo = cut(ring, 6 * SLOT + 2048, 4, D), rounded("woa_lo", 6 * SLOT + 2048, 4, D)
        wob, wob_lo = cut(slot(3), 0, 4, D), rounded("wob_lo", 3 * SLOT, 4, D)
        wab_hi = [rounded(f"wab_hi{i}", 6144 + i * 1024, 4, 2 * P, base=W_at) for i in range(2)]
        oa_hi, oa_lo = rounded("oa_hi", 0, 4, S, base=hn_at), rounded("oa_lo", 6 * SLOT, 4, S)
        ob_hi, ob_lo = rounded("ob_hi", 7 * SLOT + 2048, 4, S), rounded("ob_lo", 2048, 4, S, base=hn_at)
        yT, yT_lo = cut(W, 2048, KD, S), rounded("yT_lo", 2048, KD, S, base=W_at)
        sgb, yT_hi = cut(slot(5), 0, KD, S), rounded("yT_hi", 5 * SLOT, KD, S)
        halves = lambda v: v.rearrange("p (k c) -> p k c", k=4)
        w_out2 = [halves(slot(0)), halves(slot(1))]
        w_out2_lo = [halves(v[:]) for v in blk_lo]
        w_out2_hi = [halves(v[:].rearrange("p a b -> p (a b)")) for v in (h2_hi, w_hi)]
        ysum = [W[:, 8192 + i * S:8192 + (i + 1) * S] for i in range(2)]
        g_fin = W[:, D:2 * D]

        na_dram = nc.dram_tensor("na_scratch", [NA_H * (2 * NA_KR - 1), GRID_W, GRID_W], F32, kind="Internal").ap()

        def copy(eng, o, i, scale=None, bias=None):
            if eng is act:
                kw = {}
                if scale is not None:
                    kw["scale"] = scale
                if bias is not None:
                    kw["bias"] = bias
                return act.activation(o, i, ACT.Identity, **kw)
            if scale is None and bias is None:
                return dve.tensor_copy(o, i)
            if scale is None:
                return dve.tensor_scalar(o, i, bias, None, ALU.add)
            if bias is None:
                return dve.tensor_scalar(o, i, scale, None, ALU.mult)
            return dve.tensor_scalar(o, i, scale, bias, ALU.mult, ALU.add)

        def load_sqrt_act():
            act.wait_ge(sem("const_in"), 16)
            act.activation(stat[:, 62:63], ident[:, 0:1], ACT.Sqrt)

        norms = [0, 0]

        def rms_rows(src, dst, tiles, width, mark):
            ss, ms, rt, rs = (stat[:, i * 8:i * 8 + tiles] for i in range(4))
            squared, mean_ready, root_ready = sem("rows_squared"), sem("mean_ready"), sem("root_ready")
            norms[0] += 1
            norms[1] += tiles
            turn, rows = norms

            def on_act(junk=None):
                for t in range(tiles):
                    act.activation((junk or dst)[:, t, :], src[:, t, :], ACT.Square,
                                   accum_out=ss[:, t:t + 1]).then_inc(squared, 1)
                act.wait_ge(mean_ready, turn)
                act.activation(rt, ms, ACT.Sqrt).then_inc(root_ready, 1)

            def on_dve():
                dve.wait_ge(squared, rows)
                dve.tensor_scalar(ms, ss, 1.0 / width, EPS, ALU.mult, ALU.add).then_inc(mean_ready, 1)
                dve.wait_ge(root_ready, turn)
                link(dve.reciprocal(rs, rt))
                for t in range(tiles):
                    dve.tensor_scalar(dst[:, t, :], src[:, t, :], rs[:, t:t + 1], None, ALU.mult).then_inc(mark, 1)

            return on_act, on_dve

        def add_norm(groups, src, dst, mark, arrived=None):
            squared, mean_ready, root_ready = sem("rows_squared"), sem("mean_ready"), sem("root_ready")
            turn = list(norms)
            norms[0] += T
            norms[1] += T
            ss, ms, rt, rs = (stat[:, i * 8:i * 8 + T] for i in range(4))

            def on_act():
                for t in range(T):
                    if arrived and t % 2 == 0:
                        act.wait_ge(arrived[t // 2], 16)
                    for g in groups[2 * t:2 * t + 2]:
                        B.drained(act, g)
                    act.activation(dst[:, t, :], src[:, t, :], ACT.Square, accum_out=ss[:, t:t + 1]).then_inc(squared, 1)
                    act.wait_ge(mean_ready, turn[0] + t + 1)
                    act.activation(rt[:, t:t + 1], ms[:, t:t + 1], ACT.Sqrt).then_inc(root_ready, 1)

            def on_dve():
                for t in range(T):
                    for n, g in enumerate(groups[2 * t:2 * t + 2]):
                        o = x_sb[:, t, n * BANK:(n + 1) * BANK]
                        B.full(dve, g)
                        B.release(dve.tensor_tensor(o, B.at(g), o, ALU.add), g)
                    dve.wait_ge(squared, turn[1] + t + 1)
                    dve.tensor_scalar(ms[:, t:t + 1], ss[:, t:t + 1], 1.0 / D, EPS, ALU.mult, ALU.add).then_inc(mean_ready, 1)
                    dve.wait_ge(root_ready, turn[0] + t + 1)
                    link(dve.reciprocal(rs[:, t:t + 1], rt[:, t:t + 1]))
                    dve.tensor_scalar(dst[:, t, :], src[:, t, :], rs[:, t:t + 1], None, ALU.mult).then_inc(mark, 1)

            return on_act, on_dve

        def three_passes(g, o, w, x, weights_move=False):
            pairs = []
            for k in range(w[0].shape[1]):
                (wh, wl), (xh, xl) = ([half[:, k, :] for half in v] for v in (w, x))
                for a_, b_ in ((wh, xh), (wh, xl), (wl, xh)):
                    pairs.append((b_, a_) if weights_move else (a_, b_))
            B.filled(product(g, o, pairs), g)

        def turn_tiles(groups, src, mark, tiles=range(T)):
            for t, half in ((t, half) for t in tiles for half in range(2)):
                g = groups[2 * t + half]
                pe.wait_ge(mark, t + 1)
                B.acquire(pe, g)
                for k in range(4):
                    ins = pe.transpose(B.at(g)[:, k * P:(k + 1) * P], src[:, t, (4 * half + k) * P:(4 * half + k + 1) * P], ident)
                B.filled(ins, g)

        def drain_tiles(eng, groups, dst, scale, bias=None):
            for i, g in enumerate(groups):
                t, half = i // 2, i % 2
                if (half == 0) == (eng is act):
                    B.full(eng, g)
                    for k in range(4 * half, 4 * half + 4):
                        ins = copy(eng, dst[:, k, t * P:(t + 1) * P], B.at(g)[:, (k % 4) * P:(k % 4 + 1) * P],
                                   scale[:, k:k + 1], None if bias is None else bias[:, k:k + 1])
                    B.release(ins, g)

        def product(g, o, pairs):
            for i, (l, r) in enumerate(pairs):
                ins = pe.matmul(o, l, r, start=(i == 0), stop=(i == len(pairs) - 1))
            return ins

        def transpose_rows(groups, src, tiles):
            per = BANK // (tiles * P)
            for i, g in enumerate(groups):
                B.acquire(pe, g)
                for k in range(i * per, (i + 1) * per):
                    for t in range(tiles):
                        o = ((k - i * per) * tiles + t) * P
                        ins = pe.transpose(B.at(g)[:, o:o + P], src[:, t, k * P:(k + 1) * P], ident)
                B.filled(ins, g)

        def drain_rows(eng, groups, tiles, dst, scale=None, bias=None):
            per = BANK // (tiles * P)
            for i, g in enumerate(groups):
                if (g % 2 == 0) == (eng is act):
                    B.full(eng, g)
                    for k in range(i * per, (i + 1) * per):
                        o = (k - i * per) * tiles * P
                        ins = copy(eng, dst[:, k, :], B.at(g)[:, o:o + tiles * P],
                                   None if scale is None else scale[:, k:k + 1],
                                   None if bias is None else bias[:, k:k + 1])
                    B.release(ins, g)

        def drain(eng, g, o, i, scale=None, bias=None):
            if (g % 2 == 0) == (eng is act):
                B.full(eng, g)
                B.release(copy(eng, o, i, scale, bias), g)

        def plan_attention(heads, segs, nkt, lag):
            units = [(c, j, qt) for c in range(len(heads)) for j in range(len(heads[c])) for qt in range(T)]
            order, n_out = [], 0
            for i in range(len(units) + lag):
                if i < len(units):
                    order.append(("S", i))
                if i >= lag:
                    order.append(("T", i - lag))
                while (n_out + 1) * T + O_LATER <= i - lag + 1 or (i == len(units) + lag - 1 and n_out < len(units) // T):
                    order.append(("O", n_out))
                    n_out += 1
            size = {"S": len(segs), "T": -(-nkt // 4), "O": 1}
            return units, order, {(kind, i): list(B.take(size[kind])) for kind, i in order}

        def attention(name, heads, segs, q_at, k_at, v_at, dv, pbuf, ptbuf, o_out, ready, bias=None, besides={}):
            nkt, nseg, np_ = sum(segs) // P, len(segs), len(pbuf)
            units, order, gid = plan_attention(heads, segs, nkt, np_ - 1)
            maxed, normed = sem(name + "_max"), sem(name + "_weights")
            exp_biased = sem(name + "_exp") if bias is not None else None
            tmp_max = lambda i: stat[:, 32 + 2 * (i % 4):34 + 2 * (i % 4)]
            neg_max = lambda i: stat[:, 40 + i % 4:41 + i % 4]
            sums = lambda i: stat[:, 44 + 2 * (i % 4):46 + 2 * (i % 4)]
            recip = lambda i: stat[:, 52 + 2 * (i % 4):54 + 2 * (i % 4)]
            turned = lambda n: ptbuf[n % len(ptbuf)]
            last_out = gid["O", len(units) // T - 1][0]

            def on_pe():
                for s, n in ready:
                    pe.wait_ge(s, n)
                for kind, i in order:
                    gs = gid[kind, i]
                    if kind == "S":
                        c, j, qt = units[i]
                        for si, g in enumerate(gs):
                            B.acquire(pe, g)
                            B.filled(product(g, B.at(g)[:, 0:segs[si]], [(q_at(heads[c][j], qt), k_at(heads[c][j], si))]), g)
                    elif kind == "T":
                        pe.wait_ge(normed, i + 1)
                        for n, g in enumerate(gs):
                            B.acquire(pe, g)
                            for kt in range(4 * n, min(4 * n + 4, nkt)):
                                ins = pe.transpose(B.at(g)[:, (kt % 4) * P:(kt % 4 + 1) * P],
                                                   pbuf[i % np_][:, kt * P:(kt + 1) * P], ident)
                            B.filled(ins, g)
                    else:
                        g = gs[0]
                        B.acquire(pe, g)
                        for u in range(i * T, (i + 1) * T):
                            for gt in gid["T", u]:
                                B.drained(pe, gt)
                        c, j, _ = units[i * T]
                        B.filled(product(g, B.at(g)[j * dv:(j + 1) * dv, :],
                                         [(v_at(heads[c][j], kt), turned(i)[:, kt, :]) for kt in range(nkt)]), g)

            def on_act():
                for kind, i in order:
                    gs = gid[kind, i]
                    if kind == "S":
                        act.wait_ge(maxed, i + 1)
                        if i >= np_ and bias is None:
                            B.full(act, gid["T", i - np_][-1])
                        o = 0
                        for n, g in enumerate(gs):
                            dst = pbuf[i % np_][:, o:o + segs[n]]
                            o += segs[n]
                            if bias is not None and n == 0:
                                act.activation(dst, dst, ACT.Exp, bias=neg_max(i),
                                               accum_out=sums(i)[:, 0:1]).then_inc(exp_biased, 1)
                            else:
                                B.release(act.activation(dst, B.at(g)[:, 0:segs[n]], ACT.Exp, bias=neg_max(i),
                                                         accum_out=sums(i)[:, n:n + 1]), g)
                        if (act, i) in besides:
                            besides[act, i]()
                    elif kind == "T":
                        c, j, qt = units[i]
                        n_head = i // T
                        if qt == 0 and n_head >= len(ptbuf):
                            B.full(act, gid["O", n_head - len(ptbuf)][0])
                        for n, g in enumerate(gs):
                            m = min(4, nkt - 4 * n)
                            B.full(act, g)
                            B.release(act.activation(turned(n_head)[:, 4 * n:4 * n + m, qt * P:(qt + 1) * P],
                                                     B.at(g)[:, 0:m * P].rearrange("p (k q) -> p k q", k=m),
                                                     ACT.Identity), g)

            def on_dve():
                def divide(i):
                    if bias is not None:
                        dve.wait_ge(exp_biased, i + 1)
                    for g in gid["S", i][1 if bias is not None else 0:]:
                        B.drained(dve, g)
                    s = sums(i)[:, 0:1]
                    if nseg == 2:
                        link(dve.tensor_tensor(recip(i)[:, 0:1], sums(i)[:, 0:1], sums(i)[:, 1:2], ALU.add))
                        s = recip(i)[:, 0:1]
                    link(dve.reciprocal(recip(i)[:, 1:2], s))
                    dve.tensor_scalar(pbuf[i % np_], pbuf[i % np_], recip(i)[:, 1:2], None, ALU.mult).then_inc(normed, 1)

                for kind, i in order:
                    gs = gid[kind, i]
                    if kind == "S":
                        c, j, qt = units[i]
                        for n, g in enumerate(gs):
                            B.full(dve, g)
                            if bias is not None and n == 0:
                                if i >= np_:
                                    B.full(dve, gid["T", i - np_][-1])
                                B.release(dve.tensor_tensor_reduce(
                                    out=pbuf[i % np_][:, 0:segs[0]], in0=B.at(g)[:, 0:segs[0]],
                                    in1=bias(heads[c][j], qt), scale=1.0, scalar=NEG * 2, op0=ALU.add, op1=ALU.max,
                                    accum_out=tmp_max(i)[:, 0:1]), g)
                                B.drained(dve, g)
                            elif nseg == 1:
                                dve.tensor_reduce(neg_max(i), B.at(g)[:, 0:segs[0]], AX, ALU.max,
                                                  negate=True).then_inc(maxed, 1)
                            else:
                                link(dve.tensor_reduce(tmp_max(i)[:, n:n + 1], B.at(g)[:, 0:segs[n]], AX, ALU.max))
                        if nseg == 2:
                            dve.tensor_reduce(neg_max(i), tmp_max(i), AX, ALU.max, negate=True).then_inc(maxed, 1)
                        if i >= 1:
                            divide(i - 1)
                        if i == len(units) - 1:
                            divide(i)
                        if (dve, i) in besides:
                            besides[dve, i]()
                    elif kind == "O":
                        c, j, _ = units[i * T]
                        rows = slice(j * dv, (j + 1) * dv)
                        B.full(dve, gs[0])
                        B.release(o_out(c, rows, B.at(gs[0])[rows, :]), gs[0])

            return on_pe, on_act, on_dve, last_out

        g_memT = B.take(4)
        g_columns = B.take(1)
        hn_mix = sem("hn_mix")
        norm1_act, norm1_dve = add_norm([], x_sb, hn, hn_mix, arrived=[sem("x_in0"), sem("x_in1")])
        g_h1 = B.take(2 * T)
        g_gate = B.take(1)
        g_kca = B.take(2)
        g_vca = B.take(2)

        def first_turns_pe():
            pe.wait_ge(sem("const_in"), 16)
            pe.wait_ge(sem("mem_in"), 16)
            transpose_rows(g_memT, mem, 2)
            pe.wait_ge(sem("rows_in"), 16 * N_ROW_LOADS)
            g = g_columns[0]
            B.acquire(pe, g)
            pe.transpose(B.at(g)[:, 0:n_rows], rows, ident[0:n_rows, 0:n_rows])
            B.filled(pe.transpose(B.at(g)[0:2 * ML_H, P:P + 2], gate_b_rows, ident[0:2, 0:2]), g)
            turn_tiles(g_h1, hn, hn_mix)

        def columns_act():
            g = g_columns[0]
            B.full(act, g)
            act.activation(columns, B.at(g)[:, 0:n_rows], ACT.Identity)
            B.release(act.activation(gate_bias, B.at(g)[0:2 * ML_H, P:P + 2], ACT.Identity), g)

        def memory_pe():
            pe.wait_ge(sem("ca_wkv_in"), 16)
            for g in g_memT:
                B.drained(pe, g)
            for i, g in enumerate(g_kca):
                B.acquire(pe, g)
                for h in (2 * i, 2 * i + 1):
                    ins = product(g, B.at(g)[:, (h % 2) * N_MEM:(h % 2 + 1) * N_MEM],
                                  [(ca_wkv[:, k, h * CA_HD:(h + 1) * CA_HD], memT[:, k, :]) for k in range(KD)])
                B.filled(ins, g)
            for m, g in enumerate(g_vca):
                B.acquire(pe, g)
                B.filled(product(g, B.at(g), [(memT[:, k, m * P:(m + 1) * P], ca_wkv[:, k, BANK:]) for k in range(KD)]), g)

        def memory_drain(eng):
            for i, g in enumerate(g_kca):
                drain(eng, g, kT_ca[:, 2 * i:2 * i + 2, :], B.at(g).rearrange("p (h m) -> p h m", h=2))
            for m, g in enumerate(g_vca):
                drain(eng, g, v_ca[:, m, :], B.at(g))

        g_chan = B.take(6)
        g_akv = B.take(T)
        g_aq = B.take(2 * T)
        g_cols = B.take(1)
        g_v = B.take(T)
        g_o = B.take(T)
        g_pool = B.take(2)
        in_parts = [(0, c * P, P, c * P, None) for c in range(4)]
        in_parts += [(1, c * P, P, c * P, g_chan[c]) for c in range(2)]
        in_parts += [(1, 256, 256, 256, g_chan[3]), (3, 0, 256, 0, g_chan[5]), (3, 256, 256, 256, g_akv[-1]),
                     (2, 0, 256, 0, g_aq[T - 1]), (2, 256, 256, 256, g_aq[-1])]
        in_rounded, in_split = sem("in_rounded"), sem("in_split")
        hT_split = sem("hT_split")

        def round_in_part(i):
            b, c, n, o, used = in_parts[i]
            act.wait_ge(w_in_loaded[b], 16 * len(W_IN_COLS[b]))
            if used is not None:
                B.full(act, used)
            act.activation(w_hi[:, :, o:o + n], w_in[b][:, :, c:c + n], ACT.Identity).then_inc(in_rounded, 1)

        def rest_of_in_parts(lo, hi):
            for i in range(lo, hi):
                b, c, n, o, _ = in_parts[i]
                pool.wait_ge(in_rounded, i + 1)
                pool.tensor_tensor(w_in_lo[b][:, :, c:c + n], w_in[b][:, :, c:c + n],
                                   w_hi[:, :, o:o + n].bitcast(F32), ALU.subtract).then_inc(in_split, 1)

        def in_part(i):
            b, c, n, o, _ = in_parts[i]
            pe.wait_ge(in_split, i + 1)
            return w_hi[:, :, o:o + n], w_in_lo[b][:, :, c:c + n]

        def gate_pe():
            for g in g_h1:
                B.drained(pe, g)
            pe.wait_ge(sem("w_gate_in"), 16)
            g = g_gate[0]
            B.acquire(pe, g)
            for k in range(KD):
                for i in range(2):
                    ins = pe.matmul(B.at(g)[64 * i:64 * i + 8, :], w_gate[:, k, 8 * i:8 * i + 8], hT[:, k, :],
                                    start=(k == 0), stop=(k == KD - 1), skip_group_check=True)
            B.filled(ins, g)

        def hT_split_act():
            for g in g_h1:
                B.drained(act, g)
            act.activation(hT_hi[:], hT, ACT.Identity).then_inc(sem("hT_rounded"), 1)

        def hT_split_dve():
            dve.wait_ge(sem("hT_rounded"), 1)
            B.full(dve, g_gate[0])
            dve.tensor_tensor(hT_lo[:], hT, hT_hi[:].bitcast(F32), ALU.subtract).then_inc(hT_split, 1)

        def project_pe():
            pe.wait_ge(hT_split, 1)
            for c, g in enumerate(g_chan):
                w = in_part(c)
                B.acquire(pe, g)
                three_passes(g, B.at(g), w, (hT_hi, hT_lo))
            project_tokens_pe(g_akv, 6)
            project_tokens_pe(g_aq[0:T], 7)
            project_tokens_pe(g_aq[T:], 8)

        def project_tokens_pe(groups, i):
            w = in_part(i)
            for t, g in enumerate(groups):
                B.acquire(pe, g)
                three_passes(g, B.at(g)[:, 0:256], w, [v[:, :, t * P:(t + 1) * P] for v in (hT_hi, hT_lo)], weights_move=True)

        def gate_act():
            g = g_gate[0]
            B.full(act, g)
            B.drained(act, g_columns[0])
            act.activation(gi, B.at(g)[0:8, :], ACT.Identity, bias=gate_bias[:, 0:1])
            B.release(copy(act, gf, B.at(g)[64:72, :], None, gate_bias[:, 1:2]), g)

        def project_act():
            then = {0: (4,), 1: (5,), 3: (6,), 5: (7,)}
            for c, g in enumerate(g_chan):
                B.full(act, g)
                if c == 0:
                    act.wait_ge(sem("pads"), 2)
                dst = upad[:, c, PADL:PADL + S] if c < 2 else qkpad[:, c - 2, 2:2 + S]
                B.release(copy(act, dst, B.at(g)), g)
                for i in then.get(c, ()):
                    round_in_part(i)
            for t, g in enumerate(g_akv):
                B.full(act, g)
                act.activation(ak[:, t], B.at(g)[:, 0:128].rearrange("p (h d) -> p h d", h=2),
                               ACT.Identity).then_inc(sem("ak"), 1)
                B.release(copy(act, av[:, t, :], B.at(g)[:, 128:256]), g)
            round_in_part(8)
            for i, g in enumerate(g_aq):
                half, t = i // T, i % T
                B.full(act, g)
                B.release(copy(act, aq[:, t, half::2, :], B.at(g)[:, 0:256].rearrange("p (i d) -> p i d", i=4)), g)
                if t == T - 1:
                    round_in_part(9 + half)

        def project_vo_act():
            for t, g in enumerate(g_v):
                B.full(act, g)
                if t == 0:
                    act.wait_ge(sem("pads"), 3)
                B.release(copy(act, v_aug[:, t, :, 0:HD], B.at(g)[:, 0:256].rearrange("p (h d) -> p h d", h=ML_H)), g)
            for t, g in enumerate(g_o):
                B.full(act, g)
                B.release(act.activation(sig_o[:, t, :], B.at(g)[:, 0:256], ACT.Sigmoid), g)

        def pool_dve():
            for g in g_chan[0:2]:
                B.drained(dve, g)
            L = UP
            link(dve.tensor_tensor(p1[:, :, 1:L], upad[:, :, 0:L - 1], upad[:, :, 1:L], ALU.add))
            link(dve.tensor_tensor(p2[:, :, 2:L - 1], p1[:, :, 1:L - 2], p1[:, :, 3:L], ALU.add))
            link(dve.tensor_tensor(p3[:, 4:L - 3], p2[:, 1, 2:L - 5], p2[:, 1, 6:L - 1], ALU.add))
            link(dve.tensor_tensor(p1[64:128, 1, 8:L - 7], p3[64:128, 4:L - 11], p3[64:128, 12:L - 3], ALU.add))
            dve.wait_ge(sem("inv_n_in"), 16)
            B.full(dve, g_h1[-1])
            w = slice(PADL, PADL + S)
            for c, lo, hi, s in ((0, 0, 64, p1[0:64, 0, w]), (0, 64, 128, p2[64:128, 0, w]),
                                 (1, 0, 64, p3[0:64, w]), (1, 64, 128, p1[64:128, 1, w])):
                link(dve.tensor_tensor(d_pool[lo:hi, c, :], s, inv_n[lo:hi, c, :], ALU.mult))
                dve.tensor_tensor(d_pool[lo:hi, c, :], d_pool[lo:hi, c, :], upad[lo:hi, c, w],
                                  ALU.subtract).then_inc(sem("pooled"), 1)

        def pool_pe():
            pe.wait_ge(sem("pooled"), 4)
            pe.wait_ge(sem("pool_w_in"), 16)
            for c, g in enumerate(g_pool):
                B.acquire(pe, g)
                for lo in (0, 64):
                    ins = pe.matmul(B.at(g)[lo:lo + 64, :], pool_w[lo:lo + 64, c, :], d_pool[lo:lo + 64, c, :],
                                    start=True, stop=True)
                B.filled(ins, g)

        def pool_act():
            for c, g in enumerate(g_pool):
                B.full(act, g)
                B.release(copy(act, ymixT[:, c, :], B.at(g), pool_scale[:, c:c + 1]), g)

        def conv_dve():
            for g in g_chan[2:6]:
                B.drained(dve, g)
            for c in range(4):
                link(dve.tensor_scalar(qkT[:, c, :], qkpad[:, c, 0:S], conv_w[:, c, 0:1], None, ALU.mult))
                for w in range(1, ML_CONV):
                    ins = dve.scalar_tensor_tensor(out=qkT[:, c, :], in0=qkpad[:, c, w:w + S], scalar=conv_w[:, c, w:w + 1],
                                                   in1=qkT[:, c, :], op0=ALU.mult, op1=ALU.add)
                    if w < ML_CONV - 1:
                        link(ins)
                    else:
                        ins.then_inc(sem("conv"), 1)

        def conv_act():
            for c in range(4):
                act.wait_ge(sem("conv"), c + 1)
                act.activation(qkT[:, c, :], qkT[:, c, :], ACT.Silu).then_inc(sem("qk_silu"), 1)

        gi, gf, e_f, l_f, bsum, arow, mrow, bm = grow
        arow2, mrow2, bm2 = gi, l_f, gf
        rows_f, rows_b = sem("gate_rows_f"), sem("gate_rows_b")

        def gates_dve():
            B.drained(dve, g_gate[0])
            dve.scalar_tensor_tensor(out=e_f, in0=gf, scalar=-1.0, in1=gf, op0=ALU.mult, op1=ALU.min).then_inc(sem("neg_abs_f"), 1)
            dve.wait_ge(sem("log_f"), 1)
            link(dve.scalar_tensor_tensor(out=e_f, in0=gf, scalar=0.0, in1=l_f, op0=ALU.min, op1=ALU.subtract))
            ones8 = const[0:8, C_ONE:C_ONE + 1].to_broadcast([8, S])
            link(dve.tensor_tensor_scan(bsum, ones8, e_f, 0.0, ALU.mult, ALU.add))
            link(dve.tensor_tensor(arow, gi, bsum, ALU.subtract))
            link(dve.tensor_tensor_scan(mrow, arow, arow, 0.0, ALU.max, ALU.max))
            link(dve.tensor_tensor(bm, bsum, mrow, ALU.add))
            dve.tensor_scalar(mrow, mrow, -1.0, None, ALU.mult).then_inc(rows_f, 1)
            link(dve.tensor_tensor_scan(bsum[:, ::-1], ones8, e_f[:, ::-1], 0.0, ALU.mult, ALU.add))
            link(dve.tensor_tensor(arow2, gi, bsum, ALU.subtract))
            link(dve.tensor_tensor_scan(mrow2[:, ::-1], arow2[:, ::-1], arow2[:, ::-1], 0.0, ALU.max, ALU.max))
            link(dve.tensor_tensor(bm2, bsum, mrow2, ALU.add))
            dve.tensor_scalar(mrow2, mrow2, -1.0, None, ALU.mult).then_inc(rows_b, 1)

        def gates_act():
            act.wait_ge(sem("neg_abs_f"), 1)
            act.activation(e_f, e_f, ACT.Exp).then_inc(sem("exp_f"), 1)
            act.wait_ge(sem("exp_f"), 1)
            act.activation(l_f, e_f, ACT.Ln, bias=1.0).then_inc(sem("log_f"), 1)

        def gate_columns_act():
            g = g_cols[0]
            B.full(act, g)
            v = B.at(g)[:, 0:P].rearrange("p (k t r) -> p k t r", k=4, t=T)
            act.activation(gcols[:, 0:2], v[:, 0:2], ACT.Identity).then_inc(sem("gate_columns"), 1)
            B.release(act.activation(gcols[:, 2:4], v[:, 2:4], ACT.Exp, scale=-1.0), g)

        def gates_pe():
            pe.wait_ge(rows_f, 1)
            pe.wait_ge(rows_b, 1)
            g = g_cols[0]
            B.acquire(pe, g)
            for k, r in enumerate((arow, arow2, bm, bm2)):
                for t in range(T):
                    ins = pe.transpose(B.at(g)[:, (k * T + t) * 8:(k * T + t) * 8 + 8], r[:, t * P:(t + 1) * P], ident[0:8, 0:8])
            B.filled(ins, g)

        mod_added = sem("mod_added")

        def silu_c_act():
            B.drained(act, g_columns[0])
            for v, name in enumerate(("c_2", "c_ctx_2")):
                act.activation(mod_c[:, v, :], column[name], ACT.Silu).then_inc(sem("silu_c"), 1)

        def mod_chunk(eng, k):
            if k == 0:
                eng.wait_ge(sem("silu_c"), 2)
                B.full(eng, g_ms[ML_H - 1][-1])
            else:
                eng.wait_ge(mod_added, k)
            eng.wait_ge(w_mod_loaded[k if k < 4 else 2 + k % 2], 16 * (1 if k < 4 else k // 2))
            return mod_c[:, 1, k:k + 1], mod_c[:, 0, k:k + 1]

        def mod_pool(lo, hi):
            for k in range(lo, hi):
                c_ctx, c = mod_chunk(pool, k)
                w, total, total_ctx = w_mod[k], *mod_sum
                times = lambda o, v, scalar: pool.tensor_tensor(o, v, scalar.to_broadcast(list(v.shape)), ALU.mult)
                if k == 0:
                    times(total_ctx, w[:, 0:2 * D], c_ctx)
                    times(total, w, c).then_inc(mod_added, 1)
                    continue
                for j in range(2):
                    half, beside = slice(j * D, (j + 1) * D), slot(k)[:, 3 * D:]
                    pool_link(times(beside, w[:, half], c_ctx))
                    pool_link(pool.tensor_tensor(total_ctx[:, half], total_ctx[:, half], beside, ALU.add))
                pool_link(times(w, w, c))
                pool.tensor_tensor(total, total, w, ALU.add).then_inc(mod_added, 1)

        def mod_dve(lo, hi):
            for k in range(lo, hi):
                scalars = mod_chunk(dve, k)
                for c, total in zip(scalars, mod_sum[::-1]):
                    ins = dve.scalar_tensor_tensor(out=total, in0=w_mod[k][:, 0:total.shape[1]], scalar=c, in1=total,
                                                   op0=ALU.mult, op1=ALU.add)
                ins.then_inc(mod_added, 1)

        def mod_pe():
            pe.wait_ge(mod_added, KD)
            pe.wait_ge(sem("gate_lin_in"), 16 * 2)
            for j, g in enumerate(g_gate_row):
                B.acquire(pe, g)
                B.filled(product(g, B.at(g), [(ones, mod_sum[0][:, 2 * D + j * BANK:2 * D + (j + 1) * BANK]),
                                              (ones[0:1, :], gate_lin[j])]), g)
            pe.wait_ge(sem("pads"), 4)
            g = g_mod[0]
            B.acquire(pe, g)
            for j in range(4):
                ins = product(g, B.at(g)[32 * j:32 * j + 32, :],
                              [(pick[:, v, :], mod_sum[v][:, j * BANK:(j + 1) * BANK]) for v in range(2)])
            B.filled(ins, g)

        def mod_act():
            for j, g in enumerate(g_gate_row):
                B.full(act, g)
                B.release(copy(act, gate_row[:, j * BANK:(j + 1) * BANK], B.at(g)), g)
            g = g_mod[0]
            B.full(act, g)
            B.release(copy(act, mod_rows, B.at(g)), g)

        def mod_turn_pe():
            B.drained(pe, g_mod[0])
            g = g_modT[0]
            B.acquire(pe, g)
            for m in range(4):
                ins = pe.transpose(B.at(g)[:, m * P:(m + 1) * P], mod_rows[:, m * P:(m + 1) * P], ident)
            B.filled(ins, g)

        def mod_turn_dve():
            g = g_modT[0]
            B.full(dve, g)
            v = B.at(g).rearrange("p (m j r) -> p j m r", m=4, j=4)
            for j in range(4):
                ins = dve.tensor_tensor(mod[:, 4 * j:4 * j + 4, :], v[:, j, :, 0:2],
                                        b_mod_col[:, 4 * j:4 * j + 4].unsqueeze(2).to_broadcast([P, 4, 2]), ALU.add)
                if j < 3:
                    link(ins)
            B.release(ins, g)
            B.drained(dve, g)
            link(dve.tensor_scalar(mod[:, KD:, :], mod[:, KD:, :], 1.0, None, ALU.add))
            link(dve.tensor_tensor(mod[:, KD:, :], mod[:, KD:, :], gain["norm_g_2"].unsqueeze(2).to_broadcast([P, KD, 2]),
                                   ALU.mult))

        g_mm, g_ms, g_mo = {}, {}, {}
        g_mm[0], g_ms[0] = B.take(2), B.take(T)
        for h in range(ML_H):
            if h + 1 < ML_H:
                g_mm[h + 1] = B.take(2)
            g_mo[h] = B.take(2)
            if h + 1 < ML_H:
                g_ms[h + 1] = B.take(T)
        g_qT = B.take(4)
        g_kT = B.take(1)

        def mlstm_max_pe(h):
            for d, m in ((0, mrow), (1, mrow2)):
                g, r = g_mm[h][d], d * ML_H + h
                B.acquire(pe, g)
                B.filled(product(g, B.at(g), [(ident[0:8, r:r + 1].to_broadcast([8, P]), m)]), g)

        def mlstm_scores_pe(h):
            lo, c = (h % 2) * HD, h // 2
            for i, g in enumerate(g_ms[h]):
                B.acquire(pe, g)
                B.filled(product(g, B.at(g), [(qkT[lo:lo + HD, 2 + c, i * P:(i + 1) * P], qkT[lo:lo + HD, c, :])]), g)

        def mlstm_values_pe(h):
            for d, g in enumerate(g_mo[h]):
                B.acquire(pe, g)
                if d == 0:
                    pe.wait_ge(sem("ml_weights0"), T * (h + 1))
                else:
                    for gs in g_ms[h]:
                        B.drained(pe, gs)
                for j in range(T):
                    tiles = range(0, j + 1) if d == 0 else range(j, T)
                    ins = product(g, B.at(g)[:, j * V_MOVE:(j + 1) * V_MOVE],
                                  [(Pt[h % 2][d][:, i, j * P:(j + 1) * P], v_moving(i, h)) for i in tiles])
                B.filled(ins, g)

        def mlstm_pe():
            for g in g_v:
                B.drained(pe, g)
            mlstm_max_pe(0)
            pe.wait_ge(sem("qk_silu"), 4)
            mlstm_scores_pe(0)
            for h in range(ML_H):
                if h + 1 < ML_H:
                    mlstm_max_pe(h + 1)
                mlstm_values_pe(h)
                if h + 1 < ML_H:
                    mlstm_scores_pe(h + 1)

        def mlstm_act():
            act.wait_ge(sem("gate_columns"), 1)
            for h in range(ML_H):
                for d, g in enumerate(g_mm[h]):
                    r = d * ML_H + h
                    if h >= 2:
                        B.full(act, g_mo[h - 2][d])
                    B.full(act, g)
                    if h == 1 and d == 0:
                        B.full(act, g_pool[-1])
                    for i in range(T):
                        o = slice(i * P, S) if d == 0 else slice(0, (i + 1) * P)
                        ins = act.activation(Pt[h % 2][d][:, i, o], B.at(g)[:, o], ACT.Exp, bias=gcols[:, d, i, r:r + 1])
                    B.release(ins, g)
                if h >= 1:
                    mlstm_values_act(h - 1)
            mlstm_values_act(ML_H - 1)

        def mlstm_values_act(h):
            for d, g in enumerate(g_mo[h]):
                B.full(act, g)
                v = B.at(g)[:, 0:T * V_MOVE].rearrange("p (t e) -> p t e", t=T)
                act.activation((hsum, htmp)[d][:, :, h, :], v[:, :, 0:HD], ACT.Identity).then_inc(sem("ml_values"), 1)
                B.release(act.activation(ml_den[:, 0, d, :, h], v[:, :, HD], ACT.Identity), g)

        def diagonal(pt):
            v = pt.rearrange("p i (j q) -> p (i j) q", q=P)
            return v[:, 0::T + 1, :]

        def mlstm_pool():
            for h in range(ML_H):
                for d in range(2):
                    B.drained(pool, g_mm[h][d])
                    v = diagonal(Pt[h % 2][d])
                    sign = 1 if d == 0 else -1
                    pool.affine_select(out=v, in_=v, pattern=[[0, T], [sign, P]], compare_op=ALU.is_ge, fill=0.0,
                                       base=0, channel_multiplier=-sign).then_inc(sem(f"ml_masked{d}"), 1)

        def mlstm_weights_dve(h):
            for d in range(2):
                dve.wait_ge(sem(f"ml_masked{d}"), h + 1)
                for i, g in enumerate(g_ms[h]):
                    o = slice(i * P, S) if d == 0 else slice(0, (i + 1) * P)
                    pt = Pt[h % 2][d][:, i, o]
                    B.full(dve, g)
                    ins = dve.scalar_tensor_tensor(out=pt, in0=B.at(g)[:, o], scalar=HD ** -0.5, in1=pt,
                                                   op0=ALU.mult, op1=ALU.mult)
                    if d == 0:
                        ins.then_inc(sem("ml_weights0"), 1)
                    else:
                        B.release(ins, g)

        def mlstm_dve():
            mlstm_weights_dve(0)
            for h in range(ML_H):
                if h + 1 < ML_H:
                    mlstm_weights_dve(h + 1)

        def mlstm_size_dve():
            dve.wait_ge(sem("ml_values"), 2 * ML_H)
            for h in range(ML_H):
                for g in g_mo[h]:
                    B.drained(dve, g)
            B.drained(dve, g_cols[0])
            den, size = ml_den[:, 0], ml_den[:, 1]
            link(dve.scalar_tensor_tensor(out=size, in0=den, scalar=-1.0, in1=den, op0=ALU.mult, op1=ALU.max))
            for d in range(2):
                link(dve.tensor_tensor(size[:, d], size[:, d], gcols[:, 2 + d, :, d * ML_H:(d + 1) * ML_H], ALU.max))
            dve.reciprocal(den, size).then_inc(sem("ml_size"), 1)

        def mlstm_norm_pool():
            pool.wait_ge(sem("ml_size"), 1)
            for d, v in enumerate((hsum, htmp)):
                pool_link(pool.tensor_tensor(v, v, ml_den[:, 0, d].unsqueeze(3).to_broadcast([P, T, ML_H, HD]), ALU.mult))
            pool_link(pool.tensor_tensor(hsum, hsum, htmp, ALU.add))
            pool.tensor_tensor(htmp, hsum, hsum, ALU.mult).then_inc(sem("ml_squares"), 1)
            pool.wait_ge(sem("head_rows_in"), 16 * 3)
            for g in g_o:
                B.drained(pool, g)
            flat = hsum.rearrange("p t h d -> p t (h d)")
            pool_link(pool.tensor_tensor(sig_o, sig_o, ml_g.unsqueeze(1).to_broadcast([P, T, ML_H * HD]), ALU.mult))
            pool.wait_ge(sem("ml_recip"), 1)
            rs = stat[:, 16:32].rearrange("p (t h) -> p t h", t=T).unsqueeze(3).to_broadcast([P, T, ML_H, HD])
            pool_link(pool.tensor_tensor(hsum, hsum, rs, ALU.mult))
            pool.tensor_tensor(flat, flat, sig_o, ALU.mult).then_inc(sem("y_mlstm"), 1)

        def mlstm_mean_dve():
            dve.wait_ge(sem("ml_squares"), 1)
            link(dve.tensor_reduce(stat[:, 0:16].rearrange("p (t h) -> p t h", t=T), htmp, AX, ALU.add))
            dve.tensor_scalar(stat[:, 16:32], stat[:, 0:16], 1.0 / HD, EPS, ALU.mult, ALU.add).then_inc(sem("head_means"), 1)

        def mlstm_root_act():
            act.wait_ge(sem("head_means"), 2)
            act.activation(stat[:, 0:16], stat[:, 16:32], ACT.Sqrt).then_inc(sem("head_roots"), 1)

        def mlstm_recip_dve():
            dve.wait_ge(sem("head_roots"), 2)
            dve.reciprocal(stat[:, 16:32], stat[:, 0:16]).then_inc(sem("ml_recip"), 1)

        def mlstm_out_pe():
            pe.wait_ge(sem("y_mlstm"), 1)
            transpose_rows(g_mlT, hsum.rearrange("p t h d -> p t (h d)"), T)

        def mlstm_out_drain(eng):
            drain_rows(eng, g_mlT, T, ymixT[:, 2:4, :])

        def rope_pairs(v, heads):
            even, odd = v[:, :, :, 0::2], v[:, :, :, 1::2]
            cos, sin = (const[:, c:c + 128].rearrange("p (t f) -> p t f", t=T).unsqueeze(2).to_broadcast([P, T, heads, 32])
                        for c in (C_COS, C_SIN))
            t0, t1 = (r[:, 0:heads, :] for r in rope_t)
            for t in range(T):
                link(dve.tensor_tensor(t0, even[:, t], sin[:, t], ALU.mult))
                link(dve.tensor_tensor(t1, odd[:, t], sin[:, t], ALU.mult))
                link(dve.tensor_tensor(even[:, t], even[:, t], cos[:, t], ALU.mult))
                link(dve.tensor_tensor(odd[:, t], odd[:, t], cos[:, t], ALU.mult))
                link(dve.tensor_tensor(even[:, t], even[:, t], t1, ALU.subtract))
                ins = dve.tensor_tensor(odd[:, t], odd[:, t], t0, ALU.add)
                if t < T - 1:
                    link(ins)
            return ins

        head_groups = ((aq, AT_H, qg, 0, "q"), (ak, 2, kg, T * AT_H, "k"))
        N_HEAD_ROWS = T * (AT_H + 2)

        def heads_dve():
            for g in (*g_aq, *g_akv):
                B.drained(dve, g)
            dve.wait_ge(sem("ak"), T)
            for v, heads, gn, o, name in head_groups:
                sq = sq_q[:, :, 0:heads, :]
                link(dve.tensor_tensor(sq, v, v, ALU.mult))
                link(dve.tensor_reduce(stat[:, o:o + T * heads].rearrange("p (t h) -> p t h", t=T), sq, AX, ALU.add))
            means = stat[:, 0:N_HEAD_ROWS]
            dve.tensor_scalar(means, means, 1.0 / HD, EPS, ALU.mult, ALU.add).then_inc(sem("head_means"), 1)
            dve.wait_ge(sem("head_roots"), 1)
            link(dve.reciprocal(means, means))
            dve.wait_ge(sem("head_rows_in"), 16 * 3)
            for v, heads, gn, o, name in head_groups:
                rs = stat[:, o:o + T * heads].rearrange("p (t h) -> p t h", t=T).unsqueeze(3).to_broadcast([P, T, heads, HD])
                link(dve.tensor_tensor(v, v, rs, ALU.mult))
                flat = v.rearrange("p t h d -> p (t h) d")
                link(dve.tensor_tensor(flat, flat, gn.unsqueeze(1).to_broadcast([P, T * heads, HD]), ALU.mult))
                rope_pairs(v, heads).then_inc(sem("roped"), 1)
                if name == "q":
                    dve.wait_ge(sem("roped"), 1)

        def heads_act():
            act.wait_ge(sem("head_means"), 1)
            means = stat[:, 0:N_HEAD_ROWS]
            act.activation(means, means, ACT.Sqrt).then_inc(sem("head_roots"), 1)

        def heads_pe():
            pe.wait_ge(sem("roped"), 1)
            for i, g in enumerate(g_qT):
                B.acquire(pe, g)
                for t in range(T):
                    ins = pe.transpose(B.at(g)[:, t * P:(t + 1) * P], aq[:, t, 2 * i:2 * i + 2, :].rearrange("p g d -> p (g d)"), ident)
                B.filled(ins, g)
            pe.wait_ge(sem("roped"), 2)
            g = g_kT[0]
            B.acquire(pe, g)
            for t in range(T):
                ins = pe.transpose(B.at(g)[:, t * P:(t + 1) * P], ak[:, t].rearrange("p h d -> p (h d)"), ident)
            B.filled(ins, g)

        def heads_drain(eng):
            for i, g in enumerate(g_qT):
                drain(eng, g, qT_at[:, i, :], B.at(g), HD ** -0.5)
            drain(eng, g_kT[0], kT_at, B.at(g_kT[0]))

        def heads_ready_pe():
            for g in (*g_qT, *g_kT):
                B.drained(pe, g)

        half = lambda h: slice((h // 4) * HD, (h // 4 + 1) * HD)
        attn_pe, attn_act, attn_dve, g_attn_end = attention(
            "attn", [(i, i + 4) for i in range(4)], [S],
            lambda h, qt: qT_at[half(h), h % 4, qt * P:(qt + 1) * P], lambda h, si: kT_at[half(h), :],
            lambda h, kt: av[:, kt, half(h)], HD, p_at, pt_at,
            lambda i, rows, o: dve.tensor_copy(ymixT[rows, 4 + i, :], o), [],
            besides={(dve, 22): mlstm_mean_dve, (act, 23): mlstm_root_act, (dve, 24): mlstm_recip_dve})
        g_mlT = B.take(2)

        g_out1 = B.take(2 * T)

        def add_product_pe(groups, lhs, rhs, chunks):
            for i, g in enumerate(groups):
                t, n = i // 2, i % 2
                B.acquire(pe, g)
                B.filled(product(g, B.at(g), [(lhs(k)[:, t * P:(t + 1) * P], rhs(k)[:, n * BANK:(n + 1) * BANK])
                                              for k in range(chunks)]), g)

        def out1_pe():
            pe.wait_ge(sem("w_out_in"), 16 * 3)
            for g in (*g_pool, *g_mlT, g_attn_end):
                B.drained(pe, g)
            add_product_pe(g_out1, lambda k: ymixT[:, k, :], lambda k: w_out[:, k, :], KD)

        hn_mem = sem("hn_mem")
        norm2_act, norm2_dve = add_norm(g_out1, x_sb, hn_ca, hn_mem)
        g_gate_row = B.take(2)
        g_mod = B.take(1)
        g_h2 = B.take(KD)
        g_modT = B.take(1)
        g_qca = B.take(CA_H)

        def qca_pe():
            pe.wait_ge(sem("ca_wq_in"), 16)
            for g in g_h2:
                B.drained(pe, g)
            for h, g in enumerate(g_qca):
                B.acquire(pe, g)
                B.filled(product(g, B.at(g), [(ca_wq[:, k, h * CA_HD:(h + 1) * CA_HD], hT[:, k, :]) for k in range(KD)]), g)

        def qca_drain(eng):
            for h, g in enumerate(g_qca):
                drain(eng, g, qT_ca[:, h, :], B.at(g), CA_HD ** -0.5)

        def split_o(i, o):
            link(dve.tensor_copy(oT_hi[:, i, :], o))
            return dve.tensor_tensor(oT_lo[:, i, :], o, oT_hi[:, i, :].bitcast(F32), ALU.subtract)

        def ca_wo_act():
            act.wait_ge(sem("ca_wo_in"), 16)
            B.full(act, g_attn_end)
            B.full(act, g_mlT[-1])
            act.activation(ca_wo_hi[:], ca_wo, ACT.Identity).then_inc(in_rounded, 1)

        def ca_wo_pool():
            pool.wait_ge(in_rounded, len(in_parts) + 1)
            pool.tensor_tensor(ca_wo_lo[:], ca_wo, ca_wo_hi[:].bitcast(F32), ALU.subtract).then_inc(in_split, 1)

        ca_pe, ca_act, ca_dve, g_ca_end = attention(
            "ca", [(h,) for h in range(CA_H)], [N_MEM],
            lambda h, qt: qT_ca[:, h, qt * P:(qt + 1) * P], lambda h, si: kT_ca[:, h, :],
            lambda h, kt: v_ca[:, kt, h * CA_HD:(h + 1) * CA_HD], CA_HD, p_ca, pt_ca,
            lambda i, rows, o: split_o(i, o), [])
        g_out2 = B.take(2 * T)

        def ca_all_pe():
            for g in g_qca:
                B.drained(pe, g)
            ca_pe()
            pe.wait_ge(in_split, len(in_parts) + 1)
            B.drained(pe, g_ca_end)
            for i, g in enumerate(g_out2):
                t, c = slice(i // 2 * P, (i // 2 + 1) * P), slice(i % 2 * BANK, (i % 2 + 1) * BANK)
                B.acquire(pe, g)
                three_passes(g, B.at(g), [v[:, :, c] for v in (ca_wo_hi, ca_wo_lo)], [v[:, :, t] for v in (oT_hi, oT_lo)],
                             weights_move=True)

        hn_ffn = sem("hn_ffn")
        norm3_act, norm3_dve = add_norm(g_out2, x_sb, hn, hn_ffn)
        g_h3 = [*B.take(KD - 2)]
        g_logitT = B.take(1)
        g_h3 += B.take(2)
        hn_ctx = sem("hn_ctx")
        normc_act, normc_dve = rms_rows(ctx_n, ctx_n, 2, D, hn_ctx)
        hT_junk = cut(W, 6656, 2, D)
        g_logit = B.take(1)
        g_affT = B.take(1)
        g_ctx = B.take(4)
        g_slots = B.take(1)

        def route_pe():
            turn_tiles(g_h3, hn, hn_ffn, range(T - 1))
            pe.wait_ge(sem("router_in"), 16)
            g = g_logitT[0]
            B.acquire(pe, g)
            for t in range(T):
                for gt in g_h3[2 * t:2 * t + 2]:
                    B.drained(pe, gt)
                ins = product(g, B.at(g)[0:N_EXP, t * P:(t + 1) * P],
                              [(router_w[:, k, :], hT[:, k, t * P:(t + 1) * P]) for k in range(KD)])
                if t == 0:
                    turn_tiles(g_h3, hn, hn_ffn, (T - 1,))
            B.filled(ins, g)
            B.drained(pe, g)
            g = g_logit[0]
            B.acquire(pe, g)
            for t in range(T):
                ins = pe.transpose(B.at(g)[:, t * N_EXP:(t + 1) * N_EXP], logitsT[:, t * P:(t + 1) * P], ident[0:N_EXP, 0:N_EXP])
            B.filled(ins, g)
            pe.wait_ge(sem("aff"), 1)
            g = g_affT[0]
            B.acquire(pe, g)
            for t in range(T):
                ins = pe.transpose(B.at(g)[0:N_EXP, t * P:(t + 1) * P], aff[:, t, :], ident)
            B.filled(ins, g)
            ctx_pe()
            pe.wait_ge(sem("slot_rows"), 1)
            g = g_slots[0]
            B.acquire(pe, g)
            for t in range(T):
                ins = pe.transpose(B.at(g)[:, t * N_EXP:(t + 1) * N_EXP], slotT[:, t * P:(t + 1) * P], ident[0:N_EXP, 0:N_EXP])
            B.filled(ins, g)

        def ctx_norm_act():
            act.wait_ge(sem("ctx_in"), 16)
            normc_act(junk=hT_junk)

        def ctx_pe():
            pe.wait_ge(hn_ctx, 2)
            transpose_rows(g_ctx, ctx_n, 2)

        def ctx_drain_act():
            for i, g in enumerate(g_ctx):
                B.full(act, g)
                for k in (2 * i, 2 * i + 1):
                    ins = copy(act, hcT[:, k, :], B.at(g)[:, (k % 2) * CTX:(k % 2 + 1) * CTX], mod[:, KD + k, 1:2], mod[:, k, 1:2])
                B.release(ins, g)

        def route_act():
            B.drained(act, g_logit[0])
            act.activation(aff, aff, ACT.Exp).then_inc(sem("exp_logits"), 1)

        def route_dve():
            dve.memset(ones16, 1.0)
            g = g_logitT[0]
            B.full(dve, g)
            B.release(dve.tensor_copy(logitsT, B.at(g)[0:N_EXP, :]), g)
            g = g_logit[0]
            B.full(dve, g)
            v = B.at(g)[:, 0:T * N_EXP].rearrange("p (t e) -> p t e", t=T)
            link(dve.tensor_reduce(stat[:, 32:36], v, AX, ALU.max))
            B.release(dve.tensor_tensor(aff, v, stat[:, 32:36].unsqueeze(2).to_broadcast([P, T, N_EXP]), ALU.subtract), g)
            dve.wait_ge(sem("exp_logits"), 1)
            link(dve.tensor_reduce(stat[:, 36:40], aff, AX, ALU.add))
            link(dve.reciprocal(stat[:, 40:44], stat[:, 36:40]))
            dve.tensor_tensor(aff, aff, stat[:, 40:44].unsqueeze(2).to_broadcast([P, T, N_EXP]), ALU.mult).then_inc(sem("aff"), 1)
            g = g_affT[0]
            B.full(dve, g)
            affT = B.at(g)[0:N_EXP, :]
            for r in range(CAP // 8):
                eight, rest = top8[:, 8 * r:8 * r + 8], affT if r == 0 else left
                link(dve.max(eight, rest))
                link(dve.match_replace(left, eight, rest, -1.0))
            B.release(dve.tensor_tensor(left, left, affT, ALU.not_equal), g)
            B.drained(dve, g)
            link(dve.tensor_tensor_scan(slotT, ones16, left, 0.0, ALU.mult, ALU.add))
            dve.tensor_tensor(slotT, slotT, left, ALU.mult).then_inc(sem("slot_rows"), 1)
            g = g_slots[0]
            B.full(dve, g)
            B.release(dve.tensor_scalar(slot_of, B.at(g)[:, 0:T * N_EXP].rearrange("p (t e) -> p t e", t=T), 1.0, None,
                                        ALU.subtract), g)
            B.drained(dve, g)

        PAIRS, PIECES = N_EXP // 2, 24
        AHEAD = NSLOT
        xsT_full, xsT_sb = sem("xsT_full"), [sem("xsT_sb_act"), sem("xsT_sb_dve")]
        sel_ready, selgT_full, selgT_sb = sem("sel_ready"), sem("selgT_full"), sem("selgT_sb")
        silu_ready, hid_ready = sem("silu_ready"), sem("hid_ready")
        hidT_full, hidT_sb = sem("hidT_full"), [sem("hidT_sb_act"), sem("hidT_sb_dve")]
        y_sb = sem("y_sb")
        added_full, added = sem("added_full"), sem("added")
        posc_ready = sem("posc_ready")
        w_gu, w_down = a["expert_w_gu"][0], a["expert_w_down"][0]

        def piece_source(expert, i):
            if i < KD:
                return w_gu[bass.ds(expert, 1), i * P:(i + 1) * P, :].rearrange("e p f -> p (e f)")
            q = i - KD
            return w_down[bass.ds(expert, 1), q * 512:(q + 1) * 512, :].rearrange("e (j p) d -> p (e j) d", p=P)

        def piece_target(s, i):
            return slot(s) if i < KD else slot(s).rearrange("p (j d) -> p j d", j=4)

        def load_piece(expert, i, s):
            sp.dma_start(piece_target(s, i), piece_source(expert, i)).then_inc(slot_loaded[s], 16)

        def experts_sp():
            for used, slots in ((g_out1[-1], (0, 1)), (g_h2[-1], (4,)), (g_qca[-1], (2,)), (g_out2[-1], (3, 5, 6)),
                                (g_logit[0], (7,))):
                B.full(sp, used)
                if 3 in slots:
                    sp.dma_start(ctx_n, a["ctx_2"][0].rearrange("(t p) d -> p t d", p=P)).then_inc(sem("ctx_in"), 16)
                for i in slots:
                    load_piece(0, i, i)
            with sp.Fori(0, PAIRS - 1) as p:
                for n in range(AHEAD, PIECES + AHEAD):
                    e, i = n // 12, n % 12
                    sp.wait_ge(slot_free[n % NSLOT], 3 * p + n // NSLOT)
                    load_piece(2 * p + e, i, n % NSLOT)
            for n in range(AHEAD, PIECES):
                e, i = n // 12, n % 12
                sp.wait_ge(slot_free[n % NSLOT], 3 * (PAIRS - 1) + n // NSLOT)
                load_piece(2 * (PAIRS - 1) + e, i, n % NSLOT)

        GATHER, TURN = (4, 5), (4, 5)
        ADD_BANKS = (7, 4, 5, 0, 1, 2, 3, 6)

        def piece(n, p):
            s = n % NSLOT
            pe.wait_ge(slot_loaded[s], 48 * p + 16 * (n // NSLOT + 1))
            return slot(s)

        before_experts = range(B.next - NBANK, B.next)

        def experts_pe():
            for g in before_experts:
                B.drained(pe, g)
            with pe.Fori(0, PAIRS) as p:
                pe.wait_ge(sel_ready, 2 * p + 1)
                pe.wait_ge(added, 2 * T * p + 1)
                for k in range(KD):
                    for t in range(T):
                        ins = pe.matmul(psum[:, GATHER[k // 4], (k % 4) * P:(k % 4 + 1) * P], hn[:, t, k * P:(k + 1) * P],
                                        sel[:, t, :], start=(t == 0), stop=(t == T - 1))
                    if k % 4 == 3:
                        ins.then_inc(xsT_full, 1)
                pe.wait_ge(sel_ready, 2 * p + 2)
                for t in range(T):
                    ins = pe.transpose(psum[:, 7, t * P:(t + 1) * P], selg[:, t, :], ident)
                ins.then_inc(selgT_full, 1)
                pe.wait_ge(xsT_sb[0], p + 1)
                pe.wait_ge(xsT_sb[1], p + 1)
                for e in range(2):
                    for k in range(KD):
                        w = piece(12 * e + k, p)
                        for c in range(4):
                            for h in range(2):
                                ins = pe.matmul(psum[h * 64:(h + 1) * 64, c, :], xsT[:, k, e * CAP:(e + 1) * CAP],
                                                w[:, (2 * c + h) * BANK:(2 * c + h + 1) * BANK],
                                                start=(k == 0), stop=(k == KD - 1), skip_group_check=True)
                        ins.then_inc(slot_free[(12 * e + k) % NSLOT], 1)
                    for b in range(2):
                        pe.wait_ge(hid_ready, 4 * p + 2 * e + b + 1)
                        for j in range(4):
                            ins = pe.transpose(psum[:, TURN[b], j * P:(j + 1) * P], hid[:, b, j * P:(j + 1) * P], ident)
                        ins.then_inc(hidT_full, 1)
                    for q in range(4):
                        b, h = q // 2, q % 2
                        if h == 0:
                            pe.wait_ge(hidT_sb[b], 2 * p + e + 1)
                        if q == 0 and e == 1:
                            pe.wait_ge(y_sb, 4 * p + 2)
                        w = piece(12 * e + KD + q, p).rearrange("p (j d) -> p j d", j=4)
                        for j in range(4):
                            for n in range(2):
                                ins = pe.matmul(psum[n * 64:(n + 1) * 64, 6, :], hidT[b][:, j, h, :],
                                                w[:, j, n * BANK:(n + 1) * BANK], start=(q == 0 and j == 0),
                                                stop=(q == 3 and j == 3), skip_group_check=True)
                        ins.then_inc(slot_free[(12 * e + KD + q) % NSLOT], 1)
                pe.wait_ge(selgT_sb, p + 1)
                pe.wait_ge(y_sb, 4 * p + 4)
                for i, bank in enumerate(ADD_BANKS):
                    t, n = i // 2, i % 2
                    pe.matmul(psum[:, bank, :], selgT[:, t * P:(t + 1) * P], ypair[:, n * BANK:(n + 1) * BANK],
                              start=True, stop=True).then_inc(added_full, 1)
            pe.wait_ge(added, 2 * T * PAIRS + 1)

        def gu_done(eng, p, e):
            n = 12 * e + KD - 1
            eng.wait_ge(slot_free[n % NSLOT], 3 * p + n // NSLOT + 1)

        def y_done(eng, p, e):
            n = 12 * e + 11
            eng.wait_ge(slot_free[n % NSLOT], 3 * p + n // NSLOT + 1)

        def experts_act():
            with act.Fori(0, PAIRS) as p:
                act.wait_ge(xsT_full, 2 * p + 1)
                v = psum[:, GATHER[0], :].rearrange("p (k c) -> p k c", k=4)
                for k in range(4):
                    ins = act.activation(xsT[:, k, :], v[:, k, :], ACT.Identity, scale=gain["norm_ffn_g"][:, k:k + 1])
                ins.then_inc(xsT_sb[0], 1)
                for e in range(2):
                    gu_done(act, p, e)
                    for b in range(2):
                        act.activation(silu_g[:, b, :], psum[:, b, :], ACT.Silu).then_inc(silu_ready, 1)
                    act.wait_ge(hidT_full, 4 * p + 2 * e + 1)
                    act.activation(hidT[0].rearrange("p j h c -> p (j h c)"), psum[:, TURN[0], :],
                                   ACT.Identity).then_inc(hidT_sb[0], 1)
                    y_done(act, p, e)
                    for n in range(2):
                        act.activation(ypair[e * 64:(e + 1) * 64, n * BANK:(n + 1) * BANK], psum[n * 64:(n + 1) * 64, 6, :],
                                       ACT.Identity).then_inc(y_sb, 1)

        def experts_dve():
            link(dve.memset(stat[:, 0:1], 0.0))
            dve.memset(stat[:, 1:2], 0.0).then_inc(added, 1)
            iota = const[:, C_IOTA:C_IOTA + CAP]
            with dve.Fori(0, PAIRS) as p:
                dve.tensor_copy(posc, slot_of[:, :, bass.ds(2 * p, 2)]).then_inc(posc_ready, 1)
                dve.tensor_copy(gatec, aff[:, :, bass.ds(2 * p, 2)]).then_inc(posc_ready, 1)
                dve.wait_ge(posc_ready, 2 * p + 2)
                for t in range(T):
                    for e in range(2):
                        ins = dve.tensor_scalar(sel[:, t, e * CAP:(e + 1) * CAP], iota, posc[:, t, e:e + 1], None, ALU.is_equal)
                ins.then_inc(sel_ready, 1)
                for t in range(T):
                    for e in range(2):
                        ins = dve.tensor_scalar(selg[:, t, e * CAP:(e + 1) * CAP], iota, posc[:, t, e:e + 1],
                                                gatec[:, t, e:e + 1], ALU.is_equal, ALU.mult)
                ins.then_inc(sel_ready, 1)
                dve.wait_ge(xsT_full, 2 * p + 2)
                v = psum[:, GATHER[1], :].rearrange("p (k c) -> p k c", k=4)
                for k in range(4):
                    ins = dve.tensor_scalar(xsT[:, 4 + k, :], v[:, k, :], gain["norm_ffn_g"][:, 4 + k:5 + k], None, ALU.mult)
                ins.then_inc(xsT_sb[1], 1)
                dve.wait_ge(selgT_full, p + 1)
                dve.tensor_copy(selgT, psum[:, 7, :]).then_inc(selgT_sb, 1)
                for e in range(2):
                    for b in range(2):
                        dve.wait_ge(silu_ready, 4 * p + 2 * e + b + 1)
                        dve.tensor_tensor(hid[:, b, :], psum[:, 2 + b, :], silu_g[:, b, :], ALU.mult).then_inc(hid_ready, 1)
                    dve.wait_ge(hidT_full, 4 * p + 2 * e + 2)
                    dve.tensor_copy(hidT[1].rearrange("p j h c -> p (j h c)"), psum[:, TURN[1], :]).then_inc(hidT_sb[1], 1)
                for i, bank in enumerate(ADD_BANKS):
                    t, n = i // 2, i % 2
                    o = x_sb[:, t, n * BANK:(n + 1) * BANK]
                    dve.wait_ge(added_full, 2 * T * p + i + 1)
                    dve.tensor_tensor(o, psum[:, bank, :], o, ALU.add).then_inc(added, 1)

        w2 = a["w_in_2"][0]
        blocks = [(w2, C2["ckv"], 160), (w2, C2["cq"], Q_LORA), (w2, C2["za"], BANK)]
        blocks += [(w2, C2[n], BANK) for n in ("kb", "qb", "zb", "vb")]
        blocks += [(w2, C2[n] + j * BANK, BANK) for j in range(2) for n in ("ga", "gb")]
        BLOCK = dict(ckv=0, cq=1, za=2, kb=3, qb=4, zb=5, vb=6, g=7)
        block_loaded = [sem("block_loaded0"), sem("block_loaded1")]

        def block_view(b):
            n = blocks[b][2]
            return blk[b % 2][:, 0:KD * n].rearrange("p (k c) -> p k c", k=KD)

        def block_lo(b):
            n = blocks[b][2]
            return blk_lo[b % 2][:, 0:KD * n].rearrange("p (k c) -> p k c", k=KD)

        PLACE = (3, 2, 0, 1)
        at_place = lambda c: part_hi[:, PLACE[c]]
        parts = [(BLOCK["ckv"], 0, 160, ckv_hi), (BLOCK["cq"], 0, Q_LORA, cq_hi)]
        parts += [(BLOCK[n], c * P, P, at_place(c)) for n in ("za", "kb", "qb", "zb") for c in range(4)]
        parts += [(BLOCK["vb"], (PLACE[c] - 2) % 4 * P, P, at_place(c)) for c in range(4)]
        parts += [(BLOCK["g"] + b, c * P, P, at_place(c)) for b in range(4) for c in range(4)]
        PART = dict(ckv=0, cq=1, za=2, kb=6, qb=10, zb=14, vb=18, g=22)
        w_rounded, w_split = sem("w_rounded"), sem("w_split")

        def round_part(i, used=None):
            b, c, n, high = parts[i]
            act.wait_ge(block_loaded[b % 2], 16 * (b // 2 + 1))
            if used is not None:
                B.full(act, used)
            act.activation(high[:], block_view(b)[:, :, c:c + n], ACT.Identity).then_inc(w_rounded, 1)

        def rest_of_parts(lo, hi):
            for i in range(lo, hi):
                b, c, n, high = parts[i]
                pool.wait_ge(w_rounded, i + 1)
                pool.tensor_tensor(block_lo(b)[:, :, c:c + n], block_view(b)[:, :, c:c + n],
                                   high[:].bitcast(F32), ALU.subtract).then_inc(w_split, 1)

        def part(i):
            b, c, n, high = parts[i]
            pe.wait_ge(w_split, i + 1)
            return high, block_lo(b)[:, :, c:c + n]

        last_of_block = {}

        def load_blocks(lo, hi):
            for b in range(lo, hi):
                src, c0, n = blocks[b]
                if b >= 2:
                    B.full(sp, last_of_block[b - 2])
                sp.dma_start(block_view(b), src[:, c0:c0 + n].rearrange("(k p) c -> p k c", p=P)).then_inc(block_loaded[b % 2], 16)

        hn_x2 = sem("hn_x2")
        g_x2 = B.take(2 * T)
        sums2, means2, roots2, recips2 = (stat[:, 32 + 8 * i:40 + 8 * i] for i in range(4))

        def two_norms_act():
            load_sqrt_act()
            for n, (i, t) in enumerate(((0, 0), (0, 1), (0, 2), (1, 0), (1, 1), (0, 3), (1, 2))):
                if i == 0:
                    act.wait_ge(added, 2 * T * (PAIRS - 1) + 2 * t + 3)
                else:
                    act.wait_ge(sem("xg"), t + 1)
                act.activation(square_junk, (x_sb, hn)[i][:, t, :], ACT.Square,
                               accum_out=sums2[:, i * T + t:i * T + t + 1]).then_inc(sem("x_squared"), 1)
                act.wait_ge(sem("x_squared"), n + 1)
            act.wait_ge(sem("x_means"), 1)
            act.activation(roots2, means2, ACT.Sqrt).then_inc(sem("x_roots"), 1)
            round_part(PART["ckv"])

        def two_norms_pool():
            pool.wait_ge(sem("g_row_in"), 16)
            for t in range(T - 1):
                pool.wait_ge(added, 2 * T * (PAIRS - 1) + 2 * t + 3)
                pool.tensor_tensor(hn[:, t, :], x_sb[:, t, :], g_row, ALU.mult).then_inc(sem("xg"), 1)

        def two_norms_dve():
            dve.wait_ge(sem("g_row_in"), 16)
            dve.wait_ge(added, 2 * T * PAIRS + 1)
            t = T - 1
            link(dve.tensor_tensor(hn[:, t, :], x_sb[:, t, :], g_row, ALU.mult))
            link(dve.tensor_tensor_reduce(out=dve_junk, in0=hn[:, t, :], in1=hn[:, t, :], scale=1.0, scalar=0.0,
                                          op0=ALU.mult, op1=ALU.add, accum_out=sums2[:, T + t:T + t + 1]))
            dve.wait_ge(sem("x_squared"), 2 * T - 1)
            link(dve.tensor_scalar(means2[:, 0:T], sums2[:, 0:T], 1.0 / D, EPS, ALU.mult, ALU.add))
            link(dve.reciprocal(recips2[:, 0:T], means2[:, 0:T]))
            link(dve.tensor_tensor(means2[:, T:], sums2[:, T:], recips2[:, 0:T], ALU.mult))
            dve.tensor_scalar(means2[:, T:], means2[:, T:], 1.0 / D, EPS, ALU.mult, ALU.add).then_inc(sem("x_means"), 1)
            dve.wait_ge(sem("x_roots"), 1)
            link(dve.reciprocal(recips2, roots2))
            for t in range(T):
                dve.tensor_scalar(hn[:, t, :], hn[:, t, :], recips2[:, t:t + 1], recips2[:, T + t:T + t + 1],
                                  ALU.mult, ALU.mult).then_inc(hn_x2, 1)

        def x_mid_dve():
            for t in range(T):
                dve.scalar_tensor_tensor(out=x_sb[:, t, :], in0=x_sb[:, t, :], scalar=recips2[:, t:t + 1], in1=g_row,
                                         op0=ALU.mult, op1=ALU.mult)

        def turn2_pe():
            turn_tiles(g_x2, hn, hn_x2)

        h2_rounded, h2_split = sem("h2_rounded"), sem("h2_split")

        def ctx_split(eng):
            if eng is act:
                act.activation(hc_hi[:], hcT, ACT.Identity).then_inc(sem("hc_rounded"), 1)
            else:
                eng.wait_ge(sem("hc_rounded"), 1)
                eng.tensor_tensor(hc_lo[:], hcT, hc_hi[:].bitcast(F32), ALU.subtract).then_inc(sem("hc_split"), 1)

        def x2_split(eng):
            tile = lambda v, t: v[:, :, t * P:(t + 1) * P]
            for t in range(T + 1):
                if t < T:
                    drain_tiles(eng, g_x2[2 * t:2 * t + 2], tile(h2T, t), mod[:, KD:, 0], mod[:, 0:KD, 0])
                    if eng is act:
                        for g in g_x2[2 * t:2 * t + 2]:
                            B.drained(act, g)
                        act.activation(tile(h2_hi, t), tile(h2T, t), ACT.Identity).then_inc(h2_rounded, 1)
                        if t == 1:
                            round_part(PART["cq"])
                if eng is dve and t >= 1:
                    dve.wait_ge(h2_rounded, t)
                    dve.tensor_tensor(tile(h2_lo, t - 1), tile(h2T, t - 1), tile(h2_hi, t - 1).bitcast(F32),
                                      ALU.subtract).then_inc(h2_split, 1)

        h2 = (h2_hi, h2_lo)

        def tokens(t):
            halves, t = (h2, t) if t < T else ((hc_hi, hc_lo), t - T)
            return [v[:, :, t * P:(t + 1) * P] for v in halves]

        g_ckv = B.take(KT2)
        g_cq = B.take(T)
        g_za = B.take(4)
        last_of_block.update({BLOCK["ckv"]: g_ckv[-1], BLOCK["cq"]: g_cq[-1], BLOCK["za"]: g_za[-1]})

        def mla_in_pe():
            for i, (name, groups, n) in enumerate((("ckv", g_ckv, 160), ("cq", g_cq, Q_LORA))):
                w = part(PART[name])
                for t, g in enumerate(groups):
                    pe.wait_ge(*((h2_split, t + 1) if t < T else (sem("hc_split"), 1)))
                    B.acquire(pe, g)
                    three_passes(g, B.at(g)[:, 0:n], w, tokens(t), weights_move=True)
            channels_pe("za", g_za)

        def channels_pe(name, groups):
            for c, g in enumerate(groups):
                w = part(PART[name] + c)
                B.acquire(pe, g)
                three_passes(g, B.at(g), w, h2)

        norm_kv_act, norm_kv_dve = rms_rows(ckv[:, :, 0:KV_LORA], ckv[:, :, 0:KV_LORA], KT2, KV_LORA, sem("ckv_n"))
        norm_q_act, norm_q_dve = rms_rows(cq, cq, T, Q_LORA, sem("cq_n"))

        def mla_in_act():
            for t, g in enumerate(g_ckv):
                B.full(act, g)
                B.release(copy(act, ckv[:, t, :], B.at(g)[:, 0:160]), g)
            for c in range(2):
                round_part(PART["za"] + c, g_ckv[-1])
            for g in g_ckv:
                B.drained(act, g)
            norm_kv_act(junk=cut(hn_flat, 1024, KT2, KV_LORA))
            for t, g in enumerate(g_cq):
                B.full(act, g)
                B.release(copy(act, cq[:, t, :], B.at(g)[:, 0:Q_LORA]), g)
            for c in range(2, 4):
                round_part(PART["za"] + c, g_cq[-1])
            for g in g_cq:
                B.drained(act, g)
            norm_q_act(junk=cut(hn_flat, 2048, T, Q_LORA))
            for c, g in enumerate(g_za):
                B.full(act, g)
                B.release(act.activation(oaT[:, c, :], B.at(g), ACT.Silu), g)

        def rotate_halves(v, cos, sin, done=None):
            x1, x2 = v[:, :, :, 0, :], v[:, :, :, 1, :]
            n = v.shape[1]
            t0, t1 = (r[:, 0:n] for r in rope2_t)
            link(dve.tensor_tensor(t0, x1, sin, ALU.mult))
            link(dve.tensor_tensor(t1, x2, sin, ALU.mult))
            link(dve.tensor_tensor(x1, x1, cos, ALU.mult))
            link(dve.tensor_tensor(x2, x2, cos, ALU.mult))
            link(dve.tensor_tensor(x1, x1, t1, ALU.subtract))
            return dve.tensor_tensor(x2, x2, t0, ALU.add)

        cos2, sin2 = (const[:, c:c + 64].rearrange("p (t a f) -> p t a f", t=T, a=2) for c in (C_COS2, C_SIN2))

        def mla_in_dve():
            norm_kv_dve()
            kr = ckv[:, 0:T, KV_LORA:].rearrange("p t (a x f) -> p t a x f", a=2, x=2)
            rotate_halves(kr, cos2, sin2).then_inc(sem("kr"), 1)
            norm_q_dve()

        g_ckvT = B.take(2)
        g_krT = B.take(2)
        g_cqT = B.take(2)
        g_q = B.take(2 * T)
        g_kn = B.take(2 * MLA_H)
        g_va = B.take(KT2)
        g_qT2 = B.take(MLA_H)
        KEY_SEGS = ((0, S), (S, NTOK))

        def mla_up_pe():
            pe.wait_ge(sem("ckv_n"), KT2)
            pe.wait_ge(sem("kr"), 1)
            for groups, c0, n in ((g_ckvT, 0, KV_LORA), (g_krT, KV_LORA, ROPE)):
                for i, g in enumerate(groups):
                    B.acquire(pe, g)
                    for t in range(T * i, min(T * i + T, KT2)):
                        ins = pe.transpose(B.at(g)[0:n, (t % T) * P:(t % T + 1) * P], ckv[:, t, c0:c0 + n], ident)
                    B.filled(ins, g)
            pe.wait_ge(sem("cq_n"), T)
            for c, g in enumerate(g_cqT):
                B.acquire(pe, g)
                for t in range(T):
                    ins = pe.transpose(B.at(g)[:, t * P:(t + 1) * P], cq[:, t, c * P:(c + 1) * P], ident)
                B.filled(ins, g)
            pe.wait_ge(sem("up_in"), 16 * 2)
            for g in (*g_ckvT, *g_cqT):
                B.drained(pe, g)
            for i, g in enumerate(g_q):
                t, n = i // 2, i % 2
                B.acquire(pe, g)
                B.filled(product(g, B.at(g)[:, 0:384], [(cqT[:, c, t * P:(t + 1) * P], uq[:, c, n * 384:(n + 1) * 384])
                                                       for c in range(2)]), g)
            for i, g in enumerate(g_kn):
                h, (lo, hi) = i // 2, KEY_SEGS[i % 2]
                B.acquire(pe, g)
                B.filled(product(g, B.at(g)[0:NOPE, 0:hi - lo], [(ukv[:, h, 0:NOPE], ckvT[:, lo:hi])]), g)
            for t, g in enumerate(g_va):
                B.acquire(pe, g)
                B.filled(product(g, B.at(g).rearrange("p (h d) -> p h d", h=MLA_H),
                                 [(ckvT[:, t * P:(t + 1) * P], ukv[:, :, NOPE:])]), g)
            pe.wait_ge(sem("q_rot"), T)
            for h, g in enumerate(g_qT2):
                B.acquire(pe, g)
                for t in range(T):
                    ins = pe.transpose(B.at(g)[0:QK_MLA, t * P:(t + 1) * P], q_tok[:, t, h, :], ident)
                B.filled(ins, g)

        def mla_up_act():
            for g, (lo, hi) in zip(g_ckvT, KEY_SEGS):
                B.full(act, g)
                B.release(copy(act, ckvT[:, lo:hi], B.at(g)[:, 0:hi - lo], g_ckv_col), g)
            for c, g in enumerate(g_cqT):
                B.full(act, g)
                B.release(copy(act, cqT[:, c, :], B.at(g), g_cq_col[:, c:c + 1]), g)
            for i, g in enumerate(g_q):
                t, n = i // 2, i % 2
                B.full(act, g)
                B.release(copy(act, q_tok[:, t, 4 * n:4 * n + 4, :], B.at(g)[:, 0:384].rearrange("p (h c) -> p h c", h=4),
                               QK_MLA ** -0.5), g)
            for i, g in enumerate(g_kn):
                h, (lo, hi) = i // 2, KEY_SEGS[i % 2]
                B.full(act, g)
                B.release(copy(act, kT_mla[0:NOPE, h, lo:hi], B.at(g)[0:NOPE, 0:hi - lo]), g)
            for h, g in enumerate(g_qT2):
                if h % 2 == 0:
                    B.full(act, g)
                    B.release(copy(act, qT_mla[:, h, :], B.at(g)[0:QK_MLA, :]), g)

        def mla_up_dve():
            for g, (lo, hi) in zip(g_krT, KEY_SEGS):
                B.full(dve, g)
                B.release(dve.tensor_copy(kT_mla[NOPE:QK_MLA, :, lo:hi],
                                          B.at(g)[0:ROPE, 0:hi - lo].unsqueeze(1).to_broadcast([ROPE, MLA_H, hi - lo])), g)
            for t in range(T):
                for g in g_q[2 * t:2 * t + 2]:
                    B.drained(dve, g)
                v = q_tok[:, t, :, NOPE:].rearrange("p h (a x f) -> p h a x f", a=2, x=2)
                c, s = (r[:, t].unsqueeze(1).to_broadcast([P, MLA_H, 2, 8]) for r in (cos2, sin2))
                rotate_halves(v, c, s).then_inc(sem("q_rot"), 1)
                dve.wait_ge(sem("q_rot"), t + 1)
            for t, g in enumerate(g_va):
                B.full(dve, g)
                B.release(dve.tensor_copy(va[:, t, :], B.at(g)), g)
            for h, g in enumerate(g_qT2):
                if h % 2 == 1:
                    B.full(dve, g)
                    B.release(dve.tensor_copy(qT_mla[:, h, :], B.at(g)[0:QK_MLA, :]), g)

        def mla_ready_pe():
            for g in (*g_krT, *g_kn, *g_qT2):
                B.drained(pe, g)

        SEG2 = [S, CTX]
        seg2 = lambda si: slice(*KEY_SEGS[si])
        pairs2 = [(2 * i, 2 * i + 1) for i in range(4)]
        mla_pe, mla_act, mla_dve, g_mla_end = attention(
            "mla", pairs2, SEG2, lambda h, qt: qT_mla[:, h, qt * P:(qt + 1) * P], lambda h, si: kT_mla[:, h, seg2(si)],
            lambda h, kt: va[:, kt, h * HD:(h + 1) * HD], HD, p_mla, pt_mla,
            lambda i, rows, o: dve.tensor_tensor(oaT[rows, i, :], o, oaT[rows, i, :], ALU.mult), [],
            besides={(act, 24): lambda: round_part(PART["kb"])})

        g_kb = B.take(4 + 4)
        g_qb = B.take(4)
        g_zb = B.take(4)
        g_vb = B.take(2 * KT2)
        last_of_block.update({BLOCK["kb"]: g_kb[-1], BLOCK["vb"]: g_vb[-1], BLOCK["qb"]: g_qb[-1], BLOCK["zb"]: g_zb[-1]})

        def na_in_pe():
            for c in range(4):
                w = part(PART["kb"] + c)
                for g, x in zip(g_kb[2 * c:2 * c + 2], (h2, (hc_hi, hc_lo))):
                    B.acquire(pe, g)
                    three_passes(g, B.at(g)[:, 0:x[0].shape[2]], w, x)
            channels_pe("qb", g_qb)
            channels_pe("zb", g_zb)
            for i, g in enumerate(g_vb):
                half, t = i // KT2, i % KT2
                for n in (2 * half, 2 * half + 1):
                    part(PART["vb"] + n)
                high = part_hi[:, 2 - 2 * half:4 - 2 * half].rearrange("p q k c -> p k q c")
                low = block_lo(BLOCK["vb"])[:, :, 256 * half:256 * (half + 1)].rearrange("p k (q c) -> p k q c", q=2)
                B.acquire(pe, g)
                three_passes(g, B.at(g)[:, 0:256].rearrange("p (q c) -> p q c", q=2), (high, low), tokens(t), weights_move=True)

        def na_in_drain(eng):
            if eng is act:
                for c in range(1, 4):
                    round_part(PART["kb"] + c, g_mla_end)
            for c in range(4):
                for g, (lo, hi) in zip(g_kb[2 * c:2 * c + 2], KEY_SEGS):
                    drain(eng, g, kbT[:, c, lo:hi], B.at(g)[:, 0:hi - lo])
                if eng is act:
                    round_part(PART["qb"] + c, g_kb[2 * c + 1])
            for c, g in enumerate(g_qb):
                drain(eng, g, qbT[:, c, :], B.at(g), HD ** -0.5)
                if eng is act:
                    round_part(PART["zb"] + c, g)
            if eng is act:
                for c, g in enumerate(g_zb):
                    B.full(act, g)
                    B.release(act.activation(obT[:, c, :], B.at(g), ACT.Silu), g)
                    round_part(PART["vb"] + c, g)
            for i, g in enumerate(g_vb):
                half, t = i // KT2, i % KT2
                drain(eng, g, vb[:, t, 256 * half:256 * (half + 1)], B.at(g)[:, 0:256])

        def na_ready_pe():
            for g in (*g_kb, *g_qb):
                B.drained(pe, g)

        odd = lambda h: slice((h % 2) * HD, (h % 2 + 1) * HD)

        def na_bias(h, qt):
            o = 6 - 2 * qt
            return na_table[:, h, o * GRID_W:(o + GRID_H) * GRID_W]

        na_pe, na_act, na_dve, g_na_end = attention(
            "na", pairs2, SEG2, lambda h, qt: qbT[odd(h), h // 2, qt * P:(qt + 1) * P],
            lambda h, si: kbT[odd(h), h // 2, seg2(si)], lambda h, kt: vb[:, kt, h * HD:(h + 1) * HD], HD, p_na, pt_na,
            lambda i, rows, o: dve.tensor_tensor(obT[rows, i, :], o, obT[rows, i, :], ALU.mult), [], bias=na_bias,
            besides={(act, 24): lambda: round_part(PART["g"])})

        g_sig = B.take(2 * KD)
        last_of_block.update({BLOCK["g"] + b: g_sig[4 * b + 3] for b in range(4)})
        g_sig_of = lambda i, j: g_sig[8 * (j // 4) + 4 * i + j % 4]
        g_ya, g_yb = B.take(KD), B.take(KD)
        g_out3 = B.take(2 * T)

        out_parts = [(oaT, oa_hi[:], oa_lo[:], None, g_na_end), (obT, ob_hi[:], ob_lo[:], None, g_na_end)]
        OUT_A, OUT_B, OUT_W = {}, {}, {}

        def wab_part(i, w, w_lo, landed, groups, name):
            index = (OUT_A, OUT_B)[name == "b"]
            index[i] = len(out_parts)
            c = slice(2 * i * P, 2 * (i + 1) * P)
            used = groups[2 * i - 3] if i >= 2 else (g_ya[2 * i + 5] if name == "b" else g_na_end)
            out_parts.append((w[:, :, c], wab_hi[i % 2][:], w_lo[:][:, :, c], landed, used))

        def w_out2_part(k):
            OUT_W[k] = len(out_parts)
            out_parts.append((w_out2[k // 4][:, k % 4], w_out2_hi[k // 4][:, k % 4], w_out2_lo[k // 4][:, k % 4],
                              (w_out2_in[k // 4], 16), None))

        w_out2_in = [sem("w_out2_in0"), sem("w_out2_in1")]
        for i in range(4):
            wab_part(i, woa, woa_lo, (sem("woa_in"), 16), g_ya, "a")
        for i in range(2):
            wab_part(i, wob, wob_lo, (sem("wob_in"), 16), g_yb, "b")
            w_out2_part(i)
        for i in range(2, 4):
            wab_part(i, wob, wob_lo, (sem("wob_in"), 16), g_yb, "b")
            w_out2_part(i)
        for k in range(4, KD):
            w_out2_part(k)
        out_rounded, out_split = sem("out_rounded"), sem("out_split")

        def round_out_part(i):
            whole, high, low, landed, used = out_parts[i]
            if landed is not None:
                act.wait_ge(*landed)
            if used is not None:
                B.full(act, used)
            act.activation(high, whole, ACT.Identity).then_inc(out_rounded, 1)

        def rest_of_out_parts(lo, hi):
            for i in range(lo, hi):
                whole, high, low, landed, used = out_parts[i]
                pool.wait_ge(out_rounded, i + 1)
                pool.tensor_tensor(low, whole, high.bitcast(F32), ALU.subtract).then_inc(out_split, 1)

        def y_pe():
            B.drained(pe, g_na_end)
            B.drained(pe, g_mla_end)
            for n, g in enumerate(g_sig):
                w = part(PART["g"] + n)
                B.acquire(pe, g)
                three_passes(g, B.at(g), w, h2)
            for groups, index, w_lo, x in ((g_ya, OUT_A, woa_lo, (oa_hi, oa_lo)), (g_yb, OUT_B, wob_lo, (ob_hi, ob_lo))):
                for j, g in enumerate(groups):
                    i, c = j // 2, j % 2 * P
                    pe.wait_ge(out_split, index[i] + 1)
                    B.acquire(pe, g)
                    three_passes(g, B.at(g), (wab_hi[i % 2][:, :, c:c + P], w_lo[:, :, j * P:(j + 1) * P]), x)
            for i, g in enumerate(g_out3):
                t, n = slice(i // 2 * P, (i // 2 + 1) * P), slice(i % 2 * BANK, (i % 2 + 1) * BANK)
                B.acquire(pe, g)
                for k in range(KD):
                    if i == 0:
                        pe.wait_ge(out_split, OUT_W[k] + 1)
                        pe.wait_ge(sem("yT_split"), k + 1)
                    wh, wl = (v[k // 4][:, k % 4, n] for v in (w_out2_hi, w_out2_lo))
                    for m, (y, w) in enumerate(((yT_hi, wh), (yT_hi, wl), (yT_lo, wh))):
                        ins = pe.matmul(B.at(g), y[:, k, t], w, start=(k == 0 and m == 0), stop=(k == KD - 1 and m == 2))
                B.filled(ins, g)

        def round_y(j):
            act.wait_ge(sem("yT"), j + 1)
            act.activation(yT_hi[:, j, :], yT[:, j, :], ACT.Identity).then_inc(sem("yT_rounded"), 1)

        def y_act():
            for n in range(1, 4):
                round_part(PART["g"] + n, g_na_end)
            for n, g in enumerate(g_sig):
                b, c = n // 4, n % 4
                B.full(act, g)
                B.release(act.activation((yT, sgb)[b % 2][:, 4 * (b // 2) + c, :], B.at(g), ACT.Sigmoid), g)
                if n + 4 < len(g_sig):
                    round_part(PART["g"] + n + 4, g)
                if n == 3:
                    B.drained(act, g_mla_end)
                    B.drained(act, g_na_end)
                    round_out_part(0)
                if n == 7:
                    round_out_part(1)
                if n == 11:
                    for i in range(2):
                        round_out_part(OUT_A[i])
            for i in range(OUT_A[2], OUT_B[3] + 1):
                round_out_part(i)
            for j in range(KD):
                round_y(j)
                if OUT_B[3] + 1 + j < len(out_parts):
                    round_out_part(OUT_B[3] + 1 + j)

        def y_dve():
            for j, g in enumerate(g_ya):
                B.drained(dve, g_sig_of(0, j))
                B.full(dve, g)
                B.release(dve.tensor_tensor(yT[:, j, :], B.at(g), yT[:, j, :], ALU.mult), g)
            for j, g in enumerate(g_yb):
                B.drained(dve, g_sig_of(1, j))
                B.full(dve, g)
                B.release(dve.tensor_tensor(sgb[:, j, :], B.at(g), sgb[:, j, :], ALU.mult), g)
                B.drained(dve, g)
                B.drained(dve, g_ya[j])
                dve.tensor_tensor(yT[:, j, :], yT[:, j, :], sgb[:, j, :], ALU.add).then_inc(sem("yT"), 1)
                if j >= 1:
                    rest_of_y(j - 1)
            rest_of_y(KD - 1)
            for i, g in enumerate(g_out3):
                t, n = i // 2, i % 2
                c = slice(n * BANK, (n + 1) * BANK)
                B.full(dve, g)
                if i >= 2:
                    dve.wait_ge(sem("x_last"), i - 1)
                B.release(dve.tensor_tensor(ysum[i % 2], B.at(g), gate_row[:, c], ALU.mult), g)
                B.drained(dve, g)
                dve.tensor_tensor(x_sb[:, t, c], ysum[i % 2], x_sb[:, t, c], ALU.add).then_inc(sem("x_last"), 1)
                if n == 1:
                    last_norm_dve(t)

        def rest_of_y(j):
            dve.wait_ge(sem("yT_rounded"), j + 1)
            dve.tensor_tensor(yT_lo[:, j, :], yT[:, j, :], yT_hi[:, j, :].bitcast(F32), ALU.subtract).then_inc(sem("yT_split"), 1)

        last_stat = stat[:, 0:2 * T].rearrange("p (t i) -> p t i", i=2)
        last_turn = list(norms)
        squared, mean_ready, root_ready = sem("rows_squared"), sem("mean_ready"), sem("root_ready")

        def last_norm_act():
            for t in range(T):
                act.wait_ge(sem("x_last"), 2 * t + 2)
                act.activation(hn[:, t, :], x_sb[:, t, :], ACT.Square, accum_out=last_stat[:, t, 0:1]).then_inc(squared, 1)
                act.wait_ge(mean_ready, last_turn[0] + t + 1)
                act.activation(last_stat[:, t, 0:1], last_stat[:, t, 1:2], ACT.Sqrt).then_inc(root_ready, 1)

        def last_norm_dve(t):
            if t == 0:
                dve.wait_ge(sem("g_fin_in"), 16)
            dve.wait_ge(squared, last_turn[1] + t + 1)
            dve.tensor_scalar(last_stat[:, t, 1:2], last_stat[:, t, 0:1], 1.0 / D, EPS, ALU.mult, ALU.add).then_inc(mean_ready, 1)
            dve.wait_ge(root_ready, last_turn[0] + t + 1)
            link(dve.reciprocal(last_stat[:, t, 1:2], last_stat[:, t, 0:1]))
            dve.scalar_tensor_tensor(out=x_sb[:, t, :], in0=x_sb[:, t, :], scalar=last_stat[:, t, 1:2], in1=g_fin,
                                     op0=ALU.mult, op1=ALU.mult).then_inc(sem("result"), 1)

        def row_of(v, n):
            return v.unsqueeze(0).to_broadcast([P, n]) if len(v.shape) == 1 else v.to_broadcast([P, n])

        w_in_loaded = [sem(f"w_in_loaded{i}") for i in range(4)]
        w_mod_loaded = [sem(f"w_mod_loaded{i}") for i in range(4)]

        def first_loads():
            sp.dma_start(const[:, 0:C_END], a["shape_const"]).then_inc(sem("const_in"), 16)
            sp.dma_start(mem, a["mem"][0].rearrange("(t p) d -> p t d", p=P)).then_inc(sem("mem_in"), 16)
            for i in range(2):
                t = slice(2 * i, 2 * i + 2)
                sp.dma_start(x_sb[:, t, :], a["x"][0].rearrange("(t p) d -> p t d", p=P)[:, t, :]).then_inc(sem(f"x_in{i}"), 16)
            for dst, src in row_loads:
                sp.dma_start(dst, src).then_inc(sem("rows_in"), 16)
            w = a["w_in"][0].rearrange("(k p) c -> p k c", p=P)
            sp.dma_start(w_gate, w[:, :, GATE0:GATE1]).then_inc(sem("w_gate_in"), 16)
            sp.dma_start(ca_wkv, a["ca_wkv"][0].rearrange("(k p) c -> p k c", p=P)).then_inc(sem("ca_wkv_in"), 16)

            def load_w_in(i):
                o = 0
                for lo, hi in W_IN_COLS[i]:
                    sp.dma_start(w_in[i][:, :, o:o + hi - lo], w[:, :, lo:hi]).then_inc(w_in_loaded[i], 16)
                    o += hi - lo

            load_w_in(0)
            load_w_in(1)
            B.full(sp, g_vca[-1])
            sp.dma_start(pool_w, a["pool_w"][0].rearrange("(c g) i e -> (g i) c e", c=2)).then_inc(sem("pool_w_in"), 16)
            sp.dma_start(ml_g, row_of(a["mlstm_norm_g"], ML_H * HD)).then_inc(sem("head_rows_in"), 16)
            sp.dma_start(qg, row_of(a["q_norm_g"], HD)).then_inc(sem("head_rows_in"), 16)
            sp.dma_start(kg, row_of(a["k_norm_g"], HD)).then_inc(sem("head_rows_in"), 16)
            sp.dma_start(router_w, a["router_w"][0].rearrange("(k p) e -> p k e", p=P)).then_inc(sem("router_in"), 16)
            B.full(sp, g_gate[0])
            sp.dma_start(inv_n, a["shape_inv"].rearrange("p (c s) -> p c s", c=2)).then_inc(sem("inv_n_in"), 16)
            B.full(sp, g_chan[3])
            load_w_in(3)
            B.full(sp, g_akv[-1])
            load_w_in(2)
            wm = a["w_mod_2"][0]

            def load_w_mod(k):
                sp.dma_start(w_mod[k], wm[k * P:(k + 1) * P, :]).then_inc(w_mod_loaded[k if k < 4 else 2 + k % 2], 16)

            for k, g in enumerate((g_aq[-1], g_o[-1], g_o[-1], g_o[-1])):
                B.full(sp, g)
                load_w_mod(k)
            B.full(sp, g_ms[ML_H - 1][-1])
            for j in range(2):
                sp.dma_start(gate_lin[j], a["b_mod_2"][:, 2 * D + j * BANK:2 * D + (j + 1) * BANK]).then_inc(sem("gate_lin_in"), 16)
            sp.wait_ge(mod_added, 2)
            w = a["w_out"][0]
            sp.dma_start(w_out[:, 0:4, :], w[0:512].rearrange("(k p) c -> p k c", p=P)).then_inc(sem("w_out_in"), 16)
            for h in range(2):
                sp.dma_start(w_out[h * HD:(h + 1) * HD, 4:8, :],
                             w[512 + h * 256:768 + h * 256].rearrange("(k p) c -> p k c", p=HD)).then_inc(sem("w_out_in"), 16)
            for k in range(4, KD):
                sp.wait_ge(mod_added, k - 1)
                load_w_mod(k)
            sp.wait_ge(mod_added, KD - 1)
            sp.dma_start(ca_wq, a["ca_wq"][0].rearrange("(k p) c -> p k c", p=P)).then_inc(sem("ca_wq_in"), 16)
            sp.wait_ge(mod_added, KD)
            sp.dma_start(ca_wo, a["ca_wo"][0].rearrange("(k p) c -> p k c", p=P)).then_inc(sem("ca_wo_in"), 16)

        row_loads = [(rows[lo:hi, :], a[name].rearrange("(k p) -> k p", p=P) if len(a[name].shape) == 1 else
                      a[name][0].rearrange("w (c p) -> (w c) p", p=P) if len(a[name].shape) == 3 else
                      a[name][:, 0:(hi - lo) * P].rearrange("o (k p) -> (o k) p", p=P)) for name, (lo, hi) in ROWS.items()]
        row_loads.append((gate_b_rows, a["mlstm_gate_b"].rearrange("o (k p) -> (o k) p", k=2)))
        N_ROW_LOADS = len(row_loads)

        ctx.enter_context(nc.allow_non_contiguous_dma(reason="windows of 16 biases, and a few columns of weights"))

        def na_table_build():
            pool.wait_ge(sem("fill"), 1)
            flat = na_dram.rearrange("a w c -> (a w c)").rearrange("(p r f) -> p r f", p=P, f=240)
            pool.dma_start(flat, fill[:].unsqueeze(1).to_broadcast([P, 16, 240])).then_inc(sem("na_filled"), 16)
            pool.wait_ge(sem("na_filled"), 16)
            rpb = a["rpb_2"][0].rearrange("h r c -> (h r) c")
            mid = GRID_W - NA_KC + NA_KC // 2
            n_hr = NA_H * (2 * NA_KR - 1)
            cell, row = GRID_W, 2 * NA_KC - 1
            pool.dma_start(bass.AP(na_dram.tensor, 8 * cell, [[cell * cell, n_hr], [cell + 1, mid - 7], [1, NA_KC]]),
                           bass.AP(rpb.tensor, 7, [[row, n_hr], [0, mid - 7], [1, NA_KC]])).then_inc(sem("na_cells"), 16)
            for w in (*range(8), *range(mid + 1, GRID_W)):
                start = min(max(w - NA_KC // 2, 0), GRID_W - NA_KC)
                pool.dma_start(na_dram[:, w, start:start + NA_KC],
                               rpb[:, start - w + NA_KC - 1:start - w + 2 * NA_KC - 1]).then_inc(sem("na_cells"), 16)

        N_CELLS = 1 + 8 + 7

        def second_loads():
            for s in (0, 1):
                sp.wait_ge(slot_free[s], 3 * PAIRS)
                load_blocks(s, s + 1)
            sp.wait_ge(slot_free[6], 3 * PAIRS)
            sp.dma_start(g_row, row_of(a["final_norm_g"], D)).then_inc(sem("g_row_in"), 16)
            sp.wait_ge(added, 2 * T * PAIRS + 1)
            sp.dma_start(uq, a["w_uq_2"][0].rearrange("(k p) c -> p k c", p=P)).then_inc(sem("up_in"), 16)
            sp.dma_start(ukv, a["w_ukv_2"][0].rearrange("p (h c) -> p h c", h=MLA_H)).then_inc(sem("up_in"), 16)
            load_blocks(2, 5)
            B.full(sp, g_mla_end)
            sp.wait_ge(sem("na_cells"), 16 * N_CELLS)
            v = na_dram.rearrange("(h r) w c -> w h r c", h=NA_H)
            for i in range(2):
                for h in range(NA_H):
                    sp.dma_start(na_table[i * 64:(i + 1) * 64, h, :].rearrange("p (r c) -> p r c", r=14),
                                 v[:, h, 1 - i:15 - i, :]).then_inc(sem("na_table_in"), 16)
            load_blocks(5, 9)
            B.full(sp, g_na_end)
            sp.dma_start(woa, a["w_oa_2"][0].rearrange("(k p) c -> p k c", p=P)).then_inc(sem("woa_in"), 16)
            sp.dma_start(g_fin, row_of(a["final_g_2"], D)).then_inc(sem("g_fin_in"), 16)
            load_blocks(9, 11)
            B.full(sp, g_sig[-1])
            sp.dma_start(wob, a["w_ob_2"][0].rearrange("(k p) c -> p k c", p=P)).then_inc(sem("wob_in"), 16)
            w = a["w_out_2"][0].rearrange("(k p) c -> p k c", p=P)
            for i in range(2):
                sp.dma_start(w_out2[i], w[:, 4 * i:4 * i + 4, :]).then_inc(w_out2_in[i], 16)

        block = ctx.enter_context(nc.Block())

        @block.sync
        def _(_):
            first_loads()
            experts_sp()
            second_loads()
            for t in range(T):
                sp.wait_ge(sem("result"), t + 1)
                sp.dma_start(out[0, t * P:(t + 1) * P, :], x_sb[:, t, :]).then_inc(sem("stored"), 16)
            sp.wait_ge(sem("stored"), 16 * T)

        @block.gpsimd
        def _(_):
            pool.memset(fill[:], NEG).then_inc(sem("fill"), 1)
            rest_of_in_parts(0, 4)
            B.full(pool, g_vca[-1])
            pool.memset(upad, 0.0).then_inc(sem("pads"), 1)
            pool.memset(qkpad, 0.0).then_inc(sem("pads"), 1)
            pool.memset(v_aug[:, :, :, HD:], 1.0)
            pool.memset(v_pad, 1.0).then_inc(sem("pads"), 1)
            pool.memset(pick[:, 0, 1:], 0.0)
            pool.memset(pick[:, 1, 2:], 0.0)
            pool.memset(pick[:, 1, 0:1], 0.0)
            for v in range(2):
                ins = pool.memset(pick[:, v, v:v + 1], 1.0)
            ins.then_inc(sem("pads"), 1)
            rest_of_in_parts(4, len(in_parts))
            mlstm_pool()
            mod_pool(0, 2)
            mlstm_norm_pool()
            mod_pool(2, 3)
            ca_wo_pool()
            na_table_build()
            two_norms_pool()
            rest_of_parts(0, 1)
            ctx_split(pool)
            rest_of_parts(1, PART["g"] + 8)
            rest_of_out_parts(0, 1)
            rest_of_parts(PART["g"] + 8, PART["g"] + 12)
            rest_of_out_parts(1, 2)
            rest_of_parts(PART["g"] + 12, len(parts))
            rest_of_out_parts(2, len(out_parts))

        @block.tensor
        def _(_):
            first_turns_pe()
            gate_pe()
            memory_pe()
            project_pe()
            gates_pe()
            project_tokens_pe(g_v, 9)
            project_tokens_pe(g_o, 10)
            pool_pe()
            mlstm_pe()
            heads_pe()
            heads_ready_pe()
            attn_pe()
            mlstm_out_pe()
            out1_pe()
            mod_pe()
            turn_tiles(g_h2, hn_ca, hn_mem)
            mod_turn_pe()
            qca_pe()
            ca_all_pe()
            route_pe()
            experts_pe()
            turn2_pe()
            mla_in_pe()
            mla_up_pe()
            mla_ready_pe()
            mla_pe()
            na_in_pe()
            na_ready_pe()
            na_pe()
            y_pe()

        @block.scalar
        def _(_):
            drain_rows(act, g_memT, 2, memT)
            load_sqrt_act()
            norm1_act()
            columns_act()
            B.drained(act, g_columns[0])
            drain_tiles(act, g_h1, hT, gain["norm_mix_g"])
            hT_split_act()
            for i in range(4):
                round_in_part(i)
            gate_act()
            memory_drain(act)
            gates_act()
            project_act()
            gate_columns_act()
            conv_act()
            silu_c_act()
            heads_act()
            project_vo_act()
            pool_act()
            mlstm_act()
            heads_drain(act)
            attn_act()
            mlstm_out_drain(act)
            ca_wo_act()
            norm2_act()
            mod_act()
            drain_tiles(act, g_h2, hT, gain["norm_mem_g"])
            qca_drain(act)
            ca_act()
            norm3_act()
            drain_tiles(act, g_h3, hT, gain["norm_ffn_g"])
            ctx_norm_act()
            route_act()
            ctx_drain_act()
            experts_act()
            two_norms_act()
            ctx_split(act)
            x2_split(act)
            mla_in_act()
            mla_up_act()
            mla_act()
            na_in_drain(act)
            na_act()
            y_act()
            last_norm_act()

        @block.vector
        def _(_):
            drain_rows(dve, g_memT, 2, memT)
            norm1_dve()
            B.drained(dve, g_columns[0])
            drain_tiles(dve, g_h1, hT, gain["norm_mix_g"])
            hT_split_dve()
            memory_drain(dve)
            gates_dve()
            conv_dve()
            pool_dve()
            heads_dve()
            mlstm_dve()
            heads_drain(dve)
            mlstm_size_dve()
            attn_dve()
            mlstm_out_drain(dve)
            mod_dve(3, KD)
            norm2_dve()
            drain_tiles(dve, g_h2, hT, gain["norm_mem_g"])
            mod_turn_dve()
            qca_drain(dve)
            ca_dve()
            norm3_dve()
            drain_tiles(dve, g_h3, hT, gain["norm_ffn_g"])
            normc_dve()
            route_dve()
            experts_dve()
            two_norms_dve()
            x2_split(dve)
            x_mid_dve()
            mla_in_dve()
            mla_up_dve()
            mla_dve()
            na_in_drain(dve)
            dve.wait_ge(sem("na_table_in"), 16 * 2 * NA_H)
            na_dve()
            y_dve()


_INPUTS = ["x", "mem", "norm_mix_g", "w_in", "pool_w", "pool_scale", "mlstm_conv_w", "mlstm_gate_b", "mlstm_norm_g",
           "q_norm_g", "k_norm_g", "w_out", "norm_mem_g", "ca_wq", "ca_wkv", "ca_wo", "norm_ffn_g", "router_w",
           "expert_w_gu", "expert_w_down", "final_norm_g", "c_2", "ctx_2", "c_ctx_2", "w_mod_2", "b_mod_2", "norm_g_2",
           "w_in_2", "g_cq_2", "w_uq_2", "g_ckv_2", "w_ukv_2", "rpb_2", "w_oa_2", "w_ob_2", "w_out_2", "final_g_2"]


def kernel(**inputs):
    import concourse.bacc as bacc
    from concourse.bass_utils import run_bass_kernel_spmd

    nc = bacc.Bacc("TRN2", target_bir_lowering=False, num_devices=1)
    arrays = {f"in_{n}": np.ascontiguousarray(inputs[n]) for n in _INPUTS}
    arrays["in_shape_const"], arrays["in_shape_inv"] = shape_constants()
    aps = {n[3:]: nc.dram_tensor(n, v.shape, F32, kind="ExternalInput").ap() for n, v in arrays.items()}
    out = nc.dram_tensor("out", (1, S, D), F32, kind="ExternalOutput").ap()
    build(nc, aps, out)
    return run_bass_kernel_spmd(nc, [arrays], core_ids=[0]).results[0]["out"]
```
